# Optimizing a Trainium2 kernel written in Bass

```python
import math
import jax, jax.numpy as jnp
from jax import lax
import numpy as np

D_MODEL = 1024
BATCH = 1
SEQ = 1024
DEPTH = 2

GRID_W = 64
CTX_LEN = 256
HEAD_DIM = 64
BLOCK = 128
EPS = 1e-6
ROPE_BASE = 10000.0
DIFF_HEADS = 4
DIFF_V = 2 * HEAD_DIM
SWA_Q_HEADS = 8
SWA_KV_HEADS = 2
SWA_GROUP = SWA_Q_HEADS // SWA_KV_HEADS
WINDOW = 128
MLA_HEADS = 8
MLA_Q_LORA = 512
MLA_KV_LORA = 256
MLA_NOPE = 64
MLA_ROPE = 32
MLA_QK = MLA_NOPE + MLA_ROPE
MLA_V = 64
NA_HEADS = 8
NA_ROWS_MAX = 8
NA_COLS = 16
D_FF = 4 * D_MODEL
N_EVEN = (DEPTH + 1) // 2
N_ODD = DEPTH // 2
EVEN_SPLITS = (DIFF_HEADS * 2 * HEAD_DIM, DIFF_HEADS * 2 * HEAD_DIM, DIFF_HEADS * DIFF_V,
               SWA_Q_HEADS * HEAD_DIM, SWA_KV_HEADS * HEAD_DIM, SWA_KV_HEADS * HEAD_DIM)
ODD_SPLITS = (MLA_Q_LORA, MLA_KV_LORA, MLA_ROPE,
              NA_HEADS * HEAD_DIM, NA_HEADS * HEAD_DIM, NA_HEADS * HEAD_DIM)
EVEN_IN = sum(EVEN_SPLITS)
ODD_IN = sum(ODD_SPLITS)
MIX_OUT = DIFF_HEADS * DIFF_V + SWA_Q_HEADS * HEAD_DIM

kernel_name = 'hybrid_diffusion_prefix_trunk'

def rmsnorm(x, g):
    xf = x.astype(jnp.float32)
    y = xf * lax.rsqrt(jnp.mean(xf * xf, axis=-1, keepdims=True) + EPS)
    return (y * g.astype(jnp.float32)).astype(x.dtype)

def modulate(x, g, shift, scale):
    return rmsnorm(x, g) * (1.0 + scale) + shift

def split_cols(p, sizes):
    idx = [int(i) for i in np.cumsum(sizes)[:-1]]
    return jnp.split(p, idx, axis=-1)

def axial_rope_tables(n_tokens, rot_dim):
    t = jnp.arange(n_tokens, dtype=jnp.int32)
    row = (t // GRID_W).astype(jnp.float32)
    col = (t % GRID_W).astype(jnp.float32)
    n_freq = rot_dim // 4
    freqs = jnp.power(ROPE_BASE, -jnp.arange(n_freq, dtype=jnp.float32) / n_freq)
    ar = row[:, None] * freqs[None, :]
    ac = col[:, None] * freqs[None, :]
    ang = jnp.concatenate([ar, ar, ac, ac], axis=-1)
    return jnp.cos(ang), jnp.sin(ang)

def rope_2d(x, cos, sin):
    shape = (1, x.shape[1]) + (1,) * (x.ndim - 3) + (x.shape[-1],)
    x1, x2, x3, x4 = jnp.split(x, 4, axis=-1)
    rot = jnp.concatenate([-x2, x1, -x4, x3], axis=-1)
    return (x * cos.reshape(shape) + rot * sin.reshape(shape)).astype(x.dtype)

def sweep_query_blocks(fn, *qs):
    B, S = qs[0].shape[:2]
    nb = S // BLOCK
    blocks = tuple(jnp.moveaxis(q.reshape((B, nb, BLOCK) + q.shape[2:]), 1, 0) for q in qs)
    out = lax.map(lambda a: fn(*a), blocks)
    return jnp.moveaxis(out, 0, 1).reshape((B, S) + out.shape[3:])

def mha_attend(q, k, v, bias=None, mask=None):
    s = jnp.einsum('bqhd,bkhd->bhqk', q, k).astype(jnp.float32) * (q.shape[-1] ** -0.5)
    if bias is not None:
        s = s + bias[None]
    if mask is not None:
        s = jnp.where(mask, s, -jnp.inf)
    p = jax.nn.softmax(s, axis=-1)
    return jnp.einsum('bhqk,bkhd->bqhd', p.astype(v.dtype), v)

def diff_attend(q, k, v, lam):
    s = jnp.einsum('bqhtd,bkhtd->bthqk', q, k).astype(jnp.float32) * (q.shape[-1] ** -0.5)
    a = jax.nn.softmax(s, axis=-1)
    p = a[:, 0] - lam * a[:, 1]
    return jnp.einsum('bhqk,bkhe->bqhe', p.astype(v.dtype), v)

def gqa_sink_attend(q, k, v, sink, mask=None):
    s = jnp.einsum('bqhgd,bkhd->bhgqk', q, k).astype(jnp.float32) * (q.shape[-1] ** -0.5)
    if mask is not None:
        s = jnp.where(mask, s, -jnp.inf)
    sk = sink.astype(jnp.float32)[None, :, :, None, None]
    m = jnp.maximum(jnp.max(s, axis=-1, keepdims=True), sk)
    e = jnp.exp(s - m)
    p = e / (jnp.sum(e, axis=-1, keepdims=True) + jnp.exp(sk - m))
    return jnp.einsum('bhgqk,bkhd->bqhgd', p.astype(v.dtype), v)

def window_gqa(q, k, v, kc, vc, sink):
    B, S = q.shape[:2]
    nb = S // BLOCK
    L = kc.shape[1]

    def band(t):
        tp = jnp.pad(t, ((0, 0), (BLOCK, BLOCK), (0, 0), (0, 0))).reshape((B, nb + 2, BLOCK) + t.shape[2:])
        strip = jnp.concatenate([tp[:, :-2], tp[:, 1:-1], tp[:, 2:]], axis=2)
        return jnp.moveaxis(strip, 1, 0)

    qb = jnp.moveaxis(q.reshape((B, nb, BLOCK) + q.shape[2:]), 1, 0)
    qi = jnp.arange(BLOCK)[:, None]
    kj = jnp.arange(3 * BLOCK)[None, :] - BLOCK
    ctx_mask = jnp.ones((BLOCK, L), dtype=bool)

    def blk(args):
        n, qn, kn, vn = args
        pos_k = n * BLOCK + kj
        m = (jnp.abs(kj - qi) <= WINDOW) & (pos_k >= 0) & (pos_k < S)
        m = jnp.concatenate([m, ctx_mask], axis=1)
        kk = jnp.concatenate([kn, kc], axis=1)
        vv = jnp.concatenate([vn, vc], axis=1)
        return gqa_sink_attend(qn, kk, vv, sink, m)

    out = lax.map(blk, (jnp.arange(nb), qb, band(k), band(v)))
    return jnp.moveaxis(out, 0, 1).reshape(B, S, -1)

def neighbourhood_attn(q, k, v, kc, vc, rpb):
    B, S, H, d = q.shape
    rows = S // GRID_W
    kr = min(NA_ROWS_MAX, rows)
    L = kc.shape[1]
    qg = jnp.moveaxis(q.reshape(B, rows, GRID_W, H, d), 1, 0)
    kg = k.reshape(B, rows, GRID_W, H, d)
    vg = v.reshape(B, rows, GRID_W, H, d)
    cq = jnp.arange(GRID_W)
    cs = jnp.clip(cq - NA_COLS // 2, 0, GRID_W - NA_COLS)
    ck = jnp.arange(GRID_W)
    col_mask = (ck[None, :] >= cs[:, None]) & (ck[None, :] < cs[:, None] + NA_COLS)
    nb_mask = jnp.broadcast_to(col_mask[:, None, :], (GRID_W, kr, GRID_W)).reshape(GRID_W, kr * GRID_W)
    mask = jnp.concatenate([nb_mask, jnp.ones((GRID_W, L), dtype=bool)], axis=1)
    dc_idx = jnp.clip(ck[None, :] - cq[:, None], -(NA_COLS - 1), NA_COLS - 1) + NA_COLS - 1
    rpb32 = rpb.astype(jnp.float32)

    def row_block(args):
        r, qr = args
        rs = jnp.clip(r - kr // 2, 0, rows - kr)
        krows = lax.dynamic_slice_in_dim(kg, rs, kr, axis=1).reshape(B, kr * GRID_W, H, d)
        vrows = lax.dynamic_slice_in_dim(vg, rs, kr, axis=1).reshape(B, kr * GRID_W, H, d)
        dr_idx = rs + jnp.arange(kr) - r + NA_ROWS_MAX - 1
        bias = rpb32[:, dr_idx[None, :, None], dc_idx[:, None, :]].reshape(H, GRID_W, kr * GRID_W)
        bias = jnp.pad(bias, ((0, 0), (0, 0), (0, L)))
        kk = jnp.concatenate([krows, kc], axis=1)
        vv = jnp.concatenate([vrows, vc], axis=1)
        return mha_attend(qr, kk, vv, bias, mask)

    out = lax.map(row_block, (jnp.arange(rows), qg))
    return jnp.moveaxis(out, 0, 1).reshape(B, S, H * d)

def even_mixer(p_lat, p_ctx, q_g, k_g, lam_v, subln_g, sq_g, sk_g, sink, cos, sin, lam_init, need_ctx):
    def project(p, rope):
        B, N, _ = p.shape
        qa, ka, va, qb, kb, vb = split_cols(p, EVEN_SPLITS)
        qa = rmsnorm(qa.reshape(B, N, DIFF_HEADS, 2, HEAD_DIM), q_g)
        ka = rmsnorm(ka.reshape(B, N, DIFF_HEADS, 2, HEAD_DIM), k_g)
        va = va.reshape(B, N, DIFF_HEADS, DIFF_V)
        qb = rmsnorm(qb.reshape(B, N, SWA_KV_HEADS, SWA_GROUP, HEAD_DIM), sq_g)
        kb = rmsnorm(kb.reshape(B, N, SWA_KV_HEADS, HEAD_DIM), sk_g)
        vb = vb.reshape(B, N, SWA_KV_HEADS, HEAD_DIM)
        if rope:
            qa, ka, qb, kb = [rope_2d(t, cos, sin) for t in (qa, ka, qb, kb)]
        return qa, ka, va, qb, kb, vb

    qa_l, ka_l, va_l, qb_l, kb_l, vb_l = project(p_lat, True)
    qa_c, ka_c, va_c, qb_c, kb_c, vb_c = project(p_ctx, False)
    lv = lam_v.astype(jnp.float32)
    lam = jnp.exp(jnp.sum(lv[0] * lv[1])) - jnp.exp(jnp.sum(lv[2] * lv[3])) + lam_init
    sink_hg = sink.reshape(SWA_KV_HEADS, SWA_GROUP)

    def diff_out(o):
        B, N = o.shape[:2]
        return (rmsnorm(o, subln_g) * (1.0 - lam_init)).reshape(B, N, DIFF_HEADS * DIFF_V)

    ka_all = jnp.concatenate([ka_l, ka_c], axis=1)
    va_all = jnp.concatenate([va_l, va_c], axis=1)
    o_a = sweep_query_blocks(lambda qblk: diff_attend(qblk, ka_all, va_all, lam), qa_l)
    o_b = window_gqa(qb_l, kb_l, vb_l, kb_c, vb_c, sink_hg)
    o_lat = jnp.concatenate([diff_out(o_a), o_b], axis=-1)
    if not need_ctx:
        return o_lat, None
    B, L = p_ctx.shape[:2]
    o_ca = diff_out(diff_attend(qa_c, ka_c, va_c, lam))
    o_cb = gqa_sink_attend(qb_c, kb_c, vb_c, sink_hg).reshape(B, L, -1)
    return o_lat, jnp.concatenate([o_ca, o_cb], axis=-1)

def odd_mixer(p_lat, p_ctx, qa_g, kva_g, wq_up, wkv_up, mq_g, mk_g, nq_g, nk_g, rpb, cos, sin, need_ctx):
    def project(p, rope):
        B, N, _ = p.shape
        q_a, kv_a, k_r, nq, nk, nv = split_cols(p, ODD_SPLITS)
        q = (rmsnorm(q_a, qa_g) @ wq_up).reshape(B, N, MLA_HEADS, MLA_QK)
        kv = (rmsnorm(kv_a, kva_g) @ wkv_up).reshape(B, N, MLA_HEADS, MLA_NOPE + MLA_V)
        k = jnp.concatenate([kv[..., :MLA_NOPE],
                             jnp.broadcast_to(k_r[:, :, None, :], (B, N, MLA_HEADS, MLA_ROPE))], axis=-1)
        v = kv[..., MLA_NOPE:]
        q = rmsnorm(q, mq_g)
        k = rmsnorm(k, mk_g)
        if rope:
            q = jnp.concatenate([q[..., :MLA_NOPE], rope_2d(q[..., MLA_NOPE:], cos, sin)], axis=-1)
            k = jnp.concatenate([k[..., :MLA_NOPE], rope_2d(k[..., MLA_NOPE:], cos, sin)], axis=-1)
        nq = rmsnorm(nq.reshape(B, N, NA_HEADS, HEAD_DIM), nq_g)
        nk = rmsnorm(nk.reshape(B, N, NA_HEADS, HEAD_DIM), nk_g)
        nv = nv.reshape(B, N, NA_HEADS, HEAD_DIM)
        return q, k, v, nq, nk, nv

    q_l, k_l, v_l, nq_l, nk_l, nv_l = project(p_lat, True)
    q_c, k_c, v_c, nq_c, nk_c, nv_c = project(p_ctx, False)
    B, S = p_lat.shape[:2]
    k_all = jnp.concatenate([k_l, k_c], axis=1)
    v_all = jnp.concatenate([v_l, v_c], axis=1)
    o_c = sweep_query_blocks(lambda qblk: mha_attend(qblk, k_all, v_all), q_l).reshape(B, S, -1)
    o_d = neighbourhood_attn(nq_l, nk_l, nv_l, nk_c, nv_c, rpb)
    o_lat = jnp.concatenate([o_c, o_d], axis=-1)
    if not need_ctx:
        return o_lat, None
    L = p_ctx.shape[1]
    o_cc = mha_attend(q_c, k_c, v_c).reshape(B, L, -1)
    o_cd = mha_attend(nq_c, nk_c, nv_c).reshape(B, L, -1)
    return o_lat, jnp.concatenate([o_cc, o_cd], axis=-1)

def sq_relu_mlp(h, w1, w2):
    return jnp.square(jax.nn.relu(h @ w1)) @ w2

def setup_inputs(seed: int = 0) -> dict:
    key = jax.random.key(seed)
    ks = jax.random.split(key, 32)
    D = D_MODEL

    def nrm(k, shape, scale):
        return jax.random.normal(k, shape, jnp.float32) * scale

    def gain(k, shape):
        return 1.0 + 0.02 * jax.random.normal(k, shape, jnp.float32)

    return {
        'x': nrm(ks[0], (BATCH, SEQ, D), 1.0),
        'c': nrm(ks[1], (BATCH, D), 1.0),
        'ctx': nrm(ks[2], (BATCH, CTX_LEN, D), 1.0),
        'c_ctx': nrm(ks[3], (D,), 1.0),
        'ada_w': nrm(ks[4], (DEPTH, D, 6 * D), D ** -0.5),
        'ada_b': nrm(ks[5], (DEPTH, 6 * D), 0.02),
        'norm1_g': gain(ks[6], (DEPTH, D)),
        'norm2_g': gain(ks[7], (DEPTH, D)),
        'w_out': nrm(ks[8], (DEPTH, MIX_OUT, D), MIX_OUT ** -0.5),
        'mlp_w1': nrm(ks[9], (DEPTH, D, D_FF), D ** -0.5),
        'mlp_w2': nrm(ks[10], (DEPTH, D_FF, D), D_FF ** -0.5),
        'ev_w_in': nrm(ks[11], (N_EVEN, D, EVEN_IN), D ** -0.5),
        'diff_q_g': gain(ks[12], (N_EVEN, HEAD_DIM)),
        'diff_k_g': gain(ks[13], (N_EVEN, HEAD_DIM)),
        'diff_lam': nrm(ks[14], (N_EVEN, 4, HEAD_DIM), 0.1),
        'diff_subln_g': gain(ks[15], (N_EVEN, DIFF_V)),
        'swa_q_g': gain(ks[16], (N_EVEN, HEAD_DIM)),
        'swa_k_g': gain(ks[17], (N_EVEN, HEAD_DIM)),
        'swa_sink': nrm(ks[18], (N_EVEN, SWA_Q_HEADS), 0.5),
        'od_w_in': nrm(ks[19], (N_ODD, D, ODD_IN), D ** -0.5),
        'mla_qa_g': gain(ks[20], (N_ODD, MLA_Q_LORA)),
        'mla_kva_g': gain(ks[21], (N_ODD, MLA_KV_LORA)),
        'mla_wq_up': nrm(ks[22], (N_ODD, MLA_Q_LORA, MLA_HEADS * MLA_QK), MLA_Q_LORA ** -0.5),
        'mla_wkv_up': nrm(ks[23], (N_ODD, MLA_KV_LORA, MLA_HEADS * (MLA_NOPE + MLA_V)), MLA_KV_LORA ** -0.5),
        'mla_q_g': gain(ks[24], (N_ODD, MLA_QK)),
        'mla_k_g': gain(ks[25], (N_ODD, MLA_QK)),
        'na_q_g': gain(ks[26], (N_ODD, HEAD_DIM)),
        'na_k_g': gain(ks[27], (N_ODD, HEAD_DIM)),
        'na_rpb': nrm(ks[28], (N_ODD, NA_HEADS, 2 * NA_ROWS_MAX - 1, 2 * NA_COLS - 1), 0.2),
    }

def reference(x, c, ctx, c_ctx, ada_w, ada_b, norm1_g, norm2_g, w_out, mlp_w1, mlp_w2,
              ev_w_in, diff_q_g, diff_k_g, diff_lam, diff_subln_g, swa_q_g, swa_k_g, swa_sink,
              od_w_in, mla_qa_g, mla_kva_g, mla_wq_up, mla_wkv_up, mla_q_g, mla_k_g,
              na_q_g, na_k_g, na_rpb):
    S = x.shape[1]
    cos64, sin64 = axial_rope_tables(S, HEAD_DIM)
    cos32, sin32 = axial_rope_tables(S, MLA_ROPE)
    xc = ctx
    for layer in range(DEPTH):
        need_ctx = layer < DEPTH - 1
        mod_l = (jax.nn.silu(c) @ ada_w[layer] + ada_b[layer])[:, None, :]
        mod_c = (jax.nn.silu(c_ctx) @ ada_w[layer] + ada_b[layer])[None, None, :]
        sh1, sc1, g1, sh2, sc2, g2 = jnp.split(mod_l, 6, axis=-1)
        csh1, csc1, cg1, csh2, csc2, cg2 = jnp.split(mod_c, 6, axis=-1)
        h_l = modulate(x, norm1_g[layer], sh1, sc1)
        h_c = modulate(xc, norm1_g[layer], csh1, csc1)
        i = layer // 2
        if layer % 2 == 0:
            lam_init = 0.8 - 0.6 * math.exp(-0.3 * layer)
            o_l, o_c = even_mixer(h_l @ ev_w_in[i], h_c @ ev_w_in[i], diff_q_g[i], diff_k_g[i], diff_lam[i],
                                  diff_subln_g[i], swa_q_g[i], swa_k_g[i], swa_sink[i],
                                  cos64, sin64, lam_init, need_ctx)
        else:
            o_l, o_c = odd_mixer(h_l @ od_w_in[i], h_c @ od_w_in[i], mla_qa_g[i], mla_kva_g[i], mla_wq_up[i],
                                 mla_wkv_up[i], mla_q_g[i], mla_k_g[i], na_q_g[i], na_k_g[i], na_rpb[i],
                                 cos32, sin32, need_ctx)
        x = x + g1 * (o_l @ w_out[layer])
        x = x + g2 * sq_relu_mlp(modulate(x, norm2_g[layer], sh2, sc2), mlp_w1[layer], mlp_w2[layer])
        if need_ctx:
            xc = xc + cg1 * (o_c @ w_out[layer])
            xc = xc + cg2 * sq_relu_mlp(modulate(xc, norm2_g[layer], csh2, csc2), mlp_w1[layer], mlp_w2[layer])
    return x


_drawn_inputs = setup_inputs


def setup_inputs(seed=0):
    import zlib

    import numpy as np

    out = dict(_drawn_inputs(seed))
    spreads = {}
    factors = {'norm1_g': 8.0,
     'norm2_g': 2.735,
     'diff_q_g': 8.0,
     'diff_k_g': 8.0,
     'diff_lam': 4.038,
     'diff_subln_g': 7.826,
     'swa_q_g': 8.0,
     'swa_k_g': 8.0,
     'swa_sink': 8.0,
     'mla_qa_g': 8.0,
     'mla_kva_g': 8.0,
     'mla_q_g': 8.0,
     'mla_k_g': 8.0,
     'na_q_g': 8.0,
     'na_k_g': 8.0,
     'na_rpb': 8.0}
    for name, (base, spread) in spreads.items():
        noise = np.random.default_rng([zlib.crc32(name.encode()), seed]).standard_normal(out[name].shape)
        drawn = base * np.exp(spread * noise) if base else spread * noise
        out[name] = __import__('jax').numpy.asarray(drawn.astype(out[name].dtype))
    for name, factor in factors.items():
        out[name] = (out[name] * factor).astype(out[name].dtype)
    return out
```

```python
from collections import namedtuple
from contextlib import ExitStack, contextmanager
import math

import numpy as np

import concourse.bass as bass
from concourse import mybir

ALU = mybir.AluOpType
ACT = mybir.ActivationFunctionType
AX = mybir.AxisListType
F32 = mybir.dt.float32
F32R = mybir.dt.float32r

P = 128
D_MODEL = 1024
KT = D_MODEL // P
SEQ = 1024
CTX = 256
TOK = SEQ + CTX
NT = TOK // P
LT = SEQ // P
GRID_W = 64
HD = 64
EPS = 1e-6
MASKED = -1.0e30
DIFF_HEADS = 4
LAM_INIT = 0.8 - 0.6 * math.exp(0.0)
FF = 4 * D_MODEL
FFC = 512
MLA_HEADS, MLA_QK, MLA_NOPE, MLA_ROPE, MLA_V = 8, 96, 64, 32, 64
MLA_QL, MLA_KVL = 512, 256
NA_HEADS, NA_COLS, NA_ROWS = 8, 16, 8
RPB_R, RPB_C = 2 * NA_ROWS - 1, 2 * NA_COLS - 1
PADW = 2 * GRID_W - 1


def r32(ap):
    return ap.bitcast(F32R)


def f32(ap):
    return ap.bitcast(F32)


@contextmanager
def phase(nc, name, sems):
    with ExitStack() as st:
        s = namedtuple("Semaphores", sems)(*[st.enter_context(nc.semaphore(f"{name}_{n}")) for n in sems.split()])
        yield s
        with nc.Block() as block:
            @block.sync
            def _(sp):
                for sem in s:
                    sp.sem_clear(sem)


def token_chunks(n):
    return [(c, min(512, n - c)) for c in range(0, n, 512)]


def shape_constants():
    out = {}

    def rope(rot):
        t = np.arange(SEQ, dtype=np.int32)
        row, col = (t // GRID_W).astype(np.float32), (t % GRID_W).astype(np.float32)
        nf = rot // 4
        freqs = np.power(np.float32(10000.0), -np.arange(nf, dtype=np.float32) / np.float32(nf)).astype(np.float32)
        ar, ac = row[:, None] * freqs, col[:, None] * freqs
        ang = np.concatenate([ar, ar, ac, ac], -1).astype(np.float32)
        cos, sin = np.cos(ang), np.sin(ang)
        sign = np.repeat(np.array([-1, 1, -1, 1], np.float32), nf)
        cos = np.concatenate([cos, np.ones((CTX, rot), np.float32)])
        sin = np.concatenate([sin * sign, np.zeros((CTX, rot), np.float32)])
        both = np.stack([cos, sin]).astype(np.float32)
        return np.ascontiguousarray(both.reshape(2, NT, P, rot).transpose(2, 0, 1, 3))

    out["rope64"] = rope(HD)
    out["rope32"] = rope(MLA_ROPE)
    out["ident"] = np.eye(P, dtype=np.float32)
    q, c = np.arange(P)[:, None], np.arange(P)[None, :]
    out["wmask"] = np.stack([np.where(c >= q, 0, MASKED), np.where(c <= q, 0, MASKED)], 1).astype(np.float32)
    cq, ck = np.arange(GRID_W)[:, None], np.arange(GRID_W)[None, :]
    cs = np.clip(cq - NA_COLS // 2, 0, GRID_W - NA_COLS)
    col = np.where((ck >= cs) & (ck < cs + NA_COLS), 0, MASKED).astype(np.float32)
    out["cmask"] = np.concatenate([col, col], 0)
    rm = np.zeros((P, 2), np.float32)
    rm[GRID_W:, 0] = MASKED
    rm[:GRID_W, 1] = MASKED
    out["rmask"] = rm
    return out


class Core:

    def __init__(self, nc, st, ins, out):
        self.nc, self.ins, self.out = nc, ins, out

        def sb(name, shape, dt=F32):
            return st.enter_context(nc.sbuf_tensor(name, shape, dt))

        self.xT = sb("xT", [P, KT, TOK])
        self.rstd = sb("rstd", [P, TOK])
        self.mods = sb("mods", [P, 2, 6, KT, 2])
        self.ident = sb("ident_sb", [P, P])
        self.ones = sb("ones_sb", [P, P])
        self.eps = sb("eps_sb", [P, 1])
        self.ps = st.enter_context(nc.psum_tensor("ps", [P, 8, 512], F32))

        def dram(name, shape):
            return nc.dram_tensor(name, shape, F32, kind="Internal").ap()

        self.qkA = dram("qkA", [16, P, TOK])
        self.vA = dram("vA", [TOK, 512])
        self.qkB = dram("qkB", [10, P, TOK])
        self.vB = dram("vB", [TOK, P])
        self.qkC = dram("qkC", [16, 2, MLA_QK, TOK])
        self.vC = dram("vC", [TOK, 512])
        self.qkD = dram("qkD", [16, P, TOK])
        self.vD = dram("vD", [TOK, 512])
        self.mix = [dram(f"mix{i}", [TOK, D_MODEL]) for i in range(2)]
        self.bias = dram("rpb_bias", [GRID_W, NA_HEADS * RPB_R, GRID_W])


def opening(k):
    nc, i = k.nc, k.ins
    with phase(nc, "open", "consts rows xin0 xin1 aw0 aw1 ones rowsT cols neg e1 inv silu xTd xcp0 xcp1 ada m0 m1 modd") as s, ExitStack() as st:
        def sb(name, shape, dt=F32):
            return st.enter_context(nc.sbuf_tensor(name, shape, dt))
        rows = sb("rows", [48, P])
        brows = sb("brows", [96, P])
        cols = sb("cols", [P, 48])
        bcols = sb("bcols", [P, 96])
        sil = sb("sil", [P, 16])
        tmp = sb("siltmp", [P, 16])
        xin = sb("xin", [P, 2, D_MODEL])
        aw = sb("aw", [P, 2, KT, D_MODEL])
        ada_w = i["ada_w"].rearrange("l (k p) (j n) -> l j p k n", p=P, n=D_MODEL)
        x_rows = i["x"].rearrange("b (t p) d -> (b t) p d", p=P)
        ctx_rows = i["ctx"].rearrange("b (t p) d -> (b t) p d", p=P)
        TB, CB, AB = 0, 4, 6

        with nc.Block() as block:
            @block.sync
            def _(sp):
                sp.dma_start(k.ident[:], i["ident"]).then_inc(s.consts, 16)
                sp.dma_start(rows[0:8, :], i["c"].rearrange("b (k p) -> (b k) p", p=P)).then_inc(s.rows, 16)
                sp.dma_start(rows[8:16, :], i["c_ctx"].rearrange("(k p) -> k p", p=P)).then_inc(s.rows, 16)
                sp.dma_start(rows[16:32, :], i["norm1_g"].rearrange("l (k p) -> (l k) p", p=P)).then_inc(s.rows, 16)
                sp.dma_start(rows[32:48, :], i["norm2_g"].rearrange("l (k p) -> (l k) p", p=P)).then_inc(s.rows, 16)
                sp.dma_start(brows[:], i["ada_b"].rearrange("l (k p) -> (l k) p", p=P)).then_inc(s.rows, 16)
                for t in range(NT):
                    if t < 2:
                        sp.dma_start(aw[:, t], ada_w[0, t]).then_inc(s.aw0 if t == 0 else s.aw1, 16)
                    if t >= 2:
                        sp.wait_ge(s.xTd, t - 1)
                    sp.dma_start(xin[:, t % 2], x_rows[t] if t < LT else ctx_rows[t - LT]).then_inc(
                        s.xin0 if t % 2 == 0 else s.xin1, 16)
                for n in range(2, 12):
                    sp.wait_ge(s.ada, n - 1)
                    sp.dma_start(aw[:, n % 2], ada_w[n // 6, n % 6]).then_inc(s.aw0 if n % 2 == 0 else s.aw1, 16)

            @block.tensor
            def _(pe):
                pe.wait_ge(s.consts, 16)
                pe.wait_ge(s.rows, 80)
                pe.transpose(k.ps[:, CB, 0:48], rows[:], k.ident[0:48, 0:48])
                pe.transpose(k.ps[:, CB, 64:160], brows[:], k.ident[0:96, 0:96]).then_inc(s.rowsT, 1)

                def turn_x(t):
                    pe.wait_ge(s.xin0 if t % 2 == 0 else s.xin1, 16 * (t // 2 + 1))
                    if t >= 2:
                        pe.wait_ge(s.xcp0 if t % 2 == 0 else s.xcp1, 2 * (t // 2))
                    for f in range(KT):
                        b = TB + 2 * (t % 2) + f // 4
                        mm = pe.transpose(k.ps[:, b, (f % 4) * P:(f % 4 + 1) * P], xin[:, t % 2, f * P:(f + 1) * P], k.ident[:])
                    mm.then_inc(s.xTd, 1)

                def ada(n):
                    pe.wait_ge(s.aw0 if n % 2 == 0 else s.aw1, 16 * (n // 2 + 1))
                    if n >= 2:
                        pe.wait_ge(s.modd, n - 1)
                    for j in range(KT):
                        for f in range(KT):
                            mm = pe.matmul(k.ps[:, AB + n % 2, 2 * j:2 * j + 2], aw[:, n % 2, f, j * P:(j + 1) * P],
                                           sil[:, f:16:KT], start=(f == 0), stop=(f == KT - 1))
                    mm.then_inc(s.ada, 1)

                for t in range(NT):
                    turn_x(t)
                    if t == 1:
                        pe.wait_ge(s.silu, 1)
                for n in range(12):
                    ada(n)

            @block.scalar
            def _(act):
                act.wait_ge(s.cols, 2)
                nc.scalar.activation(tmp[:], cols[:, 0:16], ACT.Exp, scale=-1.0).then_inc(s.neg, 1)
                for t in range(NT):
                    act.wait_ge(s.xTd, t + 1)
                    nc.scalar.copy(k.xT[:, 0:4, t * P:(t + 1) * P],
                                   k.ps[:, TB + 2 * (t % 2), :].rearrange("p (f q) -> p f q", q=P)).then_inc(
                        s.xcp0 if t % 2 == 0 else s.xcp1, 1)

            @block.vector
            def _(dve):
                nc.vector.memset(k.ones[:], 1.0).then_inc(s.ones, 1)
                nc.vector.memset(k.eps[:], EPS).then_inc(s.ones, 1)
                dve.wait_ge(s.rowsT, 1)
                nc.vector.tensor_copy(cols[:], k.ps[:, CB, 0:48]).then_inc(s.cols, 1)
                nc.vector.tensor_copy(bcols[:], k.ps[:, CB, 64:160]).then_inc(s.cols, 1)
                dve.wait_ge(s.neg, 1)
                nc.vector.tensor_scalar(tmp[:], tmp[:], 1.0, None, ALU.add).then_inc(s.e1, 1)
                dve.wait_ge(s.e1, 1)
                nc.vector.reciprocal(tmp[:], tmp[:]).then_inc(s.inv, 1)
                dve.wait_ge(s.inv, 1)
                nc.vector.tensor_tensor(sil[:], cols[:, 0:16], tmp[:], ALU.mult).then_inc(s.silu, 1)
                for t in range(NT):
                    dve.wait_ge(s.xTd, t + 1)
                    nc.vector.tensor_copy(k.xT[:, 4:8, t * P:(t + 1) * P],
                                          k.ps[:, TB + 2 * (t % 2) + 1, :].rearrange("p (f q) -> p f q", q=P)).then_inc(
                        s.xcp0 if t % 2 == 0 else s.xcp1, 1)
                for n in range(12):
                    l, j = n // 6, n % 6
                    dve.wait_ge(s.ada, n + 1)
                    bias = bcols[:, n * KT:(n + 1) * KT].unsqueeze(2).broadcast_to([P, KT, 2])
                    m = k.mods[:, l, j]
                    nc.vector.tensor_tensor(m, k.ps[:, AB + n % 2, 0:16].rearrange("p (f w) -> p f w", w=2), bias,
                                            ALU.add).then_inc(s.modd, 1)
                    if j in (1, 4):
                        g = cols[:, (16 if j == 1 else 32) + l * KT:(16 if j == 1 else 32) + (l + 1) * KT]
                        dve.wait_ge(s.modd, n + 1)
                        nc.vector.scalar_tensor_tensor(out=m, in0=m, scalar=1.0, in1=g.unsqueeze(2).broadcast_to([P, KT, 2]),
                                                       op0=ALU.add, op1=ALU.mult).then_inc(s.m0, 1)


def norm_stats(k, name, n_tok):
    nc = k.nc
    with phase(nc, name, "sq acc sum root") as s, ExitStack() as st:
        sq = st.enter_context(nc.sbuf_tensor(f"{name}_sq", [P, 2, TOK], F32))
        acc = st.enter_context(nc.sbuf_tensor(f"{name}_acc", [P, TOK], F32))
        chunks = token_chunks(n_tok)
        with nc.Block() as block:
            @block.scalar
            def _(act):
                for f in range(KT):
                    if f >= 2:
                        act.wait_ge(s.acc, f - 1)
                    nc.scalar.activation(sq[:, f % 2, 0:n_tok], k.xT[:, f, 0:n_tok], ACT.Square).then_inc(s.sq, 1)
                act.wait_ge(s.sum, 1)
                for c, (c0, n) in enumerate(chunks):
                    nc.scalar.activation(k.rstd[:, c0:c0 + n], k.ps[:, c, 0:n], ACT.Sqrt, bias=k.eps[:],
                                         scale=1.0 / D_MODEL).then_inc(s.root, 1)

            @block.vector
            def _(dve):
                for f in range(KT):
                    dve.wait_ge(s.sq, f + 1)
                    if f == 0:
                        nc.vector.tensor_copy(acc[:, 0:n_tok], sq[:, 0, 0:n_tok]).then_inc(s.acc, 1)
                    else:
                        dve.wait_ge(s.acc, f)
                        nc.vector.tensor_tensor(acc[:, 0:n_tok], acc[:, 0:n_tok], sq[:, f % 2, 0:n_tok],
                                                ALU.add).then_inc(s.acc, 1)
                for c, (c0, n) in enumerate(chunks):
                    dve.wait_ge(s.root, c + 1)
                    nc.vector.reciprocal(k.rstd[:, c0:c0 + n], k.rstd[:, c0:c0 + n])

            @block.tensor
            def _(pe):
                pe.wait_ge(s.acc, KT)
                for c, (c0, n) in enumerate(chunks):
                    mm = pe.matmul(k.ps[:, c, 0:n], k.ones[:], acc[:, c0:c0 + n], start=True, stop=True)
                mm.then_inc(s.sum, 1)


def at_tile(i, p):
    return i * 2 + p


def wait_then_store(sp, sem, value, begun):
    sp.wait_ge(sem, value)
    sp.sem_inc(begun, 1)


def walk_pairs(eng, pair):
    pair(0, True, False)
    with eng.Fori(1, NT // 2 - 1) as i:
        pair(i, False, False)
    pair(NT // 2 - 1, False, True)


def load_weights(sp, s, raw, w_dram, n_k, first_waits=None):
    for f in range(n_k):
        if f >= 2:
            sp.wait_ge(s.wlo, f - 1)
        sp.dma_start(raw[:, f % 2], w_dram[f]).then_inc(s.wraw0 if f % 2 == 0 else s.wraw1, 16)


def cut_hi(nc, act, s, raw, wh, n_k):
    for f in range(n_k):
        act.wait_ge(s.wraw0 if f % 2 == 0 else s.wraw1, 16 * (f // 2 + 1))
        nc.scalar.copy(wh[:, f], raw[:, f % 2]).then_inc(s.whi, 1)


def cut_lo(nc, dve, s, raw, wh, wl, n_k):
    for f in range(n_k):
        dve.wait_ge(s.whi, f + 1)
        nc.vector.tensor_tensor(wl[:, f], raw[:, f % 2], f32(wh[:, f]), ALU.subtract).then_inc(s.wlo, 1)


class Unit:

    def __init__(self, c0, width, heads=0, gain=None, gain_scale=1.0, rope=False, dst=None, base=0, v=0, v_dst=None):
        self.c0, self.width, self.heads, self.gain, self.gain_scale = c0, width, heads, gain, gain_scale
        self.rope, self.dst, self.base, self.v, self.v_dst = rope, dst, base, v, v_dst


def project(k, name, layer, w_in, col0, n_cols, units):
    nc = k.nc
    U = len(units)
    hu = [j for j, u in enumerate(units) if u.heads]
    HU = len(hu)
    vu = [j for j, u in enumerate(units) if u.v]
    VU = len(vu)
    assert HU == 2
    ropes = sum(1 for j in hu if units[j].rope)
    assert ropes in (0, 2)
    slots = []
    for j in range(U):
        slots.append(("mm", j))
        if j == 0 and hu[-1] == U - 1:
            slots.append(("turn", HU - 1, -1))
        for n, h in enumerate(hu):
            if h == j - 1:
                slots.append(("turn", n, 0))
    names = ("gains ropec fbase fmod h wraw0 wraw1 whi wlo mm sq red y root ri yn u w yf hi lo tr tc qd0 qd1 vc va0 va1 vb0 vb1 modt ht begun")
    with phase(nc, name, names) as s, ExitStack() as st:
        def sb(nm, shape, dt=F32):
            return st.enter_context(nc.sbuf_tensor(f"{name}_{nm}", shape, dt))
        wh, wl = sb("wh", [P, KT, n_cols], F32R), sb("wl", [P, KT, n_cols], F32R)
        raw = sb("wraw", [P, 2, n_cols])
        h = sb("hfull", [P, KT, P])
        hh, hl = sb("hh", [P, 2, KT, P], F32R), sb("hl", [P, 2, KT, P], F32R)
        modt = sb("modt", [P, NT, 2, KT])
        sq, y = sb("sqh", [P, 512]), sb("yh", [P, 512])
        w_, u_ = (sb("w_", [P, 512]), sb("u_", [P, 512])) if ropes else (None, None)
        rs = sb("rsh", [P, 8])
        qh = [sb(f"qh{n}", [P, 8, 2, HD], F32R) for n in range(HU)]
        stage = sb("stage", [P, 2, 8, P])
        vst = [sb(f"vst{n}", [P, 2, units[j].v]) for n, j in enumerate(vu)]
        gain = [sb(f"gain{n}", [P, HD]) for n in range(HU)]
        rope = sb("rope", [P, 2, NT, HD]) if ropes else None
        sint = sb("sint", [P, 2, HD]) if ropes else None
        w_dram = w_in.rearrange("(f p) n -> f p n", p=P)[:, :, col0:col0 + n_cols]
        TB = 4

        def v_stored(j, p):
            return ((s.va0, s.va1), (s.vb0, s.vb1))[vu.index(j)][p]

        def done(i, p, per, j):
            return (i * 2 + p) * per + j + 1

        with nc.Block() as block:
            @block.sync
            def _(sp):
                for n, j in enumerate(hu):
                    sp.dma_start(gain[n][:], units[j].gain.unsqueeze(0).broadcast_to([P, HD])).then_inc(s.gains, 16)
                if ropes:
                    sp.dma_start(rope[:], k.ins["rope64"]).then_inc(s.ropec, 16)
                load_weights(sp, s, raw, w_dram, KT)

                def store_heads(n, i, p):
                    u = units[hu[n]]
                    wait_then_store(sp, s.tc, done(i, p, HU, n), s.begun)
                    dst = u.dst[u.base:u.base + u.heads].rearrange("h r q -> r h q")
                    sp.dma_start(dst[:, :, bass.ds(at_tile(i, p) * P, P)], stage[:, n, 0:u.heads]).then_inc(
                        s.qd0 if n == 0 else s.qd1, 16)

                def store_v(j, i, p):
                    n = vu.index(j)
                    wait_then_store(sp, s.vc, done(i, p, VU, n), s.begun)
                    sp.dma_start(units[j].v_dst[bass.ds(at_tile(i, p) * P, P)], vst[n][:, p]).then_inc(v_stored(j, p), 16)

                def pair(i, first, last):
                    for p in range(2):
                        for slot in slots:
                            if slot[0] == "turn" and not (first and p + slot[2] < 0):
                                store_heads(slot[1], i, p + slot[2])
                            if slot[0] == "mm" and units[slot[1]].v:
                                store_v(slot[1], i, p)
                walk_pairs(sp, pair)
                if hu[-1] == U - 1:
                    store_heads(HU - 1, NT // 2 - 1, 1)
                sp.wait_ge(s.qd0, 16 * NT)
                sp.wait_ge(s.qd1, 16 * NT)
                for j in vu:
                    for p in range(2):
                        sp.wait_ge(v_stored(j, p), 16 * (NT // 2))

            @block.tensor
            def _(pe):
                def products(j, i, p, first):
                    u = units[j]
                    if j == 0:
                        pe.wait_ge(s.h, done(i, p, 1, 0))
                    if not (first and p == 0):
                        if u.heads:
                            pe.wait_ge(s.y, done(i, p - 1, HU, hu.index(j)))
                        else:
                            pe.wait_ge(s.vc, done(i, p - 1, VU, vu.index(j)))
                    c = slice(u.c0, u.c0 + u.width)
                    for f in range(KT):
                        if first and p == 0 and j == 0:
                            pe.wait_ge(s.wlo, f + 1)
                        o = k.ps[:, j, 0:u.width]
                        pe.matmul(o, hh[:, p, f], wh[:, f, c], start=(f == 0), stop=False)
                        pe.matmul(o, hh[:, p, f], wl[:, f, c], start=False, stop=False)
                        mm = pe.matmul(o, hl[:, p, f], wh[:, f, c], start=False, stop=(f == KT - 1))
                    mm.then_inc(s.mm, 1)

                def turn(n, i, p, free):
                    u = units[hu[n]]
                    pe.wait_ge(s.lo, done(i, p, HU, n))
                    if free:
                        pe.wait_ge(s.tc, done(i, p - 1, HU, n))
                    for x in range(u.heads):
                        mm = pe.transpose(k.ps[:, TB + 2 * n + x // 4, (x % 4) * P:(x % 4 + 1) * P],
                                          f32(qh[n][:, x].rearrange("p a d -> p (a d)")), k.ident[:])
                    mm.then_inc(s.tr, 1)

                def pair(i, first, last):
                    for p in range(2):
                        for slot in slots:
                            if slot[0] == "mm":
                                products(slot[1], i, p, first)
                            elif not (first and p + slot[2] < 0):
                                turn(slot[1], i, p + slot[2], not (first and p + slot[2] <= 0))
                walk_pairs(pe, pair)
                if hu[-1] == U - 1:
                    turn(HU - 1, NT // 2 - 1, 1, True)

            @block.scalar
            def _(act):
                def modulate(i, p):
                    t = at_tile(i, p)
                    act.wait_ge(s.fbase, done(i, p, 1, 0))
                    if ropes:
                        nc.scalar.copy(sint[:, p % 2], rope[:, 1, bass.ds(t, 1)].squeeze(1))
                    for f in range(KT):
                        a = nc.scalar.activation(h[:, f], h[:, f], ACT.Identity,
                                                 scale=modt[:, bass.ds(t, 1), 0, f],
                                                 bias=modt[:, bass.ds(t, 1), 1, f])
                    a.then_inc(s.fmod, 1)

                def squares(j, i, p, first):
                    u, n = units[j], hu.index(j)
                    act.wait_ge(s.mm, done(i, p, U, j))
                    if not (first and p == 0 and n == 0):
                        act.wait_ge(s.red, done(i, p, HU, n - 1))
                    nc.scalar.activation(sq[:, 0:u.heads * HD], k.ps[:, j, 0:u.heads * HD], ACT.Square).then_inc(s.sq, 1)
                    act.wait_ge(s.red, done(i, p, HU, n))
                    nc.scalar.activation(rs[:, 0:u.heads], rs[:, 0:u.heads], ACT.Sqrt, bias=k.eps[:],
                                         scale=1.0 / HD).then_inc(s.root, 1)

                def values(j, i, p, first):
                    u = units[j]
                    act.wait_ge(s.mm, done(i, p, U, j))
                    if not first:
                        act.wait_ge(v_stored(j, p), i * 16)
                    nc.scalar.copy(vst[vu.index(j)][:, p], k.ps[:, j, u.heads * HD:u.heads * HD + u.v]).then_inc(s.vc, 1)

                def stage_heads(n, i, p, free):
                    u = units[hu[n]]
                    act.wait_ge(s.tr, done(i, p, HU, n))
                    if free:
                        act.wait_ge(s.qd0 if n == 0 else s.qd1, at_tile(i, p) * 16)
                    nc.scalar.copy(stage[:, n, 0:u.heads],
                                   k.ps[:, TB + 2 * n:TB + 2 * n + 2].rearrange("p b (x q) -> p (b x) q", q=P)[:, 0:u.heads]).then_inc(s.tc, 1)

                act.wait_ge(s.modt, 2)
                if ropes:
                    act.wait_ge(s.ropec, 16)
                modulate(0, 0)
                cut_hi(nc, act, s, raw, wh, KT)

                def pair(i, first, last):
                    for p in range(2):
                        for x, slot in enumerate(slots):
                            if slot[0] == "mm":
                                if units[slot[1]].v:
                                    values(slot[1], i, p, first)
                                if units[slot[1]].heads:
                                    squares(slot[1], i, p, first)
                            elif not (first and p + slot[2] < 0):
                                stage_heads(slot[1], i, p + slot[2], not (first and p + slot[2] <= 0))
                            if x == 0 and not (last and p == 1):
                                modulate(i, p + 1)
                walk_pairs(act, pair)
                if hu[-1] == U - 1:
                    stage_heads(HU - 1, NT // 2 - 1, 1, True)

            @block.vector
            def _(dve):
                for w in range(2):
                    dst = modt[:, 0:LT, :, :] if w == 0 else modt[:, LT:NT, :, :]
                    n = LT if w == 0 else NT - LT
                    for c, part in ((0, 1), (1, 0)):
                        m = nc.vector.tensor_copy(dst[:, :, c], k.mods[:, layer, part, :, w].unsqueeze(1).broadcast_to([P, n, KT]))
                    m.then_inc(s.modt, 1)
                dve.wait_ge(s.gains, 16 * HU)
                for n, j in enumerate(hu):
                    if units[j].gain_scale != 1.0:
                        nc.vector.tensor_scalar(gain[n][:], gain[n][:], units[j].gain_scale, None, ALU.mult).then_inc(s.modt, 1)
                scaled = 2 + sum(1 for j in hu if units[j].gain_scale != 1.0)

                def base(i, p, first):
                    q = bass.ds(at_tile(i, p) * P, P)
                    if not first:
                        dve.wait_ge(s.h, done(i, p - 1, 1, 0))
                    nc.vector.tensor_tensor(h[:], k.xT[:, :, q], k.rstd[:, q].unsqueeze(1).broadcast_to([P, KT, P]),
                                            ALU.mult).then_inc(s.fbase, 1)

                def cut(i, p, first):
                    dve.wait_ge(s.fmod, done(i, p, 1, 0))
                    if not first:
                        dve.wait_ge(s.mm, done(i, p - 2, U, U - 1))
                    nc.vector.tensor_copy(hh[:, p % 2], h[:]).then_inc(s.ht, 1)
                    dve.wait_ge(s.ht, done(i, p, 1, 0))
                    nc.vector.tensor_tensor(hl[:, p % 2], h[:], f32(hh[:, p % 2]), ALU.subtract).then_inc(s.h, 1)

                def heads(j, i, p, first):
                    u, n = units[j], hu.index(j)
                    H, W = u.heads, u.heads * HD
                    me = done(i, p, HU, n)
                    v3 = lambda ap: ap[:, 0:W].rearrange("p (h d) -> p h d", d=HD)
                    dve.wait_ge(s.sq, me)
                    if not (first and p == 0 and n == 0):
                        dve.wait_ge(s.lo, done(i, p, HU, n - 1))
                    nc.vector.tensor_reduce(rs[:, 0:H], v3(sq), AX.X, ALU.add).then_inc(s.red, 1)
                    nc.vector.tensor_tensor(v3(y), v3(k.ps[:, j]), gain[n][:].unsqueeze(1).broadcast_to([P, H, HD]),
                                            ALU.mult).then_inc(s.y, 1)
                    dve.wait_ge(s.root, me)
                    nc.vector.reciprocal(rs[:, 0:H], rs[:, 0:H]).then_inc(s.ri, 1)
                    dve.wait_ge(s.ri, me)
                    dve.wait_ge(s.y, me)
                    nc.vector.tensor_tensor(v3(y), v3(y), rs[:, 0:H].unsqueeze(2).broadcast_to([P, H, HD]),
                                            ALU.mult).then_inc(s.yn, 1)
                    dve.wait_ge(s.yn, me)
                    if ropes:
                        cos = rope[:, 0, bass.ds(at_tile(i, p), 1)].broadcast_to([P, H, HD])
                        nc.vector.tensor_tensor(v3(w_), v3(y), cos, ALU.mult).then_inc(s.w, 1)
                        dve.wait_ge(s.w, me)
                        dve.wait_ge(s.u, me)
                        nc.vector.tensor_tensor(y[:, 0:W], w_[:, 0:W], u_[:, 0:W], ALU.add).then_inc(s.yf, 1)
                        dve.wait_ge(s.yf, me)
                    if not (first and p == 0):
                        dve.wait_ge(s.tr, done(i, p - 1, HU, n))
                    nc.vector.tensor_copy(qh[n][:, 0:H, 0], v3(y)).then_inc(s.hi, 1)
                    dve.wait_ge(s.hi, me)
                    nc.vector.tensor_tensor(qh[n][:, 0:H, 1], v3(y), f32(qh[n][:, 0:H, 0]), ALU.subtract).then_inc(s.lo, 1)

                base(0, 0, True)
                cut(0, 0, True)
                cut_lo(nc, dve, s, raw, wh, wl, KT)
                dve.wait_ge(s.modt, scaled)
                if ropes:
                    dve.wait_ge(s.ropec, 16)

                def pair(i, first, last):
                    for p in range(2):
                        more = not (last and p == 1)
                        if more:
                            base(i, p + 1, False)
                        for x, j in enumerate(hu):
                            heads(j, i, p, first)
                            if x == 0 and more:
                                cut(i, p + 1, first and p == 0)
                walk_pairs(dve, pair)

            @block.gpsimd
            def _(pool):
                if ropes:
                    def pair(i, first, last):
                        for p in range(2):
                            for n, j in enumerate(hu):
                                H = units[j].heads
                                pool.wait_ge(s.yn, done(i, p, HU, n))
                                v5 = lambda ap: ap[:, 0:H * HD].rearrange("p (h a b d) -> p h a b d", a=2, b=2, d=HD // 4)
                                sin = sint[:, p:p + 1].rearrange("p o (a b d) -> p o a b d", a=2, b=2)
                                for b in range(2):
                                    ins = nc.gpsimd.tensor_tensor(v5(u_)[:, :, :, b], v5(y)[:, :, :, 1 - b],
                                                                  sin[:, :, :, b].broadcast_to([P, H, 2, HD // 4]), ALU.mult)
                                ins.then_inc(s.u, 1)
                    walk_pairs(pool, pair)


def project_low_rank(k, name, layer, w_in, col0, n_cols, rank, rank_gain, w_up, heads_gain, gain_scale, base, with_values):
    nc = k.nc
    H, D, R = MLA_HEADS, MLA_QK, MLA_ROPE
    RT = rank // P
    up = w_up.shape[1]
    UC = token_chunks(up)
    names = ("gains ropec fbase fmod h ht wraw0 wraw1 whi wlo ur0 ur1 uhi ulo mm sql rl rli low ah alo at atc up kn kr vc "
             "sqd red y root ri yn w u yf hi lo tr tc qd0 qd1 qd2 qd3 va0 va1 modt begun")
    with phase(nc, name, names) as s, ExitStack() as st:
        def sb(nm, shape, dt=F32):
            return st.enter_context(nc.sbuf_tensor(f"{name}_{nm}", shape, dt))
        wh, wl = sb("wh", [P, KT, n_cols], F32R), sb("wl", [P, KT, n_cols], F32R)
        uh, ul = sb("uph", [P, RT, up], F32R), sb("upl", [P, RT, up], F32R)
        raw, uraw = sb("wraw", [P, 2, n_cols]), sb("uraw", [P, 2, up])
        h = sb("hfull", [P, KT, P])
        hh, hl = sb("hh", [P, 2, KT, P], F32R), sb("hl", [P, 2, KT, P], F32R)
        modt = sb("modt", [P, NT, 2, KT])
        lsum, lr = sb("lsum", [P, 1]), sb("lr", [P, 1])
        low = sb("low", [P, rank])
        lowc = sb("lowc", [P, 2, rank], F32R)
        lowT = sb("lowT", [P, 2, RT, P], F32R)
        kr = sb("kr", [P, 2, R]) if with_values else None
        sq, y = sb("sqh", [P, H, D]), sb("yh", [P, H, D])
        w_, u_ = sb("w_", [P, H, R]), sb("u_", [P, H, R])
        rs = sb("rsh", [P, H])
        qh = sb("qh", [P, H, 2, D], F32R)
        stage = sb("stage", [D, 4, 4, P])
        vst = sb("vst", [P, 2, H * MLA_V]) if with_values else None
        rgain, gain = sb("rgain", [P, rank]), sb("gain", [P, D])
        rope = sb("rope", [P, 2, NT, R])
        w_dram = w_in.rearrange("(f p) n -> f p n", p=P)[:, :, col0:col0 + n_cols]
        u_dram = w_up.rearrange("(f p) n -> f p n", p=P)
        IB, LB, UB, TB = 0, 1, 3, 5
        ups = k.ps[:, UB:UB + 2].rearrange("p b c -> p (b c)")

        def n1(i, p):
            return i * 2 + p + 1

        def batch(i, p, b):
            return (i * 2 + p) * 4 + b + 1

        with nc.Block() as block:
            @block.sync
            def _(sp):
                sp.dma_start(rgain[:], rank_gain.unsqueeze(0).broadcast_to([P, rank])).then_inc(s.gains, 16)
                sp.dma_start(gain[:], heads_gain.unsqueeze(0).broadcast_to([P, D])).then_inc(s.gains, 16)
                sp.dma_start(rope[:], k.ins["rope32"]).then_inc(s.ropec, 16)
                load_weights(sp, s, raw, w_dram, KT)
                for f in range(RT):
                    if f >= 2:
                        sp.wait_ge(s.ulo, f - 1)
                    sp.dma_start(uraw[:, f % 2], u_dram[f]).then_inc(s.ur0 if f % 2 == 0 else s.ur1, 16)

                def pair(i, first, last):
                    for p in range(2):
                        if with_values:
                            wait_then_store(sp, s.vc, n1(i, p), s.begun)
                            sp.dma_start(k.vC[bass.ds(at_tile(i, p) * P, P)], vst[:, p]).then_inc(s.va0 if p == 0 else s.va1, 16)
                        for b in range(4):
                            wait_then_store(sp, s.tc, batch(i, p, b), s.begun)
                            dst = k.qkC[base + 2 * b:base + 2 * b + 2].rearrange("h a r q -> r (h a) q")
                            sp.dma_start(dst[:, :, bass.ds(at_tile(i, p) * P, P)], stage[:, b]).then_inc(
                                (s.qd0, s.qd1, s.qd2, s.qd3)[b], 16)
                walk_pairs(sp, pair)
                for q in (s.qd0, s.qd1, s.qd2, s.qd3):
                    sp.wait_ge(q, 16 * NT)
                if with_values:
                    sp.wait_ge(s.va0, 16 * (NT // 2))
                    sp.wait_ge(s.va1, 16 * (NT // 2))

            @block.tensor
            def _(pe):
                def products(i, p, first):
                    pe.wait_ge(s.h, n1(i, p))
                    if not (first and p == 0):
                        pe.wait_ge(s.low, n1(i, p - 1))
                        if with_values:
                            pe.wait_ge(s.kr, n1(i, p - 1))
                    for f in range(KT):
                        if first and p == 0:
                            pe.wait_ge(s.wlo, f + 1)
                        o = k.ps[:, IB, 0:n_cols]
                        pe.matmul(o, hh[:, p, f], wh[:, f], start=(f == 0), stop=False)
                        pe.matmul(o, hh[:, p, f], wl[:, f], start=False, stop=False)
                        mm = pe.matmul(o, hl[:, p, f], wh[:, f], start=False, stop=(f == KT - 1))
                    mm.then_inc(s.mm, 1)

                def turn_low(i, p, free):
                    pe.wait_ge(s.alo, n1(i, p))
                    if free:
                        pe.wait_ge(s.atc, n1(i, p - 1))
                    for a in range(2):
                        for f in range(RT):
                            mm = pe.transpose(k.ps[:, LB + a, f * P:(f + 1) * P], f32(lowc[:, a, f * P:(f + 1) * P]), k.ident[:])
                    mm.then_inc(s.at, 1)

                def up_products(i, p, free, first):
                    pe.wait_ge(s.atc, n1(i, p))
                    if free:
                        pe.wait_ge(s.y if not with_values else s.vc, n1(i, p - 1))
                    if first:
                        pe.wait_ge(s.ulo, RT)
                    for c0, n in UC:
                        for f in range(RT):
                            o, c = ups[:, c0:c0 + n], slice(c0, c0 + n)
                            pe.matmul(o, lowT[:, 0, f], uh[:, f, c], start=(f == 0), stop=False)
                            pe.matmul(o, lowT[:, 0, f], ul[:, f, c], start=False, stop=False)
                            mm = pe.matmul(o, lowT[:, 1, f], uh[:, f, c], start=False, stop=(f == RT - 1))
                    mm.then_inc(s.up, 1)

                def turn_heads(i, p, free):
                    pe.wait_ge(s.lo, n1(i, p))
                    for b in range(4):
                        if free or b >= 2:
                            pe.wait_ge(s.tc, batch(i, p, b - 2))
                        for x in range(4):
                            mm = pe.transpose(k.ps[0:D, TB + b % 2, x * P:(x + 1) * P],
                                              f32(qh[:, 2 * b + x // 2, x % 2]), k.ident[:])
                        mm.then_inc(s.tr, 1)

                def pair(i, first, last):
                    for p in range(2):
                        products(i, p, first)
                        if not (first and p == 0):
                            turn_heads(i, p - 1, not (first and p == 1))
                        turn_low(i, p, not (first and p == 0))
                        up_products(i, p, not (first and p == 0), first and p == 0)
                walk_pairs(pe, pair)
                turn_heads(NT // 2 - 1, 1, True)

            @block.scalar
            def _(act):
                def modulate(i, p):
                    t = at_tile(i, p)
                    act.wait_ge(s.fbase, n1(i, p))
                    for f in range(KT):
                        a = nc.scalar.activation(h[:, f], h[:, f], ACT.Identity, scale=modt[:, bass.ds(t, 1), 0, f],
                                                 bias=modt[:, bass.ds(t, 1), 1, f])
                    a.then_inc(s.fmod, 1)

                def low_rank(i, p, first):
                    act.wait_ge(s.mm, n1(i, p))
                    if with_values:
                        if not first:
                            act.wait_ge(s.kn, n1(i, p - 2))
                        nc.scalar.copy(kr[:, p], k.ps[:, IB, rank:rank + R]).then_inc(s.kr, 1)
                    if not (first and p == 0):
                        act.wait_ge(s.low, n1(i, p - 1))
                        act.wait_ge(s.red, n1(i, p - 1))
                    nc.scalar.activation(sq[:].rearrange("p h d -> p (h d)")[:, 0:rank], k.ps[:, IB, 0:rank], ACT.Square,
                                         accum_out=lsum[:]).then_inc(s.sql, 1)
                    act.wait_ge(s.sql, n1(i, p))
                    nc.scalar.activation(lr[:], lsum[:], ACT.Sqrt, bias=k.eps[:], scale=1.0 / rank).then_inc(s.rl, 1)

                def stage_low(i, p, free):
                    act.wait_ge(s.at, n1(i, p))
                    if free:
                        act.wait_ge(s.up, n1(i, p - 1))
                    nc.scalar.copy(lowT[:], k.ps[:, LB:LB + 2].rearrange("p a (f q) -> p a f q", q=P)[:, :, 0:RT]).then_inc(s.atc, 1)

                def heads(i, p, first):
                    act.wait_ge(s.up, n1(i, p))
                    if with_values:
                        if not (first and p == 0):
                            act.wait_ge(s.lo, n1(i, p - 1))
                        if not first:
                            act.wait_ge(s.va0 if p == 0 else s.va1, i * 16)
                        up3 = ups.rearrange("p (h d) -> p h d", d=MLA_NOPE + MLA_V)
                        nc.scalar.copy(y[:, :, 0:MLA_NOPE], up3[:, :, 0:MLA_NOPE])
                        nc.scalar.copy(y[:, :, MLA_NOPE:D], kr[:, p:p + 1].broadcast_to([P, H, R])).then_inc(s.kn, 1)
                        nc.scalar.copy(vst[:, p].rearrange("p (h d) -> p h d", d=MLA_V), up3[:, :, MLA_NOPE:]).then_inc(s.vc, 1)
                        act.wait_ge(s.kn, n1(i, p))
                        nc.scalar.activation(sq[:], y[:], ACT.Square).then_inc(s.sqd, 1)
                    else:
                        nc.scalar.activation(sq[:], ups[:, 0:H * D].rearrange("p (h d) -> p h d", d=D), ACT.Square).then_inc(s.sqd, 1)
                    act.wait_ge(s.red, n1(i, p))
                    nc.scalar.activation(rs[:], rs[:], ACT.Sqrt, bias=k.eps[:], scale=1.0 / D).then_inc(s.root, 1)

                def stage_heads(i, p, free):
                    for b in range(4):
                        act.wait_ge(s.tr, batch(i, p, b))
                        if free:
                            act.wait_ge((s.qd0, s.qd1, s.qd2, s.qd3)[b], at_tile(i, p) * 16)
                        nc.scalar.copy(stage[:, b], k.ps[0:D, TB + b % 2].rearrange("p (x q) -> p x q", q=P)).then_inc(s.tc, 1)

                act.wait_ge(s.modt, 2)
                modulate(0, 0)
                cut_hi(nc, act, s, raw, wh, KT)
                for f in range(RT):
                    act.wait_ge(s.ur0 if f % 2 == 0 else s.ur1, 16 * (f // 2 + 1))
                    nc.scalar.copy(uh[:, f], uraw[:, f % 2]).then_inc(s.uhi, 1)

                def pair(i, first, last):
                    for p in range(2):
                        low_rank(i, p, first)
                        if not (first and p == 0):
                            stage_heads(i, p - 1, not (first and p == 1))
                        stage_low(i, p, not (first and p == 0))
                        if not (last and p == 1):
                            modulate(i, p + 1)
                        heads(i, p, first)
                walk_pairs(act, pair)
                stage_heads(NT // 2 - 1, 1, True)

            @block.vector
            def _(dve):
                for w in range(2):
                    dst = modt[:, 0:LT, :, :] if w == 0 else modt[:, LT:NT, :, :]
                    n = LT if w == 0 else NT - LT
                    for c, part in ((0, 1), (1, 0)):
                        m = nc.vector.tensor_copy(dst[:, :, c], k.mods[:, layer, part, :, w].unsqueeze(1).broadcast_to([P, n, KT]))
                    m.then_inc(s.modt, 1)
                dve.wait_ge(s.gains, 32)
                nc.vector.tensor_scalar(gain[:], gain[:], gain_scale, None, ALU.mult).then_inc(s.modt, 1)

                def base_(i, p, first):
                    q = bass.ds(at_tile(i, p) * P, P)
                    if not first:
                        dve.wait_ge(s.h, n1(i, p - 1))
                    nc.vector.tensor_tensor(h[:], k.xT[:, :, q], k.rstd[:, q].unsqueeze(1).broadcast_to([P, KT, P]),
                                            ALU.mult).then_inc(s.fbase, 1)

                def cut(i, p, first):
                    dve.wait_ge(s.fmod, n1(i, p))
                    if not first:
                        dve.wait_ge(s.mm, n1(i, p - 2))
                    nc.vector.tensor_copy(hh[:, p % 2], h[:]).then_inc(s.ht, 1)
                    dve.wait_ge(s.ht, n1(i, p))
                    nc.vector.tensor_tensor(hl[:, p % 2], h[:], f32(hh[:, p % 2]), ALU.subtract).then_inc(s.h, 1)

                def low_rank(i, p, first):
                    me = n1(i, p)
                    dve.wait_ge(s.rl, me)
                    nc.vector.reciprocal(lr[:], lr[:]).then_inc(s.rli, 1)
                    dve.wait_ge(s.rli, me)
                    if not (first and p == 0):
                        dve.wait_ge(s.alo, n1(i, p - 1))
                    nc.vector.scalar_tensor_tensor(out=low[:], in0=k.ps[:, IB, 0:rank], scalar=lr[:, 0:1], in1=rgain[:],
                                                   op0=ALU.mult, op1=ALU.mult).then_inc(s.low, 1)
                    dve.wait_ge(s.low, me)
                    if not (first and p == 0):
                        dve.wait_ge(s.at, n1(i, p - 1))
                    nc.vector.tensor_copy(lowc[:, 0], low[:]).then_inc(s.ah, 1)
                    dve.wait_ge(s.ah, me)
                    nc.vector.tensor_tensor(lowc[:, 1], low[:], f32(lowc[:, 0]), ALU.subtract).then_inc(s.alo, 1)

                def heads(i, p, first):
                    me = n1(i, p)
                    dve.wait_ge(s.sqd, me)
                    nc.vector.tensor_reduce(rs[:], sq[:], AX.X, ALU.add).then_inc(s.red, 1)
                    src = y[:] if with_values else ups[:, 0:H * D].rearrange("p (h d) -> p h d", d=D)
                    if not with_values and not (first and p == 0):
                        dve.wait_ge(s.lo, n1(i, p - 1))
                    nc.vector.tensor_tensor(y[:], src, gain[:].unsqueeze(1).broadcast_to([P, H, D]), ALU.mult).then_inc(s.y, 1)
                    dve.wait_ge(s.root, me)
                    nc.vector.reciprocal(rs[:], rs[:]).then_inc(s.ri, 1)
                    dve.wait_ge(s.ri, me)
                    dve.wait_ge(s.y, me)
                    nc.vector.tensor_tensor(y[:], y[:], rs[:].unsqueeze(2).broadcast_to([P, H, D]), ALU.mult).then_inc(s.yn, 1)
                    dve.wait_ge(s.yn, me)
                    if not (first and p == 0):
                        dve.wait_ge(s.yf, n1(i, p - 1))
                    t = bass.ds(at_tile(i, p), 1)
                    rot = y[:, :, MLA_NOPE:D]
                    nc.vector.tensor_tensor(w_[:], rot, rope[:, 0, t].broadcast_to([P, H, R]), ALU.mult).then_inc(s.w, 1)
                    v5 = lambda ap: ap.rearrange("p h (a b d) -> p h a b d", a=2, b=2)
                    sin = v5(rope[:, 1, t])
                    for b in range(2):
                        ins = nc.vector.tensor_tensor(v5(u_[:])[:, :, :, b], v5(rot)[:, :, :, 1 - b],
                                                      sin[:, :, :, b].broadcast_to([P, H, 2, R // 4]), ALU.mult)
                    ins.then_inc(s.u, 1)
                    dve.wait_ge(s.w, me)
                    dve.wait_ge(s.u, me)
                    nc.vector.tensor_tensor(rot, w_[:], u_[:], ALU.add).then_inc(s.yf, 1)
                    dve.wait_ge(s.yf, me)
                    if not (first and p == 0):
                        dve.wait_ge(s.tr, batch(i, p - 1, 3))
                    nc.vector.tensor_copy(qh[:, :, 0], y[:]).then_inc(s.hi, 1)
                    dve.wait_ge(s.hi, me)
                    nc.vector.tensor_tensor(qh[:, :, 1], y[:], f32(qh[:, :, 0]), ALU.subtract).then_inc(s.lo, 1)

                base_(0, 0, True)
                cut(0, 0, True)
                cut_lo(nc, dve, s, raw, wh, wl, KT)
                for f in range(RT):
                    dve.wait_ge(s.uhi, f + 1)
                    nc.vector.tensor_tensor(ul[:, f], uraw[:, f % 2], f32(uh[:, f]), ALU.subtract).then_inc(s.ulo, 1)
                dve.wait_ge(s.modt, 3)
                dve.wait_ge(s.ropec, 16)

                def pair(i, first, last):
                    for p in range(2):
                        low_rank(i, p, first)
                        if not (last and p == 1):
                            base_(i, p + 1, False)
                            cut(i, p + 1, first and p == 0)
                        heads(i, p, first)
                walk_pairs(dve, pair)


def bias_pad(k, rpb):
    nc = k.nc
    with phase(nc, "pad", "zero rows wide bias") as s, ExitStack() as st:
        rows = st.enter_context(nc.sbuf_tensor("pad_rows", [NA_HEADS * RPB_R, PADW + 1], F32))
        wide = st.enter_context(nc.sbuf_tensor("pad_wide", [NA_HEADS * RPB_R, GRID_W * (PADW + 1)], F32))
        with nc.Block() as block:
            @block.vector
            def _(dve):
                nc.vector.memset(rows[:], 0.0).then_inc(s.zero, 1)
                dve.wait_ge(s.rows, 16)
                nc.vector.tensor_copy(wide[:].rearrange("r (c j) -> r c j", c=GRID_W),
                                      rows[:].unsqueeze(1).to_broadcast([NA_HEADS * RPB_R, GRID_W, PADW + 1])
                                      ).then_inc(s.wide, 1)

            @block.sync
            def _(sp):
                sp.wait_ge(s.zero, 1)
                mid = (PADW - RPB_C) // 2
                sp.dma_start(rows[:, mid:mid + RPB_C], rpb.rearrange("h r c -> (h r) c")).then_inc(s.rows, 16)
                sp.wait_ge(s.wide, 1)
                falling = wide[:, GRID_W - 1:GRID_W - 1 + GRID_W * PADW].rearrange("r (c j) -> r c j", c=GRID_W)
                sp.dma_start(k.bias.rearrange("c r k -> r c k"), falling[:, :, :GRID_W]).then_inc(s.bias, 16)
                sp.wait_ge(s.bias, 16)


class Piece:

    def __init__(self, q, runs, masks=(), bias=None):
        self.q, self.masks, self.bias = q, masks, bias
        self.tiles, self.mm, col = [], [], 0
        for key, n in runs:
            for c in range(0, n, P):
                self.tiles.append(((key + c) // P, min(P, n - c)))
            while n:
                m = min(n, 512 - col % 512)
                if self.mm and self.mm[-1][0] + self.mm[-1][2] == col and self.mm[-1][1] + self.mm[-1][2] == key and col % 512:
                    self.mm[-1] = (self.mm[-1][0], self.mm[-1][1], self.mm[-1][2] + m)
                else:
                    self.mm.append((col, key, m))
                col, key, n = col + m, key + m, n - m
        self.width = col


def window_pieces():
    out = []
    for q in range(LT):
        lo, hi = max(0, q - 1), min(LT, q + 2)
        masks = ([(0, CTX)] if q > 0 else []) + ([(1, CTX + (q + 1 - lo) * P)] if q < LT - 1 else [])
        out.append(Piece(q, [(SEQ, CTX), (lo * P, (hi - lo) * P)], masks=masks))
    return out + [Piece(q, [(SEQ, CTX)]) for q in range(LT, NT)]


def neighbour_pieces():
    out = []
    for q in range(LT):
        rows = [min(max(r - NA_ROWS // 2, 0), 2 * LT - NA_ROWS) for r in (2 * q, 2 * q + 1)]
        n = rows[1] - rows[0] + NA_ROWS
        out.append(Piece(q, [(SEQ, CTX), (rows[0] * GRID_W, n * GRID_W)],
                         bias=(rows[0] - 2 * q + NA_ROWS - 1, n, rows[1] > rows[0])))
    return out


def walk(eng, n, body):
    body(0, True, False)
    if n > 2:
        with eng.Fori(1, n - 1) as i:
            body(i, False, False)
    body(n - 1, False, True)


def attend(k, name, pieces, heads, load_head, parts, v_width, mix, mix_col, sink=None, bias=None):
    nc = k.nc
    V = 2 * len(pieces)
    NQ = len(pieces)
    PAIRS = heads // 2
    wide = max(p.width for p in pieces)
    names = "ld0 ld1 S msk mx mx2 ex es T evA evD pv ri ls o st0 st1 sinkc bm bl0 bl1 bd mk"
    with phase(nc, name, names) as s, ExitStack() as st:
        def sb(nm, shape, dt=F32):
            return st.enter_context(nc.sbuf_tensor(f"{name}_{nm}", shape, dt))
        rows = MLA_QK if parts == "three" else P
        q_sb = sb("q", [rows, 2, 2 if parts == "three" else 1, TOK], F32R)
        k_sb = sb("k", [rows, 2, 2, TOK], F32R)
        v_sb = sb("v", [P, 2, NT, v_width])
        e_sb = sb("e", [P, 2, wide])
        pt_sb = sb("pt", [P, 2, wide // P + 1, P])
        negmax, top = sb("nm", [P, 2]), sb("top", [P, 2])
        rowsum, esink = sb("ls", [P, 4]), sb("es", [P, 4])
        o_sb = sb("o", [P, 2, NQ, v_width])
        wmask = sb("wm", [P, 2, P]) if sink is not None else None
        sinks = sb("sinks", [P, heads]) if sink is not None else None
        b_sb = sb("b", [P, 2, 2 * NA_ROWS - 2, GRID_W]) if bias is not None else None
        cmask = sb("cm", [P, GRID_W]) if bias is not None else None
        rmask = sb("rm", [P, 2]) if bias is not None else None
        loads = load_head(None, None, None, None, None, None)
        OB = 6

        def scores(b):
            return k.ps[:, 3 * b:3 * b + 3].rearrange("p b c -> p (b c)")

        def nth(i, v):
            return i * V + v + 1

        def masked(i, v):
            has = [bool(u.masks or u.bias) for u in pieces] * 2
            return (i + v // V) * sum(has) + sum(has[:v % V + 1])

        with nc.Block() as block:
            @block.sync
            def _(sp):
                if sink is not None:
                    sp.dma_start(wmask[:], k.ins["wmask"]).then_inc(s.sinkc, 16)
                    sp.dma_start(sinks[:], sink.unsqueeze(0).broadcast_to([P, heads])).then_inc(s.sinkc, 16)
                if bias is not None:
                    sp.dma_start(cmask[:], k.ins["cmask"]).then_inc(s.bm, 16)
                    sp.dma_start(rmask[:], k.ins["rmask"]).then_inc(s.bm, 16)

                def fetch(i, p, free):
                    if free:
                        wait_then_store(sp, s.pv, (i - 1) * V + (p + 1) * NQ, s.mk)
                    load_head(sp, i, p, (q_sb[:, p], k_sb[:, p], v_sb[:, p]), None, s.ld0 if p == 0 else s.ld1)
                    if bias is not None:
                        if free:
                            wait_then_store(sp, s.msk, (i - 1) * V + (p + 1) * NQ, s.mk)
                        bias(sp, i, p, b_sb[:, p], s.bl0 if p == 0 else s.bl1)

                def pair(i, first, last):
                    if first:
                        fetch(0, 0, False)
                        fetch(0, 1, False)
                    for p in range(2):
                        if not last:
                            fetch(i + 1, p, True)
                        wait_then_store(sp, s.o, i * V + (p + 1) * NQ, s.mk)
                        dst = mix.rearrange("(t p) d -> p t d", p=P)[:, 0:NQ, bass.ds((i * 2 + p) * v_width + mix_col, v_width)]
                        sp.dma_start(dst, o_sb[:, p]).then_inc(s.st0 if p == 0 else s.st1, 16)
                walk(sp, PAIRS, pair)
                sp.wait_ge(s.st0, 16 * PAIRS)
                sp.wait_ge(s.st1, 16 * PAIRS)

            @block.tensor
            def _(pe):
                def score(i, v, free):
                    p, u = v // NQ % 2, pieces[v % NQ]
                    if v % NQ == 0:
                        pe.wait_ge(s.ld0 if p == 0 else s.ld1, (i + v // V) * 16 * loads + 16 * loads)
                    if free:
                        pe.wait_ge(s.evA, nth(i, v - 2))
                        pe.wait_ge(s.evD, nth(i, v - 2))
                    qs = slice(u.q * P, (u.q + 1) * P)
                    prods = ((0, 0), (0, 1), (1, 0)) if parts == "three" else ((0, 0), (0, 1))
                    for c, key, n in u.mm:
                        for x, (a, b) in enumerate(prods):
                            mm = pe.matmul(scores(v % 2)[:, c:c + n], q_sb[:, p, a, qs], k_sb[:, p, b, key:key + n],
                                           start=(x == 0), stop=(x == len(prods) - 1))
                    mm.then_inc(s.S, 1)

                def turn(i, v):
                    u = pieces[v % NQ]
                    pe.wait_ge(s.ex, nth(i, v))
                    for x, (_, n) in enumerate(u.tiles):
                        mm = pe.transpose(scores(v % 2)[0:n, x * P:(x + 1) * P], e_sb[:, v % 2, x * P:x * P + n], k.ident[:])
                    mm.then_inc(s.T, 1)

                def values(i, v, free):
                    p, u = v // NQ % 2, pieces[v % NQ]
                    pe.wait_ge(s.evA, nth(i, v))
                    pe.wait_ge(s.evD, nth(i, v))
                    if free:
                        pe.wait_ge(s.o, nth(i, v - 2))
                    for x, (t, n) in enumerate(u.tiles):
                        mm = pe.matmul(k.ps[:, OB + v % 2, 0:v_width], pt_sb[0:n, v % 2, x], v_sb[0:n, p, t],
                                       start=(x == 0), stop=(x == len(u.tiles) - 1))
                    mm.then_inc(s.pv, 1)

                def pair(i, first, last):
                    if first:
                        score(0, 0, False)
                    for v in range(V):
                        if not (last and v == V - 1):
                            score(i, v + 1, not (first and v < 1))
                        if not (first and v == 0):
                            values(i, v - 1, not (first and v < 3))
                        turn(i, v)
                walk(pe, PAIRS, pair)
                values(PAIRS - 1, V - 1, True)

            @block.scalar
            def _(act):
                def exps(i, v):
                    u = pieces[v % NQ]
                    b = v % 2
                    act.wait_ge(s.mx, nth(i, v))
                    nc.scalar.activation(e_sb[:, b, 0:u.width], scores(b)[:, 0:u.width], ACT.Exp,
                                         bias=negmax[:, b:b + 1], accum_out=rowsum[:, v % 4:v % 4 + 1]).then_inc(s.ex, 1)
                    if sink is not None:
                        hd = i * 2 + v // NQ
                        nc.scalar.activation(esink[:, v % 4:v % 4 + 1], sinks[:, bass.ds(hd, 1)], ACT.Exp,
                                             bias=negmax[:, b:b + 1]).then_inc(s.es, 1)

                def evacuate(i, v, free):
                    u, b = pieces[v % NQ], v % 2
                    act.wait_ge(s.T, nth(i, v))
                    if free:
                        act.wait_ge(s.pv, nth(i, v - 2))
                    if u.width <= 512:
                        nt = len(u.tiles)
                        ins = nc.scalar.copy(pt_sb[64:P, b, 0:nt], scores(b)[64:P, 0:nt * P].rearrange("p (t q) -> p t q", q=P))
                    else:
                        full = [x for x, (_, n) in enumerate(u.tiles) if n == P and x >= 4]
                        ins = nc.scalar.copy(pt_sb[:, b, 4:4 + len(full)],
                                             scores(b)[:, 512:512 + P * len(full)].rearrange("p (t q) -> p t q", q=P))
                        if u.tiles[-1][1] < P:
                            x = len(u.tiles) - 1
                            ins = nc.scalar.copy(pt_sb[0:64, b, x], scores(b)[0:64, x * P:(x + 1) * P])
                    ins.then_inc(s.evA, 1)

                if sink is not None:
                    act.wait_ge(s.sinkc, 32)

                def pair(i, first, last):
                    if first:
                        exps(0, 0)
                    for v in range(V):
                        evacuate(i, v, not (first and v < 2))
                        if not (last and v == V - 1):
                            exps(i, v + 1)
                walk(act, PAIRS, pair)

            @block.vector
            def _(dve):
                def maxima(i, v, free):
                    u, b = pieces[v % NQ], v % 2
                    p = v // NQ % 2
                    dve.wait_ge(s.S, nth(i, v))
                    if bias is not None and v % NQ == 0:
                        dve.wait_ge(s.bl0 if p == 0 else s.bl1, (i + v // V) * 32 + 32)
                        nc.vector.tensor_tensor(b_sb[:, p], b_sb[:, p], cmask[:].unsqueeze(1).broadcast_to([P, 2 * NA_ROWS - 2, GRID_W]),
                                                ALU.add).then_inc(s.bd, 1)
                        dve.wait_ge(s.bd, (i + v // V) * 2 + p + 1)
                    if bias is not None:
                        e0, n, edge = u.bias
                        local = scores(b)[:, CTX:CTX + n * GRID_W].rearrange("p (e c) -> p e c", c=GRID_W)
                        if edge:
                            for e, m in ((0, 0), (n - 1, 1)):
                                nc.vector.scalar_tensor_tensor(out=local[:, e], in0=local[:, e], scalar=rmask[:, m:m + 1],
                                                               in1=b_sb[:, p, e0 - 1 + e], op0=ALU.add, op1=ALU.add)
                            ins = nc.vector.tensor_tensor(local[:, 1:n - 1], local[:, 1:n - 1], b_sb[:, p, e0:e0 + n - 2], ALU.add)
                        else:
                            ins = nc.vector.tensor_tensor(local, local, b_sb[:, p, e0 - 1:e0 - 1 + n], ALU.add)
                        ins.then_inc(s.msk, 1)
                        dve.wait_ge(s.msk, masked(i, v))
                    if sink is not None:
                        for m, c in u.masks:
                            ins = nc.vector.tensor_tensor(scores(b)[:, c:c + P], scores(b)[:, c:c + P], wmask[:, m], ALU.add)
                        if u.masks:
                            ins.then_inc(s.msk, 1)
                            dve.wait_ge(s.msk, masked(i, v))
                        nc.vector.tensor_reduce(top[:, b:b + 1], scores(b)[:, 0:u.width], AX.X, ALU.max).then_inc(s.mx2, 1)
                        dve.wait_ge(s.mx2, nth(i, v))
                        hd = i * 2 + v // NQ
                        nc.vector.tensor_scalar(negmax[:, b:b + 1], top[:, b:b + 1], sinks[:, bass.ds(hd, 1)], -1.0,
                                                ALU.max, ALU.mult).then_inc(s.mx, 1)
                    else:
                        nc.vector.tensor_reduce(negmax[:, b:b + 1], scores(b)[:, 0:u.width], AX.X, ALU.max,
                                                negate=True).then_inc(s.mx, 1)

                def evacuate(i, v, free):
                    u, b = pieces[v % NQ], v % 2
                    dve.wait_ge(s.T, nth(i, v))
                    if free:
                        dve.wait_ge(s.pv, nth(i, v - 2))
                    if u.width <= 512:
                        nt = len(u.tiles)
                        ins = nc.vector.tensor_copy(pt_sb[0:64, b, 0:nt], scores(b)[0:64, 0:nt * P].rearrange("p (t q) -> p t q", q=P))
                    else:
                        ins = nc.vector.tensor_copy(pt_sb[:, b, 0:4], scores(b)[:, 0:512].rearrange("p (t q) -> p t q", q=P))
                    ins.then_inc(s.evD, 1)

                def result(i, v, free):
                    b, p, r = v % 2, v // NQ % 2, v % 4
                    me = nth(i, v)
                    if sink is not None:
                        dve.wait_ge(s.es, me)
                        nc.vector.tensor_tensor(rowsum[:, r:r + 1], rowsum[:, r:r + 1], esink[:, r:r + 1], ALU.add).then_inc(s.ls, 1)
                        dve.wait_ge(s.ls, me)
                    dve.wait_ge(s.ex, me)
                    nc.vector.reciprocal(rowsum[:, r:r + 1], rowsum[:, r:r + 1]).then_inc(s.ri, 1)
                    dve.wait_ge(s.ri, me)
                    dve.wait_ge(s.pv, me)
                    if free and v % NQ == 0:
                        dve.wait_ge(s.st0 if p == 0 else s.st1, (i + v // V) * 16)
                    nc.vector.tensor_scalar(o_sb[:, p, v % NQ], k.ps[:, OB + b, 0:v_width], rowsum[:, r:r + 1], None,
                                            ALU.mult).then_inc(s.o, 1)

                if sink is not None:
                    dve.wait_ge(s.sinkc, 32)
                if bias is not None:
                    dve.wait_ge(s.bm, 32)

                def pair(i, first, last):
                    if first:
                        maxima(0, 0, False)
                    for v in range(V):
                        if not (last and v == V - 1):
                            maxima(i, v + 1, True)
                        if not (first and v == 0):
                            result(i, v - 1, not first)
                        evacuate(i, v, not (first and v < 2))
                walk(dve, PAIRS, pair)
                result(PAIRS - 1, V - 1, True)


def stacked_loader(qk, q_base, k_index, v_dram, v_index, v_width):
    def load(sp, i, p, places, _, sem):
        if sp is None:
            return 6
        q_sb, k_sb, v_sb = places
        h, kh, vh = i * 2 + p, k_index(i, p), v_index(i, p)
        one = lambda x: qk[bass.ds(x, 1)].squeeze(0)
        sp.dma_start(f32(q_sb[:, 0]), one(h + q_base)).then_inc(sem, 16)
        for part in range(2):
            for half in range(2):
                sp.dma_start(f32(k_sb[half * HD:(half + 1) * HD, part]), one(kh)[part * HD:(part + 1) * HD]).then_inc(sem, 16)
        sp.dma_start(v_sb, v_dram.rearrange("(t p) d -> p t d", p=P)[:, :, bass.ds(vh * v_width, v_width)]).then_inc(sem, 16)
    return load


def parts_loader(k):
    def load(sp, i, p, places, _, sem):
        if sp is None:
            return 3
        q_sb, k_sb, v_sb = places
        h = i * 2 + p
        one = lambda x: k.qkC[bass.ds(x, 1)].squeeze(0).rearrange("a r q -> r a q")
        sp.dma_start(f32(q_sb), one(h)).then_inc(sem, 16)
        sp.dma_start(f32(k_sb), one(h + MLA_HEADS)).then_inc(sem, 16)
        sp.dma_start(v_sb, k.vC.rearrange("(t p) d -> p t d", p=P)[:, :, bass.ds(h * MLA_V, MLA_V)]).then_inc(sem, 16)
    return load


def bias_loader(k):
    def load(sp, i, p, place, sem):
        for half in range(2):
            first_row = (i * 2 + p) * RPB_R + 1 - half
            sp.dma_start(place[half * GRID_W:(half + 1) * GRID_W],
                         k.bias[:, bass.ds(first_row, 2 * NA_ROWS - 2)]).then_inc(sem, 16)
    return load


def attend_diff(k, name, ins):
    nc = k.nc
    pieces = [Piece(q, [(0, TOK)]) for q in range(LT)] + [Piece(q, [(SEQ, CTX)]) for q in range(LT, NT)]
    NQ, V, PAIRS, DV = NT, 2 * NT, DIFF_HEADS // 2, 2 * HD
    names = "ld0 ld1 lam lp lr le l1 nl S mx ex r1 c mix T evA evD pv r0 o st0 st1"
    with phase(nc, name, names) as s, ExitStack() as st:
        def sb(nm, shape, dt=F32):
            return st.enter_context(nc.sbuf_tensor(f"{name}_{nm}", shape, dt))
        q_sb = sb("q", [P, 2, 2, TOK], F32R)
        k_sb = sb("k", [P, 2, 2, 2, TOK], F32R)
        v_sb = sb("v", [P, 2, NT, DV])
        e_sb = sb("e", [P, 2, 2, TOK])
        pt_sb = sb("pt", [P, 2, NT, P])
        negmax = sb("nm", [P, 2, 2])
        rowsum = sb("ls", [P, 4, 2])
        r1, coef, r0 = sb("r1", [P, 2]), sb("c", [P, 2]), sb("r0", [P, 2])
        o_sb = sb("o", [P, 2, NQ, DV])
        lam4, lprod, lsum, nlam = sb("lam4", [P, 4, HD]), sb("lprod", [P, 2, HD]), sb("lsum", [P, 2]), sb("nlam", [P, 1])
        OB = 6

        def scores(b):
            return k.ps[:, 3 * b:3 * b + 3].rearrange("p b c -> p (b c)")

        def nth(i, v):
            return i * V + v + 1

        def map_nth(i, v, m):
            return (i * V + v) * 2 + m + 1

        with nc.Block() as block:
            @block.sync
            def _(sp):
                sp.dma_start(lam4[:], ins["diff_lam"][0].unsqueeze(0).broadcast_to([P, 4, HD])).then_inc(s.lam, 16)

                def fetch(i, p):
                    sem = s.ld0 if p == 0 else s.ld1
                    hd = i * 2 + p
                    for m in range(2):
                        sp.dma_start(f32(q_sb[:, p, m]), k.qkA[hd * 2 + m]).then_inc(sem, 16)
                        for part in range(2):
                            for half in range(2):
                                sp.dma_start(f32(k_sb[half * HD:(half + 1) * HD, p, m, part]),
                                             k.qkA[8 + hd * 2 + m, part * HD:(part + 1) * HD]).then_inc(sem, 16)
                    sp.dma_start(v_sb[:, p], k.vA.rearrange("(t p) d -> p t d", p=P)[:, :, hd * DV:(hd + 1) * DV]).then_inc(sem, 16)

                fetch(0, 0)
                fetch(0, 1)
                for i in range(PAIRS):
                    for p in range(2):
                        sp.wait_ge(s.o, i * V + (p + 1) * NQ)
                        if i + 1 < PAIRS:
                            fetch(i + 1, p)
                        dst = k.mix[0].rearrange("(t p) d -> p t d", p=P)[:, :, (i * 2 + p) * DV:(i * 2 + p + 1) * DV]
                        sp.dma_start(dst, o_sb[:, p]).then_inc(s.st0 if p == 0 else s.st1, 16)
                sp.wait_ge(s.st0, 16 * PAIRS)
                sp.wait_ge(s.st1, 16 * PAIRS)

            @block.tensor
            def _(pe):
                def score(i, v, m):
                    i, v = i + v // V, v % V
                    p, u = v // NQ, pieces[v % NQ]
                    if v % NQ == 0 and m == 0:
                        pe.wait_ge(s.ld0 if p == 0 else s.ld1, (i + 1) * 16 * 11)
                    if i or v:
                        if m == 0:
                            pe.wait_ge(s.ex, map_nth(i, v - 1, 0))
                        else:
                            pe.wait_ge(s.evA, nth(i, v - 1))
                            pe.wait_ge(s.evD, nth(i, v - 1))
                    for c, key, n in u.mm:
                        for x in range(2):
                            mm = pe.matmul(scores(m)[:, c:c + n], q_sb[:, p, m, u.q * P:(u.q + 1) * P],
                                           k_sb[:, p, m, x, key:key + n], start=(x == 0), stop=(x == 1))
                    mm.then_inc(s.S, 1)

                def turn(i, v):
                    u = pieces[v % NQ]
                    pe.wait_ge(s.mix, nth(i, v))
                    for x in range(len(u.tiles)):
                        mm = pe.transpose(scores(1)[:, x * P:(x + 1) * P], e_sb[:, v % 2, 0, x * P:(x + 1) * P], k.ident[:])
                    mm.then_inc(s.T, 1)

                def values(i, v):
                    u = pieces[v % NQ]
                    pe.wait_ge(s.evA, nth(i, v))
                    pe.wait_ge(s.evD, nth(i, v))
                    if i or v >= 2:
                        pe.wait_ge(s.o, nth(i, v - 2))
                    for x, (t, n) in enumerate(u.tiles):
                        mm = pe.matmul(k.ps[:, OB + v % 2, 0:DV], pt_sb[:, v % 2, x], v_sb[:, v // NQ, t],
                                       start=(x == 0), stop=(x == len(u.tiles) - 1))
                    mm.then_inc(s.pv, 1)

                score(0, 0, 0)
                score(0, 0, 1)
                for i in range(PAIRS):
                    for v in range(V):
                        more = (i, v) != (PAIRS - 1, V - 1)
                        if more:
                            score(i, v + 1, 0)
                        turn(i, v)
                        if more:
                            score(i, v + 1, 1)
                        values(i, v)

            @block.scalar
            def _(act):
                act.wait_ge(s.lr, 1)
                nc.scalar.activation(lsum[:], lsum[:], ACT.Exp).then_inc(s.le, 1)

                def exps(i, v, m):
                    i, v = i + v // V, v % V
                    act.wait_ge(s.mx, map_nth(i, v, m))
                    w = pieces[v % NQ].width
                    nc.scalar.activation(e_sb[:, v % 2, m, 0:w], scores(m)[:, 0:w], ACT.Exp, bias=negmax[:, v % 2, m:m + 1],
                                         accum_out=rowsum[:, v % 4, m:m + 1]).then_inc(s.ex, 1)

                def evacuate(i, v):
                    u, b = pieces[v % NQ], v % 2
                    act.wait_ge(s.T, nth(i, v))
                    if i or v >= 2:
                        act.wait_ge(s.pv, nth(i, v - 2))
                    nt = len(u.tiles)
                    if nt <= 4:
                        ins = nc.scalar.copy(pt_sb[64:P, b, 0:nt], scores(1)[64:P, 0:nt * P].rearrange("p (t q) -> p t q", q=P))
                    else:
                        ins = nc.scalar.copy(pt_sb[:, b, 4:nt], scores(1)[:, 512:nt * P].rearrange("p (t q) -> p t q", q=P))
                    ins.then_inc(s.evA, 1)

                exps(0, 0, 0)
                exps(0, 0, 1)
                for i in range(PAIRS):
                    for v in range(V):
                        evacuate(i, v)
                        if (i, v) != (PAIRS - 1, V - 1):
                            exps(i, v + 1, 0)
                            exps(i, v + 1, 1)

            @block.vector
            def _(dve):
                dve.wait_ge(s.lam, 16)
                nc.vector.tensor_tensor(lprod[:], lam4[:, 0:4:2], lam4[:, 1:4:2], ALU.mult).then_inc(s.lp, 1)
                dve.wait_ge(s.lp, 1)
                nc.vector.tensor_reduce(lsum[:], lprod[:], AX.X, ALU.add).then_inc(s.lr, 1)
                dve.wait_ge(s.le, 1)
                nc.vector.tensor_tensor(nlam[:], lsum[:, 1:2], lsum[:, 0:1], ALU.subtract).then_inc(s.l1, 1)
                dve.wait_ge(s.l1, 1)
                nc.vector.tensor_scalar(nlam[:], nlam[:], -LAM_INIT, None, ALU.add).then_inc(s.nl, 1)
                dve.wait_ge(s.nl, 1)

                def maxima(i, v, m):
                    i, v = i + v // V, v % V
                    dve.wait_ge(s.S, map_nth(i, v, m))
                    nc.vector.tensor_reduce(negmax[:, v % 2, m:m + 1], scores(m)[:, 0:pieces[v % NQ].width], AX.X, ALU.max,
                                            negate=True).then_inc(s.mx, 1)

                def mixed(i, v):
                    b, w = v % 2, pieces[v % NQ].width
                    dve.wait_ge(s.ex, map_nth(i, v, 1))
                    nc.vector.reciprocal(r1[:, b:b + 1], rowsum[:, v % 4, 1:2]).then_inc(s.r1, 1)
                    dve.wait_ge(s.r1, nth(i, v))
                    nc.vector.tensor_scalar(coef[:, b:b + 1], rowsum[:, v % 4, 0:1], r1[:, b:b + 1], nlam[:, 0:1],
                                            ALU.mult, ALU.mult).then_inc(s.c, 1)
                    dve.wait_ge(s.c, nth(i, v))
                    nc.vector.scalar_tensor_tensor(out=e_sb[:, b, 0, 0:w], in0=e_sb[:, b, 1, 0:w], scalar=coef[:, b:b + 1],
                                                   in1=e_sb[:, b, 0, 0:w], op0=ALU.mult, op1=ALU.add).then_inc(s.mix, 1)

                def evacuate(i, v):
                    u, b = pieces[v % NQ], v % 2
                    dve.wait_ge(s.T, nth(i, v))
                    if i or v >= 2:
                        dve.wait_ge(s.pv, nth(i, v - 2))
                    nt = len(u.tiles)
                    if nt <= 4:
                        ins = nc.vector.tensor_copy(pt_sb[0:64, b, 0:nt], scores(1)[0:64, 0:nt * P].rearrange("p (t q) -> p t q", q=P))
                    else:
                        ins = nc.vector.tensor_copy(pt_sb[:, b, 0:4], scores(1)[:, 0:512].rearrange("p (t q) -> p t q", q=P))
                    ins.then_inc(s.evD, 1)

                def result(i, v):
                    b, p = v % 2, v // NQ
                    nc.vector.reciprocal(r0[:, b:b + 1], rowsum[:, v % 4, 0:1]).then_inc(s.r0, 1)
                    dve.wait_ge(s.r0, nth(i, v))
                    dve.wait_ge(s.pv, nth(i, v))
                    if i and v % NQ == 0:
                        dve.wait_ge(s.st0 if p == 0 else s.st1, i * 16)
                    nc.vector.tensor_scalar(o_sb[:, p, v % NQ], k.ps[:, OB + b, 0:DV], r0[:, b:b + 1], None,
                                            ALU.mult).then_inc(s.o, 1)

                maxima(0, 0, 0)
                maxima(0, 0, 1)
                for i in range(PAIRS):
                    for v in range(V):
                        more = (i, v) != (PAIRS - 1, V - 1)
                        mixed(i, v)
                        if more:
                            maxima(i, v + 1, 0)
                        evacuate(i, v)
                        if v:
                            result(i, v - 1)
                        elif i:
                            result(i - 1, V - 1)
                        if more:
                            maxima(i, v + 1, 1)
                result(PAIRS - 1, V - 1)


def out_project(k, name, layer, n_tok, w_out, subln=None):
    nc = k.nc
    nt = n_tok // P
    chunks = token_chunks(n_tok)
    SB = len(chunks)
    names = "in0 in1 g sqa red root ri ya yb T hi lo wr0 wr1 whi wlo mm x g2"
    with phase(nc, name, names) as s, ExitStack() as st:
        def sb(nm, shape, dt=F32):
            return st.enter_context(nc.sbuf_tensor(f"{name}_{nm}", shape, dt))
        rows = sb("rows", [P, 2, D_MODEL])
        oh, ol = sb("oh", [P, KT, n_tok], F32R), sb("ol", [P, KT, n_tok], F32R)
        raw = sb("raw", [P, 2, KT, P])
        wh, wl = sb("wh", [P, 2, KT, P], F32R), sb("wl", [P, 2, KT, P], F32R)
        if subln is not None:
            sq, rs, gain = sb("sq", [P, 512]), sb("rs", [P, 2, DIFF_HEADS]), sb("gain", [P, P])
        w_dram = w_out.rearrange("(f p) (n c) -> n p f c", p=P, c=P)

        with nc.Block() as block:
            @block.sync
            def _(sp):
                if subln is not None:
                    sp.dma_start(gain[:], subln.unsqueeze(0).broadcast_to([P, P])).then_inc(s.g, 16)
                for t in range(nt):
                    if t >= 2:
                        sp.wait_ge(s.T, t - 1)
                    sp.dma_start(rows[:, t % 2], k.mix[layer][t * P:(t + 1) * P]).then_inc(s.in0 if t % 2 == 0 else s.in1, 16)

                def pair(i, first, last):
                    for p in range(2):
                        if not first:
                            wait_then_store(sp, s.wlo, i * 2 + p - 1, s.g2)
                        sp.dma_start(raw[:, p], w_dram[bass.ds(i * 2 + p, 1)].squeeze(0)).then_inc(s.wr0 if p == 0 else s.wr1, 16)
                walk(sp, KT // 2, pair)

            @block.tensor
            def _(pe):
                for t in range(nt):
                    if subln is None:
                        pe.wait_ge(s.in0 if t % 2 == 0 else s.in1, 16 * (t // 2 + 1))
                    else:
                        pe.wait_ge(s.yb, t + 1)
                    if t >= 3:
                        pe.wait_ge(s.lo, t - 2)
                    for f in range(KT):
                        mm = pe.transpose(k.ps[:, 2 * (t % 3) + f // 4, (f % 4) * P:(f % 4 + 1) * P],
                                          rows[:, t % 2, f * P:(f + 1) * P], k.ident[:])
                    mm.then_inc(s.T, 1)

                def pair(i, first, last):
                    for p in range(2):
                        if first and p == 0:
                            pe.wait_ge(s.lo, nt)
                        pe.wait_ge(s.wlo, i * 2 + p + 1)
                        if not first:
                            pe.wait_ge(s.x, i * 2 + p - 1)
                        for f in range(KT):
                            for x, (w, o) in enumerate(((wh, oh), (wh, ol), (wl, oh))):
                                for c, (c0, n) in enumerate(chunks):
                                    mm = pe.matmul(k.ps[:, SB * p + c, 0:n], w[:, p, f], o[:, f, c0:c0 + n],
                                                   start=(f == 0 and x == 0), stop=(f == KT - 1 and x == 2))
                        mm.then_inc(s.mm, 1)
                walk(pe, KT // 2, pair)

            @block.scalar
            def _(act):
                for t in range(nt):
                    if subln is not None:
                        act.wait_ge(s.in0 if t % 2 == 0 else s.in1, 16 * (t // 2 + 1))
                        if t:
                            act.wait_ge(s.red, t)
                        nc.scalar.activation(sq[:], rows[:, t % 2, 0:512], ACT.Square).then_inc(s.sqa, 1)
                        act.wait_ge(s.red, t + 1)
                        nc.scalar.activation(rs[:, t % 2], rs[:, t % 2], ACT.Sqrt, bias=k.eps[:], scale=1.0 / P).then_inc(s.root, 1)
                    act.wait_ge(s.T, t + 1)
                    nc.scalar.copy(oh[:, :, t * P:(t + 1) * P],
                                   k.ps[:, 2 * (t % 3):2 * (t % 3) + 2].rearrange("p b (f q) -> p (b f) q", q=P)).then_inc(s.hi, 1)

                def pair(i, first, last):
                    for p in range(2):
                        act.wait_ge(s.wr0 if p == 0 else s.wr1, i * 16 + 16)
                        if not first:
                            act.wait_ge(s.mm, i * 2 + p - 1)
                        nc.scalar.copy(wh[:, p], raw[:, p]).then_inc(s.whi, 1)
                walk(act, KT // 2, pair)

            @block.vector
            def _(dve):
                if subln is not None:
                    dve.wait_ge(s.g, 16)
                    nc.vector.tensor_scalar(gain[:], gain[:], 1.0 - LAM_INIT, None, ALU.mult).then_inc(s.ya, 1)
                    dve.wait_ge(s.ya, 1)

                def norm(t):
                    heads = lambda ap: ap.rearrange("p (h d) -> p h d", d=P)
                    r = rows[:, t % 2, 0:512]
                    dve.wait_ge(s.sqa, t + 1)
                    nc.vector.tensor_reduce(rs[:, t % 2], heads(sq[:]), AX.X, ALU.add).then_inc(s.red, 1)
                    dve.wait_ge(s.root, t + 1)
                    nc.vector.reciprocal(rs[:, t % 2], rs[:, t % 2]).then_inc(s.ri, 1)
                    dve.wait_ge(s.ri, t + 1)
                    nc.vector.tensor_tensor(heads(r), heads(r), rs[:, t % 2].unsqueeze(2).broadcast_to([P, DIFF_HEADS, P]),
                                            ALU.mult).then_inc(s.ya, 1)
                    dve.wait_ge(s.ya, t + 2)
                    nc.vector.tensor_tensor(heads(r), heads(r), gain[:].unsqueeze(1).broadcast_to([P, DIFF_HEADS, P]),
                                            ALU.mult).then_inc(s.yb, 1)

                def lo(t):
                    dve.wait_ge(s.hi, t + 1)
                    q = slice(t * P, (t + 1) * P)
                    nc.vector.tensor_tensor(ol[:, :, q], k.ps[:, 2 * (t % 3):2 * (t % 3) + 2].rearrange("p b (f q) -> p (b f) q", q=P),
                                            f32(oh[:, :, q]), ALU.subtract).then_inc(s.lo, 1)

                for t in range(nt):
                    if subln is not None:
                        norm(t)
                    if t:
                        lo(t - 1)
                lo(nt - 1)

                def cut(i, p):
                    dve.wait_ge(s.whi, i * 2 + p + 1)
                    nc.vector.tensor_tensor(wl[:, p], raw[:, p], f32(wh[:, p]), ALU.subtract).then_inc(s.wlo, 1)

                def add(i, p):
                    dve.wait_ge(s.mm, i * 2 + p + 1)
                    add_gated(k, dve, layer, 2, i * 2 + p, SB * p, n_tok).then_inc(s.x, 1)

                def pair(i, first, last):
                    if first:
                        cut(0, 0)
                    cut(i, 1)
                    add(i, 0)
                    if not last:
                        cut(i + 1, 0)
                    add(i, 1)
                walk(dve, KT // 2, pair)


def add_gated(k, dve, layer, gate, n, bank, n_tok):
    for w, a, b in ((0, 0, SEQ), (1, SEQ, n_tok)):
        if b > a:
            x = k.xT[:, bass.ds(n, 1), a:b].squeeze(1)
            ps = k.ps[:, bank:bank + (n_tok + 511) // 512].rearrange("p b c -> p (b c)")[:, a:b]
            ins = k.nc.vector.scalar_tensor_tensor(out=x, in0=ps, scalar=k.mods[:, layer, gate, bass.ds(n, 1), w], in1=x,
                                                   op0=ALU.mult, op1=ALU.add)
    return ins


def mlp(k, name, layer, n_tok, w1, w2):
    nc = k.nc
    chunks = token_chunks(n_tok)
    SB = len(chunks)
    C, F, U = FF // FFC, FFC // P, FFC // P + KT
    names = "f fm hh h wr0 wr1 whi wlo mm relu sq gh g x tick"
    with phase(nc, name, names) as s, ExitStack() as st:
        def sb(nm, shape, dt=F32):
            return st.enter_context(nc.sbuf_tensor(f"{name}_{nm}", shape, dt))
        hh, hl = sb("hh", [P, KT, n_tok], F32R), sb("hl", [P, KT, n_tok], F32R)
        gh, gl = sb("gh", [P, F, n_tok], F32R), sb("gl", [P, F, n_tok], F32R)
        g = sb("g", [P, n_tok])
        raw = sb("raw", [P, 2, KT, P])
        w1h, w1l = sb("w1h", [P, 2, KT, P], F32R), sb("w1l", [P, 2, KT, P], F32R)
        w2h, w2l = sb("w2h", [P, 2, F, P], F32R), sb("w2l", [P, 2, F, P], F32R)
        w1_dram = w1.rearrange("(f p) (c n q) -> c n p f q", p=P, n=F, q=P)
        w2_dram = w2.rearrange("(c f p) (n q) -> c n p f q", f=F, p=P, q=P)

        def nth(c, e):
            return c * U + e + 1

        def places(e):
            return (w1h, w1l, KT) if e % U < F else (w2h, w2l, F)

        def waits_for(e):
            return e - 2 if (e >= F + 2 or 2 <= e < F) else e - U + (F - 2 if e < F else KT - 2)

        with nc.Block() as block:
            @block.sync
            def _(sp):
                def chunk(c, first, last):
                    for e in range(U):
                        if not (first and e < 2):
                            wait_then_store(sp, s.wlo, nth(c, e - 2), s.tick)
                        src = w1_dram[bass.ds(c, 1), e].squeeze(0) if e < F else w2_dram[bass.ds(c, 1), e - F].squeeze(0)
                        sp.dma_start(raw[:, e % 2, 0:places(e)[2]], src).then_inc(s.wr0 if e % 2 == 0 else s.wr1, 16)
                walk(sp, C, chunk)

            @block.tensor
            def _(pe):
                def unit(c, e, first):
                    pe.wait_ge(s.wlo, nth(c, e))
                    if not (first and e < 2):
                        b = (e - 2) % U
                        n = c - 1 if e < 2 else c
                        if b < F:
                            pe.wait_ge(s.relu, n * F + b + 1)
                        else:
                            pe.wait_ge(s.x, n * KT + b - F + 1)
                    wh, wl, nf = places(e)
                    mh, ml = (hh, hl) if e < F else (gh, gl)
                    for f in range(nf):
                        if first and e == 0:
                            pe.wait_ge(s.h, f + 1)
                        if e == F:
                            pe.wait_ge(s.g, c * F + f + 1)
                        for x, (w, m) in enumerate(((wh, mh), (wh, ml), (wl, mh))):
                            for b, (c0, n) in enumerate(chunks):
                                mm = pe.matmul(k.ps[:, SB * (e % 2) + b, 0:n], w[:, e % 2, f], m[:, f, c0:c0 + n],
                                               start=(f == 0 and x == 0), stop=(f == nf - 1 and x == 2))
                    mm.then_inc(s.mm, 1)

                def chunk(c, first, last):
                    for e in range(U):
                        unit(c, e, first)
                walk(pe, C, chunk)

            @block.scalar
            def _(act):
                def cut(c, e, first):
                    wh, _, nf = places(e)
                    act.wait_ge(s.wr0 if e % 2 == 0 else s.wr1, c * (8 * U) + (e // 2 + 1) * 16)
                    if waits_for(e) >= 0 or not first:
                        act.wait_ge(s.mm, nth(c, waits_for(e)))
                    nc.scalar.copy(wh[:, e % 2], raw[:, e % 2, 0:nf]).then_inc(s.whi, 1)

                cut(0, 0, True)
                for f in range(KT):
                    act.wait_ge(s.f, f + 1)
                    for w, a, b in ((0, 0, SEQ), (1, SEQ, n_tok)):
                        if b > a:
                            ins = nc.scalar.activation(g[:, a:b], g[:, a:b], ACT.Identity, scale=k.mods[:, layer, 4, f, w:w + 1],
                                                       bias=k.mods[:, layer, 3, f, w:w + 1])
                    ins.then_inc(s.fm, 1)

                def chunk(c, first, last):
                    for e in range(U):
                        if e + 1 < U:
                            cut(c, e + 1, first)
                        elif not last:
                            cut(c + 1, 0, False)
                        if e < F:
                            act.wait_ge(s.mm, nth(c, e))
                            if not (first and e == 0):
                                act.wait_ge(s.g, c * F + e)
                            nc.scalar.activation(g[:], k.ps[:, SB * (e % 2):SB * (e % 2) + SB].rearrange("p b c -> p (b c)")[:, 0:n_tok],
                                                 ACT.Relu).then_inc(s.relu, 1)
                walk(act, C, chunk)

            @block.vector
            def _(dve):
                def cut(c, e):
                    wh, wl, nf = places(e)
                    dve.wait_ge(s.whi, nth(c, e))
                    nc.vector.tensor_tensor(wl[:, e % 2], raw[:, e % 2, 0:nf], f32(wh[:, e % 2]), ALU.subtract).then_inc(s.wlo, 1)

                cut(0, 0)
                for f in range(KT):
                    if f:
                        dve.wait_ge(s.h, f)
                    nc.vector.tensor_tensor(g[:], k.xT[:, f, 0:n_tok], k.rstd[:, 0:n_tok], ALU.mult).then_inc(s.f, 1)
                    dve.wait_ge(s.fm, f + 1)
                    nc.vector.tensor_copy(hh[:, f], g[:]).then_inc(s.hh, 1)
                    dve.wait_ge(s.hh, f + 1)
                    nc.vector.tensor_tensor(hl[:, f], g[:], f32(hh[:, f]), ALU.subtract).then_inc(s.h, 1)

                def chunk(c, first, last):
                    for e in range(U):
                        if e + 1 < U:
                            cut(c, e + 1)
                        elif not last:
                            cut(c + 1, 0)
                        if e < F:
                            me = c * F + e + 1
                            dve.wait_ge(s.relu, me)
                            nc.vector.tensor_tensor(g[:], g[:], g[:], ALU.mult).then_inc(s.sq, 1)
                            dve.wait_ge(s.sq, me)
                            nc.vector.tensor_copy(gh[:, e], g[:]).then_inc(s.gh, 1)
                            dve.wait_ge(s.gh, me)
                            nc.vector.tensor_tensor(gl[:, e], g[:], f32(gh[:, e]), ALU.subtract).then_inc(s.g, 1)
                        else:
                            dve.wait_ge(s.mm, nth(c, e))
                            add_gated(k, dve, layer, 5, e - F, SB * (e % 2), n_tok).then_inc(s.x, 1)
                walk(dve, C, chunk)


def closing(k):
    nc = k.nc
    with phase(nc, "close", "T cp0 cp1 st0 st1") as s, ExitStack() as st:
        rows = st.enter_context(nc.sbuf_tensor("out_rows", [P, 2, D_MODEL], F32))
        out = k.out.rearrange("b (t p) d -> (b t) p d", p=P)
        with nc.Block() as block:
            @block.tensor
            def _(pe):
                for t in range(LT):
                    if t >= 2:
                        pe.wait_ge(s.cp0, t - 1)
                        pe.wait_ge(s.cp1, t - 1)
                    for f in range(KT):
                        mm = pe.transpose(k.ps[:, 2 * (t % 2) + f // 4, (f % 4) * P:(f % 4 + 1) * P],
                                          k.xT[:, f, t * P:(t + 1) * P], k.ident[:])
                    mm.then_inc(s.T, 1)

            @block.scalar
            def _(act):
                for t in range(LT):
                    act.wait_ge(s.T, t + 1)
                    if t >= 2:
                        act.wait_ge(s.st0 if t % 2 == 0 else s.st1, 16 * (t // 2))
                    nc.scalar.copy(rows[:, t % 2, 0:512], k.ps[:, 2 * (t % 2)]).then_inc(s.cp0, 1)

            @block.vector
            def _(dve):
                for t in range(LT):
                    dve.wait_ge(s.T, t + 1)
                    if t >= 2:
                        dve.wait_ge(s.st0 if t % 2 == 0 else s.st1, 16 * (t // 2))
                    nc.vector.tensor_copy(rows[:, t % 2, 512:1024], k.ps[:, 2 * (t % 2) + 1]).then_inc(s.cp1, 1)

            @block.sync
            def _(sp):
                for t in range(LT):
                    sp.wait_ge(s.cp0, t + 1)
                    sp.wait_ge(s.cp1, t + 1)
                    sp.dma_start(out[t], rows[:, t % 2]).then_inc(s.st0 if t % 2 == 0 else s.st1, 16)
                sp.wait_ge(s.st0, 16 * LT // 2)
                sp.wait_ge(s.st1, 16 * LT // 2)


def trunk(nc, out, **ins):
    with ExitStack() as st:
        k = Core(nc, st, ins, out)
        ev = ins["ev_w_in"][0]
        opening(k)
        norm_stats(k, "n0", TOK)
        project(k, "pa", 0, ev, 0, 1024, [
            Unit(0, 512, 8, ins["diff_q_g"][0], HD ** -0.5, True, k.qkA, 0),
            Unit(512, 512, 8, ins["diff_k_g"][0], 1.0, True, k.qkA, 8)])
        project(k, "pb", 0, ev, 1024, 1280, [
            Unit(512, 512, 8, ins["swa_q_g"][0], HD ** -0.5, True, k.qkB, 0),
            Unit(1024, 256, 2, ins["swa_k_g"][0], 1.0, True, k.qkB, 8, v=128, v_dst=k.vB),
            Unit(0, 512, v=512, v_dst=k.vA)])
        attend(k, "ab", window_pieces(), 8,
               stacked_loader(k.qkB, 0, lambda i, p: 8 + i // 2, k.vB, lambda i, p: i // 2, HD),
               "two", HD, k.mix[0], 512, sink=ins["swa_sink"][0])
        attend_diff(k, "aa", ins)
        out_project(k, "o0", 0, TOK, ins["w_out"][0], subln=ins["diff_subln_g"][0])
        norm_stats(k, "n1", TOK)
        mlp(k, "m0", 0, TOK, ins["mlp_w1"][0], ins["mlp_w2"][0])
        od = ins["od_w_in"][0]
        bias_pad(k, ins["na_rpb"][0])
        norm_stats(k, "n2", TOK)
        project_low_rank(k, "pq", 1, od, 0, MLA_QL, MLA_QL, ins["mla_qa_g"][0], ins["mla_wq_up"][0],
                         ins["mla_q_g"][0], MLA_QK ** -0.5, 0, False)
        project_low_rank(k, "pk", 1, od, MLA_QL, MLA_KVL + MLA_ROPE, MLA_KVL, ins["mla_kva_g"][0], ins["mla_wkv_up"][0],
                         ins["mla_k_g"][0], 1.0, MLA_HEADS, True)
        project(k, "pd", 1, od, MLA_QL + MLA_KVL + MLA_ROPE, 1536, [
            Unit(0, 512, 8, ins["na_q_g"][0], HD ** -0.5, False, k.qkD, 0),
            Unit(512, 512, 8, ins["na_k_g"][0], 1.0, False, k.qkD, 8),
            Unit(1024, 512, v=512, v_dst=k.vD)])
        attend(k, "ac", [Piece(q, [(0, TOK)]) for q in range(LT)], MLA_HEADS, parts_loader(k), "three", MLA_V, k.mix[1], 0)
        attend(k, "ad", neighbour_pieces(), NA_HEADS,
               stacked_loader(k.qkD, 0, lambda i, p: i * 2 + p + 8, k.vD, lambda i, p: i * 2 + p, HD),
               "two", HD, k.mix[1], 512, bias=bias_loader(k))
        out_project(k, "o1", 1, SEQ, ins["w_out"][1])
        norm_stats(k, "n3", SEQ)
        mlp(k, "m1", 1, SEQ, ins["mlp_w1"][1], ins["mlp_w2"][1])
        closing(k)


_OUTS = [((1, SEQ, D_MODEL), "float32")]


def kernel(**inputs):
    import numpy as _np
    import concourse.bacc as _bacc
    from concourse import mybir as _mybir
    from concourse.bass_utils import run_bass_kernel_spmd as _run

    nc = _bacc.Bacc("TRN2", target_bir_lowering=False, num_devices=1)
    arrays, args = {}, {}
    for name, a in {**inputs, **shape_constants()}.items():
        a = _np.ascontiguousarray(a)
        arrays[f"in_{name}"] = a
        args[name] = nc.dram_tensor(f"in_{name}", a.shape, _mybir.dt.from_np(a.dtype), kind="ExternalInput").ap()
    out = nc.dram_tensor("out_0", _OUTS[0][0], _mybir.dt.float32, kind="ExternalOutput").ap()
    trunk(nc, out, **args)
    r = _run(nc, [arrays], core_ids=[0])
    return r.results[0]["out_0"]
```

```python
from collections import namedtuple
from contextlib import ExitStack, contextmanager
import math

import numpy as np

import concourse.bass as bass
from concourse import mybir

ALU = mybir.AluOpType
ACT = mybir.ActivationFunctionType
AX = mybir.AxisListType
F32 = mybir.dt.float32
F32R = mybir.dt.float32r

P = 128
D_MODEL = 1024
KT = D_MODEL // P
SEQ = 1024
CTX = 256
TOK = SEQ + CTX
NT = TOK // P
LT = SEQ // P
GRID_W = 64
HD = 64
EPS = 1e-6
MASKED = -2.0 ** 100
DIFF_HEADS = 4
LAM_INIT = 0.8 - 0.6 * math.exp(0.0)
FF = 4 * D_MODEL
FFC = 512
MLA_HEADS, MLA_QK, MLA_NOPE, MLA_ROPE, MLA_V = 8, 96, 64, 32, 64
MLA_QL, MLA_KVL = 512, 256
NA_HEADS, NA_COLS, NA_ROWS = 8, 16, 8
RPB_R, RPB_C = 2 * NA_ROWS - 1, 2 * NA_COLS - 1
PADW = 2 * GRID_W - 1


def r32(ap):
    return ap.bitcast(F32R)


def f32(ap):
    return ap.bitcast(F32)


@contextmanager
def phase(nc, name, sems):
    with ExitStack() as st:
        s = namedtuple("Semaphores", sems)(*[st.enter_context(nc.semaphore(f"{name}_{n}")) for n in sems.split()])
        yield s
        with nc.Block() as block:
            @block.sync
            def _(sp):
                for sem in s:
                    sp.sem_clear(sem)


def token_chunks(n):
    return [(c, min(512, n - c)) for c in range(0, n, 512)]


def shape_constants():
    out = {}

    def rope(rot):
        t = np.arange(SEQ, dtype=np.int32)
        row, col = (t // GRID_W).astype(np.float32), (t % GRID_W).astype(np.float32)
        nf = rot // 4
        freqs = np.power(np.float32(10000.0), -np.arange(nf, dtype=np.float32) / np.float32(nf)).astype(np.float32)
        ar, ac = row[:, None] * freqs, col[:, None] * freqs
        ang = np.concatenate([ar, ar, ac, ac], -1).astype(np.float32)
        cos, sin = np.cos(ang), np.sin(ang)
        sign = np.repeat(np.array([-1, 1, -1, 1], np.float32), nf)
        cos = np.concatenate([cos, np.ones((CTX, rot), np.float32)])
        sin = np.concatenate([sin * sign, np.zeros((CTX, rot), np.float32)])
        both = np.stack([cos, sin]).astype(np.float32)
        return np.ascontiguousarray(both.reshape(2, NT, P, rot).transpose(2, 0, 1, 3))

    out["rope64"] = rope(HD)
    out["rope32"] = rope(MLA_ROPE)
    out["ident"] = np.eye(P, dtype=np.float32)
    q, c = np.arange(P)[:, None], np.arange(P)[None, :]
    before, after = np.where(c >= q, 0, MASKED), np.where(c <= q, 0, MASKED)
    out["wmask"] = np.stack([before, after], 1).astype(np.float32)
    out["wband"] = np.stack([after.T, np.zeros((P, P)), before.T], 1).astype(np.float32)
    cq, ck = np.arange(GRID_W)[:, None], np.arange(GRID_W)[None, :]
    cs = np.clip(cq - NA_COLS // 2, 0, GRID_W - NA_COLS)
    col = np.where((ck >= cs) & (ck < cs + NA_COLS), 0, MASKED).astype(np.float32)
    out["cmask"] = np.concatenate([col, col], 0)
    out["cmaskT"] = np.tile(col.T, (2, 2))
    first, last = np.zeros((2, P, P), np.float32)
    first[GRID_W:, :GRID_W] = MASKED
    last[:GRID_W, :GRID_W] = MASKED
    last[:, GRID_W:] = MASKED
    out["rmask"] = np.ascontiguousarray(np.stack([first, last, first.T, last.T], 1))
    return out


class Core:

    def __init__(self, nc, st, ins, out):
        self.nc, self.ins, self.out = nc, ins, out

        def sb(name, shape, dt=F32):
            return st.enter_context(nc.sbuf_tensor(name, shape, dt))

        self.xT = sb("xT", [P, KT, TOK])
        self.rstd = sb("rstd", [P, TOK])
        self.mods = sb("mods", [P, 2, 6, KT, 2])
        self.ident = sb("ident_sb", [P, P])
        self.ones = sb("ones_sb", [P, P])
        self.identr = sb("identr_sb", [P, P], F32R)
        self.onesr = sb("onesr_sb", [P, P], F32R)
        self.eps = sb("eps_sb", [P, 1])
        self.ps = st.enter_context(nc.psum_tensor("ps", [P, 8, 512], F32))

        def dram(name, shape):
            return nc.dram_tensor(name, shape, F32, kind="Internal").ap()

        self.qkA = dram("qkA", [16, P, TOK])
        self.vA = dram("vA", [TOK, 512])
        self.qkB = dram("qkB", [10, P, TOK])
        self.vB = dram("vB", [TOK, P])
        self.qkC = dram("qkC", [16, 2, MLA_QK, TOK])
        self.vC = dram("vC", [TOK, 512])
        self.qkD = dram("qkD", [16, P, TOK])
        self.vD = dram("vD", [TOK, 512])
        self.mix = [dram(f"mix{i}", [TOK, D_MODEL]) for i in range(2)]
        self.bias = dram("rpb_bias", [GRID_W, NA_HEADS * RPB_R, GRID_W])
        self.biasT = dram("rpb_biasT", [GRID_W, RPB_R + 1, NA_HEADS, GRID_W])


def opening(k):
    nc, i = k.nc, k.ins
    names = ("consts rows rowsT cols ones neg e1 inv silu sh sl xin0 xin1 xin2 xin3 xTd xcpA xcpD "
             "aw0 aw1 aw2 whi wlo ada rowcp colT m1 modd m0")
    with phase(nc, "open", names) as s, ExitStack() as st:
        def sb(name, shape, dt=F32):
            return st.enter_context(nc.sbuf_tensor(name, shape, dt))
        HALF = D_MODEL // 2
        HF = HALF // P
        N_HALVES = 2 * 6 * D_MODEL // HALF
        XB, WB = 4, 3
        rows = sb("rows", [48, P])
        brows = sb("brows", [96, P])
        cols = sb("cols", [P, 48])
        bcols = sb("bcols", [P, 96])
        sil = sb("sil", [P, 16])
        tmp = sb("siltmp", [P, 16])
        sil4 = sb("sil4", [P, KT, 4], F32R)
        xin = sb("xin", [P, XB, D_MODEL])
        aw = sb("aw", [P, WB, KT, HALF])
        awh, awl = sb("awh", [P, 2, KT, HALF], F32R), sb("awl", [P, 2, KT, HALF], F32R)
        mrow = sb("mrow", [4, 2, HALF])
        msum = sb("msum", [P, HF, 2])
        ada_w = i["ada_w"].rearrange("l (k p) (j n) -> l j p k n", p=P, n=D_MODEL)
        x_rows = i["x"].rearrange("b (t p) d -> (b t) p d", p=P)
        ctx_rows = i["ctx"].rearrange("b (t p) d -> (b t) p d", p=P)
        TB, CB, AB = 0, 4, 6
        xin_sem, aw_sem = (s.xin0, s.xin1, s.xin2, s.xin3), (s.aw0, s.aw1, s.aw2)
        steps = [("x", t) for t in range(XB)]
        for n in range(N_HALVES):
            steps += [("ada", n)] + [("x", t) for t in (XB + 2 * n, XB + 2 * n + 1) if t < NT]

        with nc.Block() as block:
            @block.sync
            def _(sp):
                sp.dma_start(k.ident[:], i["ident"]).then_inc(s.consts, 16)
                sp.dma_start(rows[0:8, :], i["c"].rearrange("b (k p) -> (b k) p", p=P)).then_inc(s.rows, 16)
                sp.dma_start(rows[8:16, :], i["c_ctx"].rearrange("(k p) -> k p", p=P)).then_inc(s.rows, 16)
                sp.dma_start(rows[16:32, :], i["norm1_g"].rearrange("l (k p) -> (l k) p", p=P)).then_inc(s.rows, 16)
                sp.dma_start(rows[32:48, :], i["norm2_g"].rearrange("l (k p) -> (l k) p", p=P)).then_inc(s.rows, 16)
                sp.dma_start(brows[:], i["ada_b"].rearrange("l (k p) -> (l k) p", p=P)).then_inc(s.rows, 16)
                for what, n in steps:
                    if what == "x":
                        if n >= XB:
                            sp.wait_ge(s.xTd, n - XB + 1)
                        sp.dma_start(xin[:, n % XB], x_rows[n] if n < LT else ctx_rows[n - LT]).then_inc(xin_sem[n % XB], 16)
                    else:
                        if n >= WB:
                            sp.wait_ge(s.wlo, n - WB + 1)
                        c = (n % 2) * HALF
                        sp.dma_start(aw[:, n % WB], ada_w[n // 12, n // 2 % 6, :, :, c:c + HALF]).then_inc(aw_sem[n % WB], 16)

            @block.tensor
            def _(pe):
                pe.wait_ge(s.consts, 16)
                pe.wait_ge(s.rows, 80)
                pe.transpose(k.ps[:, CB, 0:48], rows[:], k.ident[0:48, 0:48])
                pe.transpose(k.ps[:, CB, 64:160], brows[:], k.ident[0:96, 0:96]).then_inc(s.rowsT, 1)

                def turn_x(t):
                    pe.wait_ge(xin_sem[t % XB], 16 * (t // XB + 1))
                    if t >= 2:
                        pe.wait_ge(s.xcpA, t - 1)
                        pe.wait_ge(s.xcpD, t - 1)
                    for f in range(KT):
                        b = TB + 2 * (t % 2) + f // 4
                        mm = pe.transpose(k.ps[:, b, (f % 4) * P:(f % 4 + 1) * P], xin[:, t % XB, f * P:(f + 1) * P], k.ident[:])
                    mm.then_inc(s.xTd, 1)

                def ada(n):
                    if n == 0:
                        pe.wait_ge(s.sl, 1)
                    pe.wait_ge(s.wlo, n + 1)
                    if n >= 2:
                        pe.wait_ge(s.rowcp, n - 1)
                    for f in range(KT):
                        o = k.ps[0:4, AB + n % 2, :]
                        pe.matmul(o, sil4[:, f], awh[:, n % 2, f], start=(f == 0), stop=False)
                        mm = pe.matmul(o, sil4[:, f], awl[:, n % 2, f], start=False, stop=(f == KT - 1))
                    mm.then_inc(s.ada, 1)

                def turn_rows(n):
                    pe.wait_ge(s.rowcp, n + 1)
                    pe.wait_ge(s.cols, 2)
                    if n >= 2:
                        pe.wait_ge(s.modd, n - 1)
                    for f in range(HF):
                        mm = pe.transpose(k.ps[:, CB + n % 2, 4 * f:4 * f + 4], mrow[:, n % 2, f * P:(f + 1) * P], k.ident[0:4, 0:4])
                    mm.then_inc(s.colT, 1)

                for what, n in steps:
                    if what == "x":
                        turn_x(n)
                    else:
                        ada(n)
                        if n:
                            turn_rows(n - 1)
                turn_rows(N_HALVES - 1)

            @block.scalar
            def _(act):
                act.wait_ge(s.cols, 2)
                nc.scalar.activation(tmp[:], cols[:, 0:16], ACT.Exp, scale=-1.0).then_inc(s.neg, 1)

                def rows_out(n):
                    act.wait_ge(s.ada, n + 1)
                    if n >= 2:
                        act.wait_ge(s.colT, n - 1)
                    nc.scalar.copy(mrow[:, n % 2], k.ps[0:4, AB + n % 2, :]).then_inc(s.rowcp, 1)

                for what, n in steps:
                    if what == "x":
                        act.wait_ge(s.xTd, n + 1)
                        nc.scalar.copy(k.xT[:, 0:4, n * P:(n + 1) * P],
                                       k.ps[:, TB + 2 * (n % 2), :].rearrange("p (f q) -> p f q", q=P)).then_inc(s.xcpA, 1)
                    else:
                        act.wait_ge(aw_sem[n % WB], 16 * (n // WB + 1))
                        if n >= 2:
                            act.wait_ge(s.ada, n - 1)
                        nc.scalar.copy(awh[:, n % 2], aw[:, n % WB]).then_inc(s.whi, 1)
                        if n:
                            rows_out(n - 1)
                rows_out(N_HALVES - 1)

            @block.vector
            def _(dve):
                nc.vector.memset(k.ones[:], 1.0).then_inc(s.ones, 1)
                nc.vector.memset(k.eps[:], EPS).then_inc(s.ones, 1)
                dve.wait_ge(s.ones, 2)
                nc.vector.tensor_copy(k.onesr[:], k.ones[:]).then_inc(s.ones, 1)
                dve.wait_ge(s.consts, 16)
                nc.vector.tensor_copy(k.identr[:], k.ident[:]).then_inc(s.ones, 1)
                dve.wait_ge(s.rowsT, 1)
                nc.vector.tensor_copy(cols[:], k.ps[:, CB, 0:48]).then_inc(s.cols, 1)
                nc.vector.tensor_copy(bcols[:], k.ps[:, CB, 64:160]).then_inc(s.cols, 1)
                dve.wait_ge(s.neg, 1)
                nc.vector.tensor_scalar(tmp[:], tmp[:], 1.0, None, ALU.add).then_inc(s.e1, 1)
                dve.wait_ge(s.e1, 1)
                nc.vector.reciprocal(tmp[:], tmp[:]).then_inc(s.inv, 1)
                dve.wait_ge(s.inv, 1)
                nc.vector.tensor_tensor(sil[:], cols[:, 0:16], tmp[:], ALU.mult).then_inc(s.silu, 1)
                dve.wait_ge(s.silu, 1)
                by_tile = sil[:].rearrange("p (w f) -> p f w", w=2)
                nc.vector.tensor_copy(sil4[:, :, 0:2], by_tile).then_inc(s.sh, 1)
                dve.wait_ge(s.sh, 1)
                nc.vector.tensor_tensor(sil4[:, :, 2:4], by_tile, f32(sil4[:, :, 0:2]), ALU.subtract).then_inc(s.sl, 1)

                def modulation(n):
                    l, j, f0 = n // 12, n // 2 % 6, (n % 2) * HF
                    dve.wait_ge(s.colT, n + 1)
                    if n:
                        dve.wait_ge(s.modd, n)
                    part = k.ps[:, CB + n % 2, 0:4 * HF].rearrange("p (f a) -> p f a", a=4)
                    c = (n // 2) * KT + f0
                    nc.vector.tensor_tensor(msum[:], part[:, :, 0:2], bcols[:, c:c + HF].unsqueeze(2).broadcast_to([P, HF, 2]),
                                            ALU.add).then_inc(s.m1, 1)
                    dve.wait_ge(s.m1, n + 1)
                    m = k.mods[:, l, j, f0:f0 + HF]
                    nc.vector.tensor_tensor(m, msum[:], part[:, :, 2:4], ALU.add).then_inc(s.modd, 1)
                    if j in (1, 4):
                        c = (16 if j == 1 else 32) + l * KT + f0
                        dve.wait_ge(s.modd, n + 1)
                        nc.vector.scalar_tensor_tensor(out=m, in0=m, scalar=1.0,
                                                       in1=cols[:, c:c + HF].unsqueeze(2).broadcast_to([P, HF, 2]),
                                                       op0=ALU.add, op1=ALU.mult).then_inc(s.m0, 1)

                for what, n in steps:
                    if what == "x":
                        dve.wait_ge(s.xTd, n + 1)
                        nc.vector.tensor_copy(k.xT[:, 4:8, n * P:(n + 1) * P],
                                              k.ps[:, TB + 2 * (n % 2) + 1, :].rearrange("p (f q) -> p f q", q=P)).then_inc(s.xcpD, 1)
                    else:
                        dve.wait_ge(s.whi, n + 1)
                        if n >= 2:
                            dve.wait_ge(s.ada, n - 1)
                        nc.vector.tensor_tensor(awl[:, n % 2], aw[:, n % WB], f32(awh[:, n % 2]), ALU.subtract).then_inc(s.wlo, 1)
                        if n >= 2:
                            modulation(n - 2)
                modulation(N_HALVES - 2)
                modulation(N_HALVES - 1)


def norm_stats(k, name, n_tok):
    nc = k.nc
    with phase(nc, name, "sq acc sum root") as s, ExitStack() as st:
        sq = st.enter_context(nc.sbuf_tensor(f"{name}_sq", [P, 2, TOK], F32))
        acc = st.enter_context(nc.sbuf_tensor(f"{name}_acc", [P, TOK], F32))
        chunks = token_chunks(n_tok)
        with nc.Block() as block:
            @block.scalar
            def _(act):
                for f in range(KT):
                    if f >= 2:
                        act.wait_ge(s.acc, f - 1)
                    nc.scalar.activation(sq[:, f % 2, 0:n_tok], k.xT[:, f, 0:n_tok], ACT.Square).then_inc(s.sq, 1)
                act.wait_ge(s.sum, 1)
                for c, (c0, n) in enumerate(chunks):
                    nc.scalar.activation(k.rstd[:, c0:c0 + n], k.ps[:, c, 0:n], ACT.Sqrt, bias=k.eps[:],
                                         scale=1.0 / D_MODEL).then_inc(s.root, 1)

            @block.vector
            def _(dve):
                for f in range(KT):
                    dve.wait_ge(s.sq, f + 1)
                    if f == 0:
                        nc.vector.tensor_copy(acc[:, 0:n_tok], sq[:, 0, 0:n_tok]).then_inc(s.acc, 1)
                    else:
                        dve.wait_ge(s.acc, f)
                        nc.vector.tensor_tensor(acc[:, 0:n_tok], acc[:, 0:n_tok], sq[:, f % 2, 0:n_tok],
                                                ALU.add).then_inc(s.acc, 1)
                for c, (c0, n) in enumerate(chunks):
                    dve.wait_ge(s.root, c + 1)
                    nc.vector.reciprocal(k.rstd[:, c0:c0 + n], k.rstd[:, c0:c0 + n])

            @block.tensor
            def _(pe):
                pe.wait_ge(s.acc, KT)
                for c, (c0, n) in enumerate(chunks):
                    mm = pe.matmul(k.ps[:, c, 0:n], k.ones[:], acc[:, c0:c0 + n], start=True, stop=True)
                mm.then_inc(s.sum, 1)


def at_tile(i, p):
    return i * 2 + p


def wait_then_store(sp, sem, value, begun):
    sp.wait_ge(sem, value)
    sp.sem_inc(begun, 1)


def walk_pairs(eng, pair):
    pair(0, True, False)
    with eng.Fori(1, NT // 2 - 1) as i:
        pair(i, False, False)
    pair(NT // 2 - 1, False, True)


def load_weights(sp, s, raw, w_dram, n_k, first_waits=None):
    for f in range(n_k):
        if f >= 2:
            sp.wait_ge(s.wlo, f - 1)
        sp.dma_start(raw[:, f % 2], w_dram[f]).then_inc(s.wraw0 if f % 2 == 0 else s.wraw1, 16)


def cut_hi(nc, act, s, raw, wh, n_k):
    for f in range(n_k):
        act.wait_ge(s.wraw0 if f % 2 == 0 else s.wraw1, 16 * (f // 2 + 1))
        nc.scalar.copy(wh[:, f], raw[:, f % 2]).then_inc(s.whi, 1)


def cut_lo(nc, dve, s, raw, wh, wl, n_k):
    for f in range(n_k):
        dve.wait_ge(s.whi, f + 1)
        nc.vector.tensor_tensor(wl[:, f], raw[:, f % 2], f32(wh[:, f]), ALU.subtract).then_inc(s.wlo, 1)


class Unit:

    def __init__(self, c0, width, heads=0, gain=None, gain_scale=1.0, rope=False, dst=None, base=0, v=0, v_dst=None):
        self.c0, self.width, self.heads, self.gain, self.gain_scale = c0, width, heads, gain, gain_scale
        self.rope, self.dst, self.base, self.v, self.v_dst = rope, dst, base, v, v_dst


def project(k, name, layer, w_in, col0, n_cols, units):
    nc = k.nc
    U = len(units)
    hu = [j for j, u in enumerate(units) if u.heads]
    HU = len(hu)
    vu = [j for j, u in enumerate(units) if u.v]
    VU = len(vu)
    assert HU == 2
    ropes = sum(1 for j in hu if units[j].rope)
    assert ropes in (0, 2)
    slots = []
    for j in range(U):
        slots.append(("mm", j))
        if j == 0 and hu[-1] == U - 1:
            slots.append(("turn", HU - 1, -1))
        for n, h in enumerate(hu):
            if h == j - 1:
                slots.append(("turn", n, 0))
    names = ("gains ropec fbase fmod h wraw0 wraw1 whi wlo mm sq red y root ri yn u w yf hi lo tr tc qd0 qd1 vc va0 va1 vb0 vb1 modt ht begun")
    with phase(nc, name, names) as s, ExitStack() as st:
        def sb(nm, shape, dt=F32):
            return st.enter_context(nc.sbuf_tensor(f"{name}_{nm}", shape, dt))
        wh, wl = sb("wh", [P, KT, n_cols], F32R), sb("wl", [P, KT, n_cols], F32R)
        raw = sb("wraw", [P, 2, n_cols])
        h = sb("hfull", [P, KT, P])
        hh, hl = sb("hh", [P, 2, KT, P], F32R), sb("hl", [P, 2, KT, P], F32R)
        modt = sb("modt", [P, NT, 2, KT])
        sq, y = sb("sqh", [P, 512]), sb("yh", [P, 512])
        w_, u_ = (sb("w_", [P, 512]), sb("u_", [P, 512])) if ropes else (None, None)
        rs = sb("rsh", [P, 8])
        qh = [sb(f"qh{n}", [P, 8, 2, HD], F32R) for n in range(HU)]
        stage = sb("stage", [P, 2, 8, P])
        vst = [sb(f"vst{n}", [P, 2, units[j].v]) for n, j in enumerate(vu)]
        gain = [sb(f"gain{n}", [P, HD]) for n in range(HU)]
        rope = sb("rope", [P, 2, NT, HD]) if ropes else None
        sint = sb("sint", [P, 2, HD]) if ropes else None
        w_dram = w_in.rearrange("(f p) n -> f p n", p=P)[:, :, col0:col0 + n_cols]
        TB = 4

        def v_stored(j, p):
            return ((s.va0, s.va1), (s.vb0, s.vb1))[vu.index(j)][p]

        def done(i, p, per, j):
            return (i * 2 + p) * per + j + 1

        with nc.Block() as block:
            @block.sync
            def _(sp):
                for n, j in enumerate(hu):
                    sp.dma_start(gain[n][:], units[j].gain.unsqueeze(0).broadcast_to([P, HD])).then_inc(s.gains, 16)
                if ropes:
                    sp.dma_start(rope[:], k.ins["rope64"]).then_inc(s.ropec, 16)
                load_weights(sp, s, raw, w_dram, KT)

                def store_heads(n, i, p):
                    u = units[hu[n]]
                    wait_then_store(sp, s.tc, done(i, p, HU, n), s.begun)
                    dst = u.dst[u.base:u.base + u.heads].rearrange("h r q -> r h q")
                    sp.dma_start(dst[:, :, bass.ds(at_tile(i, p) * P, P)], stage[:, n, 0:u.heads]).then_inc(
                        s.qd0 if n == 0 else s.qd1, 16)

                def store_v(j, i, p):
                    n = vu.index(j)
                    wait_then_store(sp, s.vc, done(i, p, VU, n), s.begun)
                    sp.dma_start(units[j].v_dst[bass.ds(at_tile(i, p) * P, P)], vst[n][:, p]).then_inc(v_stored(j, p), 16)

                def pair(i, first, last):
                    for p in range(2):
                        for slot in slots:
                            if slot[0] == "turn" and not (first and p + slot[2] < 0):
                                store_heads(slot[1], i, p + slot[2])
                            if slot[0] == "mm" and units[slot[1]].v:
                                store_v(slot[1], i, p)
                walk_pairs(sp, pair)
                if hu[-1] == U - 1:
                    store_heads(HU - 1, NT // 2 - 1, 1)
                sp.wait_ge(s.qd0, 16 * NT)
                sp.wait_ge(s.qd1, 16 * NT)
                for j in vu:
                    for p in range(2):
                        sp.wait_ge(v_stored(j, p), 16 * (NT // 2))

            @block.tensor
            def _(pe):
                def products(j, i, p, first):
                    u = units[j]
                    if j == 0:
                        pe.wait_ge(s.h, done(i, p, 1, 0))
                    if not (first and p == 0):
                        if u.heads:
                            pe.wait_ge(s.y, done(i, p - 1, HU, hu.index(j)))
                        else:
                            pe.wait_ge(s.vc, done(i, p - 1, VU, vu.index(j)))
                    c = slice(u.c0, u.c0 + u.width)
                    for f in range(KT):
                        if first and p == 0 and j == 0:
                            pe.wait_ge(s.wlo, f + 1)
                        o = k.ps[:, j, 0:u.width]
                        pe.matmul(o, hh[:, p, f], wh[:, f, c], start=(f == 0), stop=False)
                        pe.matmul(o, hh[:, p, f], wl[:, f, c], start=False, stop=False)
                        mm = pe.matmul(o, hl[:, p, f], wh[:, f, c], start=False, stop=(f == KT - 1))
                    mm.then_inc(s.mm, 1)

                def turn(n, i, p, free):
                    u = units[hu[n]]
                    pe.wait_ge(s.lo, done(i, p, HU, n))
                    if free:
                        pe.wait_ge(s.tc, done(i, p - 1, HU, n))
                    for x in range(u.heads):
                        mm = pe.transpose(k.ps[:, TB + 2 * n + x // 4, (x % 4) * P:(x % 4 + 1) * P],
                                          f32(qh[n][:, x].rearrange("p a d -> p (a d)")), k.ident[:])
                    mm.then_inc(s.tr, 1)

                def pair(i, first, last):
                    for p in range(2):
                        for slot in slots:
                            if slot[0] == "mm":
                                products(slot[1], i, p, first)
                            elif not (first and p + slot[2] < 0):
                                turn(slot[1], i, p + slot[2], not (first and p + slot[2] <= 0))
                walk_pairs(pe, pair)
                if hu[-1] == U - 1:
                    turn(HU - 1, NT // 2 - 1, 1, True)

            @block.scalar
            def _(act):
                def modulate(i, p):
                    t = at_tile(i, p)
                    act.wait_ge(s.fbase, done(i, p, 1, 0))
                    if ropes:
                        nc.scalar.copy(sint[:, p % 2], rope[:, 1, bass.ds(t, 1)].squeeze(1))
                    for f in range(KT):
                        a = nc.scalar.activation(h[:, f], h[:, f], ACT.Identity,
                                                 scale=modt[:, bass.ds(t, 1), 0, f],
                                                 bias=modt[:, bass.ds(t, 1), 1, f])
                    a.then_inc(s.fmod, 1)

                def squares(j, i, p, first):
                    u, n = units[j], hu.index(j)
                    act.wait_ge(s.mm, done(i, p, U, j))
                    if not (first and p == 0 and n == 0):
                        act.wait_ge(s.red, done(i, p, HU, n - 1))
                    nc.scalar.activation(sq[:, 0:u.heads * HD], k.ps[:, j, 0:u.heads * HD], ACT.Square).then_inc(s.sq, 1)
                    act.wait_ge(s.red, done(i, p, HU, n))
                    nc.scalar.activation(rs[:, 0:u.heads], rs[:, 0:u.heads], ACT.Sqrt, bias=k.eps[:],
                                         scale=1.0 / HD).then_inc(s.root, 1)

                def values(j, i, p, first):
                    u = units[j]
                    act.wait_ge(s.mm, done(i, p, U, j))
                    if not first:
                        act.wait_ge(v_stored(j, p), i * 16)
                    nc.scalar.copy(vst[vu.index(j)][:, p], k.ps[:, j, u.heads * HD:u.heads * HD + u.v]).then_inc(s.vc, 1)

                def stage_heads(n, i, p, free):
                    u = units[hu[n]]
                    act.wait_ge(s.tr, done(i, p, HU, n))
                    if free:
                        act.wait_ge(s.qd0 if n == 0 else s.qd1, at_tile(i, p) * 16)
                    nc.scalar.copy(stage[:, n, 0:u.heads],
                                   k.ps[:, TB + 2 * n:TB + 2 * n + 2].rearrange("p b (x q) -> p (b x) q", q=P)[:, 0:u.heads]).then_inc(s.tc, 1)

                act.wait_ge(s.modt, 2)
                if ropes:
                    act.wait_ge(s.ropec, 16)
                modulate(0, 0)
                cut_hi(nc, act, s, raw, wh, KT)

                def pair(i, first, last):
                    for p in range(2):
                        for x, slot in enumerate(slots):
                            if slot[0] == "mm":
                                if units[slot[1]].v:
                                    values(slot[1], i, p, first)
                                if units[slot[1]].heads:
                                    squares(slot[1], i, p, first)
                            elif not (first and p + slot[2] < 0):
                                stage_heads(slot[1], i, p + slot[2], not (first and p + slot[2] <= 0))
                            if x == 0 and not (last and p == 1):
                                modulate(i, p + 1)
                walk_pairs(act, pair)
                if hu[-1] == U - 1:
                    stage_heads(HU - 1, NT // 2 - 1, 1, True)

            @block.vector
            def _(dve):
                for w in range(2):
                    dst = modt[:, 0:LT, :, :] if w == 0 else modt[:, LT:NT, :, :]
                    n = LT if w == 0 else NT - LT
                    for c, part in ((0, 1), (1, 0)):
                        m = nc.vector.tensor_copy(dst[:, :, c], k.mods[:, layer, part, :, w].unsqueeze(1).broadcast_to([P, n, KT]))
                    m.then_inc(s.modt, 1)
                dve.wait_ge(s.gains, 16 * HU)
                for n, j in enumerate(hu):
                    if units[j].gain_scale != 1.0:
                        nc.vector.tensor_scalar(gain[n][:], gain[n][:], units[j].gain_scale, None, ALU.mult).then_inc(s.modt, 1)
                scaled = 2 + sum(1 for j in hu if units[j].gain_scale != 1.0)

                def base(i, p, first):
                    q = bass.ds(at_tile(i, p) * P, P)
                    if not first:
                        dve.wait_ge(s.h, done(i, p - 1, 1, 0))
                    nc.vector.tensor_tensor(h[:], k.xT[:, :, q], k.rstd[:, q].unsqueeze(1).broadcast_to([P, KT, P]),
                                            ALU.mult).then_inc(s.fbase, 1)

                def cut(i, p, first):
                    dve.wait_ge(s.fmod, done(i, p, 1, 0))
                    if not first:
                        dve.wait_ge(s.mm, done(i, p - 2, U, U - 1))
                    nc.vector.tensor_copy(hh[:, p % 2], h[:]).then_inc(s.ht, 1)
                    dve.wait_ge(s.ht, done(i, p, 1, 0))
                    nc.vector.tensor_tensor(hl[:, p % 2], h[:], f32(hh[:, p % 2]), ALU.subtract).then_inc(s.h, 1)

                def heads(j, i, p, first):
                    u, n = units[j], hu.index(j)
                    H, W = u.heads, u.heads * HD
                    me = done(i, p, HU, n)
                    v3 = lambda ap: ap[:, 0:W].rearrange("p (h d) -> p h d", d=HD)
                    dve.wait_ge(s.sq, me)
                    if not (first and p == 0 and n == 0):
                        dve.wait_ge(s.lo, done(i, p, HU, n - 1))
                    nc.vector.tensor_reduce(rs[:, 0:H], v3(sq), AX.X, ALU.add).then_inc(s.red, 1)
                    nc.vector.tensor_tensor(v3(y), v3(k.ps[:, j]), gain[n][:].unsqueeze(1).broadcast_to([P, H, HD]),
                                            ALU.mult).then_inc(s.y, 1)
                    dve.wait_ge(s.root, me)
                    nc.vector.reciprocal(rs[:, 0:H], rs[:, 0:H]).then_inc(s.ri, 1)
                    dve.wait_ge(s.ri, me)
                    dve.wait_ge(s.y, me)
                    nc.vector.tensor_tensor(v3(y), v3(y), rs[:, 0:H].unsqueeze(2).broadcast_to([P, H, HD]),
                                            ALU.mult).then_inc(s.yn, 1)
                    dve.wait_ge(s.yn, me)
                    if ropes:
                        cos = rope[:, 0, bass.ds(at_tile(i, p), 1)].broadcast_to([P, H, HD])
                        nc.vector.tensor_tensor(v3(w_), v3(y), cos, ALU.mult).then_inc(s.w, 1)
                        dve.wait_ge(s.w, me)
                        dve.wait_ge(s.u, me)
                        nc.vector.tensor_tensor(y[:, 0:W], w_[:, 0:W], u_[:, 0:W], ALU.add).then_inc(s.yf, 1)
                        dve.wait_ge(s.yf, me)
                    if not (first and p == 0):
                        dve.wait_ge(s.tr, done(i, p - 1, HU, n))
                    nc.vector.tensor_copy(qh[n][:, 0:H, 0], v3(y)).then_inc(s.hi, 1)
                    dve.wait_ge(s.hi, me)
                    nc.vector.tensor_tensor(qh[n][:, 0:H, 1], v3(y), f32(qh[n][:, 0:H, 0]), ALU.subtract).then_inc(s.lo, 1)

                base(0, 0, True)
                cut(0, 0, True)
                cut_lo(nc, dve, s, raw, wh, wl, KT)
                dve.wait_ge(s.modt, scaled)
                if ropes:
                    dve.wait_ge(s.ropec, 16)

                def pair(i, first, last):
                    for p in range(2):
                        more = not (last and p == 1)
                        if more:
                            base(i, p + 1, False)
                        for x, j in enumerate(hu):
                            heads(j, i, p, first)
                            if x == 0 and more:
                                cut(i, p + 1, first and p == 0)
                walk_pairs(dve, pair)

            @block.gpsimd
            def _(pool):
                if ropes:
                    def pair(i, first, last):
                        for p in range(2):
                            for n, j in enumerate(hu):
                                H = units[j].heads
                                pool.wait_ge(s.yn, done(i, p, HU, n))
                                v5 = lambda ap: ap[:, 0:H * HD].rearrange("p (h a b d) -> p h a b d", a=2, b=2, d=HD // 4)
                                sin = sint[:, p:p + 1].rearrange("p o (a b d) -> p o a b d", a=2, b=2)
                                for b in range(2):
                                    ins = nc.gpsimd.tensor_tensor(v5(u_)[:, :, :, b], v5(y)[:, :, :, 1 - b],
                                                                  sin[:, :, :, b].broadcast_to([P, H, 2, HD // 4]), ALU.mult)
                                ins.then_inc(s.u, 1)
                    walk_pairs(pool, pair)


def project_low_rank(k, name, layer, w_in, col0, n_cols, rank, rank_gain, w_up, heads_gain, gain_scale, base, with_values):
    nc = k.nc
    H, D, R = MLA_HEADS, MLA_QK, MLA_ROPE
    RT = rank // P
    up = w_up.shape[1]
    UC = token_chunks(up)
    names = ("gains ropec fbase fmod h ht wraw0 wraw1 whi wlo ur0 ur1 uhi ulo mm sql rl rli low ah alo at atc up kn kr vc "
             "sqd red y root ri yn w u yf hi lo tr tc qd0 qd1 qd2 qd3 va0 va1 modt begun")
    with phase(nc, name, names) as s, ExitStack() as st:
        def sb(nm, shape, dt=F32):
            return st.enter_context(nc.sbuf_tensor(f"{name}_{nm}", shape, dt))
        wh, wl = sb("wh", [P, KT, n_cols], F32R), sb("wl", [P, KT, n_cols], F32R)
        uh, ul = sb("uph", [P, RT, up], F32R), sb("upl", [P, RT, up], F32R)
        raw, uraw = sb("wraw", [P, 2, n_cols]), sb("uraw", [P, 2, up])
        h = sb("hfull", [P, KT, P])
        hh, hl = sb("hh", [P, 2, KT, P], F32R), sb("hl", [P, 2, KT, P], F32R)
        modt = sb("modt", [P, NT, 2, KT])
        lsum, lr = sb("lsum", [P, 1]), sb("lr", [P, 1])
        low = sb("low", [P, rank])
        lowc = sb("lowc", [P, 2, rank], F32R)
        lowT = sb("lowT", [P, 2, RT, P], F32R)
        kr = sb("kr", [P, 2, R]) if with_values else None
        sq, y = sb("sqh", [P, H, D]), sb("yh", [P, H, D])
        w_, u_ = sb("w_", [P, H, R]), sb("u_", [P, H, R])
        rs = sb("rsh", [P, H])
        qh = sb("qh", [P, H, 2, D], F32R)
        stage = sb("stage", [D, 4, 4, P])
        vst = sb("vst", [P, 2, H * MLA_V]) if with_values else None
        rgain, gain = sb("rgain", [P, rank]), sb("gain", [P, D])
        rope = sb("rope", [P, 2, NT, R])
        w_dram = w_in.rearrange("(f p) n -> f p n", p=P)[:, :, col0:col0 + n_cols]
        u_dram = w_up.rearrange("(f p) n -> f p n", p=P)
        IB, LB, UB, TB = 0, 1, 3, 5
        ups = k.ps[:, UB:UB + 2].rearrange("p b c -> p (b c)")

        def n1(i, p):
            return i * 2 + p + 1

        def batch(i, p, b):
            return (i * 2 + p) * 4 + b + 1

        with nc.Block() as block:
            @block.sync
            def _(sp):
                sp.dma_start(rgain[:], rank_gain.unsqueeze(0).broadcast_to([P, rank])).then_inc(s.gains, 16)
                sp.dma_start(gain[:], heads_gain.unsqueeze(0).broadcast_to([P, D])).then_inc(s.gains, 16)
                sp.dma_start(rope[:], k.ins["rope32"]).then_inc(s.ropec, 16)
                load_weights(sp, s, raw, w_dram, KT)
                for f in range(RT):
                    if f >= 2:
                        sp.wait_ge(s.ulo, f - 1)
                    sp.dma_start(uraw[:, f % 2], u_dram[f]).then_inc(s.ur0 if f % 2 == 0 else s.ur1, 16)

                def pair(i, first, last):
                    for p in range(2):
                        if with_values:
                            wait_then_store(sp, s.vc, n1(i, p), s.begun)
                            sp.dma_start(k.vC[bass.ds(at_tile(i, p) * P, P)], vst[:, p]).then_inc(s.va0 if p == 0 else s.va1, 16)
                        for b in range(4):
                            wait_then_store(sp, s.tc, batch(i, p, b), s.begun)
                            dst = k.qkC[base + 2 * b:base + 2 * b + 2].rearrange("h a r q -> r (h a) q")
                            sp.dma_start(dst[:, :, bass.ds(at_tile(i, p) * P, P)], stage[:, b]).then_inc(
                                (s.qd0, s.qd1, s.qd2, s.qd3)[b], 16)
                walk_pairs(sp, pair)
                for q in (s.qd0, s.qd1, s.qd2, s.qd3):
                    sp.wait_ge(q, 16 * NT)
                if with_values:
                    sp.wait_ge(s.va0, 16 * (NT // 2))
                    sp.wait_ge(s.va1, 16 * (NT // 2))

            @block.tensor
            def _(pe):
                def products(i, p, first):
                    pe.wait_ge(s.h, n1(i, p))
                    if not (first and p == 0):
                        pe.wait_ge(s.low, n1(i, p - 1))
                        if with_values:
                            pe.wait_ge(s.kr, n1(i, p - 1))
                    for f in range(KT):
                        if first and p == 0:
                            pe.wait_ge(s.wlo, f + 1)
                        o = k.ps[:, IB, 0:n_cols]
                        pe.matmul(o, hh[:, p, f], wh[:, f], start=(f == 0), stop=False)
                        pe.matmul(o, hh[:, p, f], wl[:, f], start=False, stop=False)
                        mm = pe.matmul(o, hl[:, p, f], wh[:, f], start=False, stop=(f == KT - 1))
                    mm.then_inc(s.mm, 1)

                def turn_low(i, p, free):
                    pe.wait_ge(s.alo, n1(i, p))
                    if free:
                        pe.wait_ge(s.atc, n1(i, p - 1))
                    for a in range(2):
                        for f in range(RT):
                            mm = pe.transpose(k.ps[:, LB + a, f * P:(f + 1) * P], f32(lowc[:, a, f * P:(f + 1) * P]), k.ident[:])
                    mm.then_inc(s.at, 1)

                def up_products(i, p, free, first):
                    pe.wait_ge(s.atc, n1(i, p))
                    if free:
                        pe.wait_ge(s.y if not with_values else s.vc, n1(i, p - 1))
                    if first:
                        pe.wait_ge(s.ulo, RT)
                    for c0, n in UC:
                        for f in range(RT):
                            o, c = ups[:, c0:c0 + n], slice(c0, c0 + n)
                            pe.matmul(o, lowT[:, 0, f], uh[:, f, c], start=(f == 0), stop=False)
                            pe.matmul(o, lowT[:, 0, f], ul[:, f, c], start=False, stop=False)
                            mm = pe.matmul(o, lowT[:, 1, f], uh[:, f, c], start=False, stop=(f == RT - 1))
                    mm.then_inc(s.up, 1)

                def turn_heads(i, p, free):
                    pe.wait_ge(s.lo, n1(i, p))
                    for b in range(4):
                        if free or b >= 2:
                            pe.wait_ge(s.tc, batch(i, p, b - 2))
                        for x in range(4):
                            mm = pe.transpose(k.ps[0:D, TB + b % 2, x * P:(x + 1) * P],
                                              f32(qh[:, 2 * b + x // 2, x % 2]), k.ident[:])
                        mm.then_inc(s.tr, 1)

                def pair(i, first, last):
                    for p in range(2):
                        products(i, p, first)
                        if not (first and p == 0):
                            turn_heads(i, p - 1, not (first and p == 1))
                        turn_low(i, p, not (first and p == 0))
                        up_products(i, p, not (first and p == 0), first and p == 0)
                walk_pairs(pe, pair)
                turn_heads(NT // 2 - 1, 1, True)

            @block.scalar
            def _(act):
                def modulate(i, p):
                    t = at_tile(i, p)
                    act.wait_ge(s.fbase, n1(i, p))
                    for f in range(KT):
                        a = nc.scalar.activation(h[:, f], h[:, f], ACT.Identity, scale=modt[:, bass.ds(t, 1), 0, f],
                                                 bias=modt[:, bass.ds(t, 1), 1, f])
                    a.then_inc(s.fmod, 1)

                def low_rank(i, p, first):
                    act.wait_ge(s.mm, n1(i, p))
                    if with_values:
                        if not first:
                            act.wait_ge(s.kn, n1(i, p - 2))
                        nc.scalar.copy(kr[:, p], k.ps[:, IB, rank:rank + R]).then_inc(s.kr, 1)
                    if not (first and p == 0):
                        act.wait_ge(s.low, n1(i, p - 1))
                        act.wait_ge(s.red, n1(i, p - 1))
                    nc.scalar.activation(sq[:].rearrange("p h d -> p (h d)")[:, 0:rank], k.ps[:, IB, 0:rank], ACT.Square,
                                         accum_out=lsum[:]).then_inc(s.sql, 1)
                    act.wait_ge(s.sql, n1(i, p))
                    nc.scalar.activation(lr[:], lsum[:], ACT.Sqrt, bias=k.eps[:], scale=1.0 / rank).then_inc(s.rl, 1)

                def stage_low(i, p, free):
                    act.wait_ge(s.at, n1(i, p))
                    if free:
                        act.wait_ge(s.up, n1(i, p - 1))
                    nc.scalar.copy(lowT[:], k.ps[:, LB:LB + 2].rearrange("p a (f q) -> p a f q", q=P)[:, :, 0:RT]).then_inc(s.atc, 1)

                def heads(i, p, first):
                    act.wait_ge(s.up, n1(i, p))
                    if with_values:
                        if not (first and p == 0):
                            act.wait_ge(s.lo, n1(i, p - 1))
                        if not first:
                            act.wait_ge(s.va0 if p == 0 else s.va1, i * 16)
                        up3 = ups.rearrange("p (h d) -> p h d", d=MLA_NOPE + MLA_V)
                        nc.scalar.copy(y[:, :, 0:MLA_NOPE], up3[:, :, 0:MLA_NOPE])
                        nc.scalar.copy(y[:, :, MLA_NOPE:D], kr[:, p:p + 1].broadcast_to([P, H, R])).then_inc(s.kn, 1)
                        nc.scalar.copy(vst[:, p].rearrange("p (h d) -> p h d", d=MLA_V), up3[:, :, MLA_NOPE:]).then_inc(s.vc, 1)
                        act.wait_ge(s.kn, n1(i, p))
                        nc.scalar.activation(sq[:], y[:], ACT.Square).then_inc(s.sqd, 1)
                    else:
                        nc.scalar.activation(sq[:], ups[:, 0:H * D].rearrange("p (h d) -> p h d", d=D), ACT.Square).then_inc(s.sqd, 1)
                    act.wait_ge(s.red, n1(i, p))
                    nc.scalar.activation(rs[:], rs[:], ACT.Sqrt, bias=k.eps[:], scale=1.0 / D).then_inc(s.root, 1)

                def stage_heads(i, p, free):
                    for b in range(4):
                        act.wait_ge(s.tr, batch(i, p, b))
                        if free:
                            act.wait_ge((s.qd0, s.qd1, s.qd2, s.qd3)[b], at_tile(i, p) * 16)
                        nc.scalar.copy(stage[:, b], k.ps[0:D, TB + b % 2].rearrange("p (x q) -> p x q", q=P)).then_inc(s.tc, 1)

                act.wait_ge(s.modt, 2)
                modulate(0, 0)
                cut_hi(nc, act, s, raw, wh, KT)
                for f in range(RT):
                    act.wait_ge(s.ur0 if f % 2 == 0 else s.ur1, 16 * (f // 2 + 1))
                    nc.scalar.copy(uh[:, f], uraw[:, f % 2]).then_inc(s.uhi, 1)

                def pair(i, first, last):
                    for p in range(2):
                        low_rank(i, p, first)
                        if not (first and p == 0):
                            stage_heads(i, p - 1, not (first and p == 1))
                        stage_low(i, p, not (first and p == 0))
                        if not (last and p == 1):
                            modulate(i, p + 1)
                        heads(i, p, first)
                walk_pairs(act, pair)
                stage_heads(NT // 2 - 1, 1, True)

            @block.vector
            def _(dve):
                for w in range(2):
                    dst = modt[:, 0:LT, :, :] if w == 0 else modt[:, LT:NT, :, :]
                    n = LT if w == 0 else NT - LT
                    for c, part in ((0, 1), (1, 0)):
                        m = nc.vector.tensor_copy(dst[:, :, c], k.mods[:, layer, part, :, w].unsqueeze(1).broadcast_to([P, n, KT]))
                    m.then_inc(s.modt, 1)
                dve.wait_ge(s.gains, 32)
                nc.vector.tensor_scalar(gain[:], gain[:], gain_scale, None, ALU.mult).then_inc(s.modt, 1)

                def base_(i, p, first):
                    q = bass.ds(at_tile(i, p) * P, P)
                    if not first:
                        dve.wait_ge(s.h, n1(i, p - 1))
                    nc.vector.tensor_tensor(h[:], k.xT[:, :, q], k.rstd[:, q].unsqueeze(1).broadcast_to([P, KT, P]),
                                            ALU.mult).then_inc(s.fbase, 1)

                def cut(i, p, first):
                    dve.wait_ge(s.fmod, n1(i, p))
                    if not first:
                        dve.wait_ge(s.mm, n1(i, p - 2))
                    nc.vector.tensor_copy(hh[:, p % 2], h[:]).then_inc(s.ht, 1)
                    dve.wait_ge(s.ht, n1(i, p))
                    nc.vector.tensor_tensor(hl[:, p % 2], h[:], f32(hh[:, p % 2]), ALU.subtract).then_inc(s.h, 1)

                def low_rank(i, p, first):
                    me = n1(i, p)
                    dve.wait_ge(s.rl, me)
                    nc.vector.reciprocal(lr[:], lr[:]).then_inc(s.rli, 1)
                    dve.wait_ge(s.rli, me)
                    if not (first and p == 0):
                        dve.wait_ge(s.alo, n1(i, p - 1))
                    nc.vector.scalar_tensor_tensor(out=low[:], in0=k.ps[:, IB, 0:rank], scalar=lr[:, 0:1], in1=rgain[:],
                                                   op0=ALU.mult, op1=ALU.mult).then_inc(s.low, 1)
                    dve.wait_ge(s.low, me)
                    if not (first and p == 0):
                        dve.wait_ge(s.at, n1(i, p - 1))
                    nc.vector.tensor_copy(lowc[:, 0], low[:]).then_inc(s.ah, 1)
                    dve.wait_ge(s.ah, me)
                    nc.vector.tensor_tensor(lowc[:, 1], low[:], f32(lowc[:, 0]), ALU.subtract).then_inc(s.alo, 1)

                def heads(i, p, first):
                    me = n1(i, p)
                    dve.wait_ge(s.sqd, me)
                    nc.vector.tensor_reduce(rs[:], sq[:], AX.X, ALU.add).then_inc(s.red, 1)
                    src = y[:] if with_values else ups[:, 0:H * D].rearrange("p (h d) -> p h d", d=D)
                    if not with_values and not (first and p == 0):
                        dve.wait_ge(s.lo, n1(i, p - 1))
                    nc.vector.tensor_tensor(y[:], src, gain[:].unsqueeze(1).broadcast_to([P, H, D]), ALU.mult).then_inc(s.y, 1)
                    dve.wait_ge(s.root, me)
                    nc.vector.reciprocal(rs[:], rs[:]).then_inc(s.ri, 1)
                    dve.wait_ge(s.ri, me)
                    dve.wait_ge(s.y, me)
                    nc.vector.tensor_tensor(y[:], y[:], rs[:].unsqueeze(2).broadcast_to([P, H, D]), ALU.mult).then_inc(s.yn, 1)
                    dve.wait_ge(s.yn, me)
                    if not (first and p == 0):
                        dve.wait_ge(s.yf, n1(i, p - 1))
                    t = bass.ds(at_tile(i, p), 1)
                    rot = y[:, :, MLA_NOPE:D]
                    nc.vector.tensor_tensor(w_[:], rot, rope[:, 0, t].broadcast_to([P, H, R]), ALU.mult).then_inc(s.w, 1)
                    v5 = lambda ap: ap.rearrange("p h (a b d) -> p h a b d", a=2, b=2)
                    sin = v5(rope[:, 1, t])
                    for b in range(2):
                        ins = nc.vector.tensor_tensor(v5(u_[:])[:, :, :, b], v5(rot)[:, :, :, 1 - b],
                                                      sin[:, :, :, b].broadcast_to([P, H, 2, R // 4]), ALU.mult)
                    ins.then_inc(s.u, 1)
                    dve.wait_ge(s.w, me)
                    dve.wait_ge(s.u, me)
                    nc.vector.tensor_tensor(rot, w_[:], u_[:], ALU.add).then_inc(s.yf, 1)
                    dve.wait_ge(s.yf, me)
                    if not (first and p == 0):
                        dve.wait_ge(s.tr, batch(i, p - 1, 3))
                    nc.vector.tensor_copy(qh[:, :, 0], y[:]).then_inc(s.hi, 1)
                    dve.wait_ge(s.hi, me)
                    nc.vector.tensor_tensor(qh[:, :, 1], y[:], f32(qh[:, :, 0]), ALU.subtract).then_inc(s.lo, 1)

                base_(0, 0, True)
                cut(0, 0, True)
                cut_lo(nc, dve, s, raw, wh, wl, KT)
                for f in range(RT):
                    dve.wait_ge(s.uhi, f + 1)
                    nc.vector.tensor_tensor(ul[:, f], uraw[:, f % 2], f32(uh[:, f]), ALU.subtract).then_inc(s.ulo, 1)
                dve.wait_ge(s.modt, 3)
                dve.wait_ge(s.ropec, 16)

                def pair(i, first, last):
                    for p in range(2):
                        low_rank(i, p, first)
                        if not (last and p == 1):
                            base_(i, p + 1, False)
                            cut(i, p + 1, first and p == 0)
                        heads(i, p, first)
                walk_pairs(dve, pair)


def bias_pad(k, rpb):
    nc = k.nc
    HR = NA_HEADS * RPB_R
    with phase(nc, "pad", "zero rows rowsR wide wideR turned bias") as s, ExitStack() as st:
        rows, rowsR = (st.enter_context(nc.sbuf_tensor(n, [HR, PADW + 1], F32)) for n in ("pad_rows", "pad_rowsR"))
        wide = st.enter_context(nc.sbuf_tensor("pad_wide", [HR, GRID_W * (PADW + 1)], F32))
        wideR = st.enter_context(nc.sbuf_tensor("pad_wideR", [HR, GRID_W * (PADW + 1)], F32))
        turned = st.enter_context(nc.sbuf_tensor("pad_turned", [HR, GRID_W, GRID_W], F32))

        def copies(ap):
            return ap[:].rearrange("r (c j) -> r c j", c=GRID_W)

        def falling(ap):
            return ap[:, GRID_W - 1:GRID_W - 1 + GRID_W * PADW].rearrange("r (c j) -> r c j", c=GRID_W)[:, :, :GRID_W]

        with nc.Block() as block:
            @block.vector
            def _(dve):
                nc.vector.memset(rows[:], 0.0).then_inc(s.zero, 1)
                nc.vector.memset(rowsR[:], 0.0).then_inc(s.zero, 1)
                dve.wait_ge(s.rows, 16)
                nc.vector.tensor_copy(copies(wide), rows[:].unsqueeze(1).to_broadcast([HR, GRID_W, PADW + 1])).then_inc(s.wide, 1)
                dve.wait_ge(s.rowsR, 16 * RPB_R)
                nc.vector.tensor_copy(copies(wideR), rowsR[:].unsqueeze(1).to_broadcast([HR, GRID_W, PADW + 1])).then_inc(s.wideR, 1)
                dve.wait_ge(s.wideR, 1)
                nc.vector.tensor_copy(turned[:], falling(wideR).rearrange("r c j -> r j c")).then_inc(s.turned, 1)

            @block.sync
            def _(sp):
                sp.wait_ge(s.zero, 2)
                mid = (PADW - RPB_C) // 2
                sp.dma_start(rows[:, mid:mid + RPB_C], rpb.rearrange("h r c -> (h r) c")).then_inc(s.rows, 16)
                for r in range(RPB_R):
                    at = (RPB_R - 1 - r) * NA_HEADS
                    sp.dma_start(rowsR[at:at + NA_HEADS, mid:mid + RPB_C], rpb[:, r]).then_inc(s.rowsR, 16)
                sp.wait_ge(s.wide, 1)
                sp.dma_start(k.bias.rearrange("c r k -> r c k"), falling(wide)).then_inc(s.bias, 16)
                sp.wait_ge(s.turned, 1)
                sp.dma_start(k.biasT[:, 0:RPB_R].rearrange("k r h c -> (r h) k c"), turned[:]).then_inc(s.bias, 16)
                sp.wait_ge(s.bias, 32)


class Piece:

    def __init__(self, q, runs, masks=(), bias=None):
        self.q, self.masks, self.bias = q, masks, bias
        self.tiles, self.mm, col = [], [], 0
        for key, n in runs:
            for c in range(0, n, P):
                self.tiles.append(((key + c) // P, min(P, n - c)))
            while n:
                m = min(n, 512 - col % 512)
                if self.mm and self.mm[-1][0] + self.mm[-1][2] == col and self.mm[-1][1] + self.mm[-1][2] == key and col % 512:
                    self.mm[-1] = (self.mm[-1][0], self.mm[-1][1], self.mm[-1][2] + m)
                else:
                    self.mm.append((col, key, m))
                col, key, n = col + m, key + m, n - m
        self.width = col


def window_pieces():
    out = []
    for q in range(LT):
        lo, hi = max(0, q - 1), min(LT, q + 2)
        masks = ([(0, CTX)] if q > 0 else []) + ([(1, CTX + (q + 1 - lo) * P)] if q < LT - 1 else [])
        out.append(Piece(q, [(SEQ, CTX), (lo * P, (hi - lo) * P)], masks=masks))
    return out + [Piece(q, [(SEQ, CTX)]) for q in range(LT, NT)]


def neighbour_pieces():
    out = []
    for q in range(LT):
        rows = [min(max(r - NA_ROWS // 2, 0), 2 * LT - NA_ROWS) for r in (2 * q, 2 * q + 1)]
        n = rows[1] - rows[0] + NA_ROWS
        n += n % 2
        out.append(Piece(q, [(SEQ, CTX), (rows[0] * GRID_W, n * GRID_W)],
                         bias=(rows[0] - 2 * q + NA_ROWS - 1, n, rows[1] > rows[0])))
    return out


def walk(eng, n, body):
    body(0, True, False)
    if n > 2:
        with eng.Fori(1, n - 1) as i:
            body(i, False, False)
    body(n - 1, False, True)


class Step:

    def __init__(self, block, key, q, n, first, last):
        self.block, self.key, self.q, self.n, self.first, self.last = block, key, q, n, first, last


def steps_of_head(pieces):
    seen = [[t for t, _ in u.tiles] for u in pieces]
    out, blocks = [], []
    for b, q0 in enumerate(range(0, len(pieces), 4)):
        tiles = range(q0, min(q0 + 4, len(pieces)))
        blocks.append((q0, len(tiles)))
        for key in [LT] + list(range(LT)) + list(range(LT + 1, NT)):
            qs = [q for q in tiles if key in seen[q]]
            if qs:
                assert qs == list(range(qs[0], qs[-1] + 1))
                out.append(Step(b, key, qs[0], len(qs), key == LT, key == NT - 1))
    return out, blocks


def attend(k, name, pieces, heads, load_head, parts, v_width, mix, mix_col, sink=None, bias=None):
    nc = k.nc
    NQ = len(pieces)
    PAIRS = heads // 2
    BANK = 512
    head_steps, head_blocks = steps_of_head(pieces)
    NS, NB = len(head_steps), len(head_blocks)
    V, NU, BLOCKS = 2 * NS, 2 * NQ, 2 * NB
    PT = 4
    assert V % PT == 0
    wide = max(p.width for p in pieces)
    RB = -(-wide // BANK)
    SB = 2 if RB == 3 else 4
    OB, TB = 6, 7
    loads = load_head(None, None, None, None, None, None)
    last_step = [max(x for x in range(V) if (x // NS) * NB + head_steps[x % NS].block == b) for b in range(BLOCKS)]
    first_step = [0] + [x + 1 for x in last_step[:-1]]
    place = [V] * NU
    for u in 2 * list(reversed(range(NU))):
        b = (u // NQ) * NB + u % NQ // 4
        following = place[u + 1] if u + 1 < NU else place[0] + V
        place[u] = min(first_step[b] - 2, following - max(1, NS // NQ))

    def maxima_at(x):
        return [(n, u) for n in range(2) for u in range(NU) if place[u] + n * V == x]

    def blocks_at(x, later):
        return [(n, b) for n in range(2) for b in range(BLOCKS) if last_step[b] + later == x + n * V]

    def after(later):
        return [b for b in range(BLOCKS) if last_step[b] + later >= V]

    names = "ld0 ld1 st0 st1 tab rt vone R top nm sm dg S ex pv ocp oT es ls ri o mk bl0 bl1 bh bp"
    with phase(nc, name, names) as s, ExitStack() as st:
        def sb(nm, shape, dt=F32):
            return st.enter_context(nc.sbuf_tensor(f"{name}_{nm}", shape, dt))
        rows = MLA_QK if parts == "three" else P
        q_sb = sb("q", [rows, 2, 2 if parts == "three" else 1, TOK], F32R)
        k_sb = sb("k", [rows, 2, 2, TOK], F32R)
        v_sb = sb("v", [P, 2, NT, v_width + 1])
        pt_sb = sb("pt", [P, PT, BANK])
        diag = sb("diag", [P, BLOCKS, 4, P], F32R)
        negmax = sb("nm", [P, BLOCKS, 4], F32R if sink is not None else F32)
        oT_sb = sb("oT", [v_width + 1, 2, BANK])
        top, rowsum = sb("top", [P, 2]), sb("ls", [P, 4])
        o_sb = sb("o", [P, 2, NQ, v_width])
        if sink is not None:
            sinkm, esink = sb("sinkm", [P, BLOCKS, 4]), sb("es", [P, BLOCKS, 4])
            wmask, wband = sb("wm", [P, 2, P], F32R), sb("wb", [P, 3, P], F32R)
            sinks = sb("sinks", [P, heads])
        if bias is not None:
            BR, ND = 2 * NA_ROWS - 2, NA_ROWS - 1
            raw, rawT = sb("br", [P, 2, BR, GRID_W]), sb("brT", [P, 2, ND, P])
            b_sb, bT = sb("b", [P, 2, BR, GRID_W], F32R), sb("bT", [P, 2, 2, ND, P], F32R)
            cmask, cmaskT = sb("cm", [P, GRID_W]), sb("cmT", [P, P])
            rmask = sb("rm", [P, 4, P], F32R)
        mtab = sb("mtab", [P, 5, P]) if sink is not None or bias is not None else None
        tables = 3 if sink is not None or bias is not None else 0

        def rough_scores():
            return k.ps[:, 0:RB].rearrange("p b c -> p (b c)")

        def scores(x):
            return k.ps[:, RB + x % SB]

        def nth(i, x):
            return i * V + x + 1

        def unit_nth(i, u):
            return i * NU + u + 1

        def block_nth(i, b):
            return i * BLOCKS + b + 1

        def rough_added(p, u):
            out = [(c, P, wmask[:, m]) for m, c in u.masks]
            if u.bias:
                e0, n, edge = u.bias
                flat = b_sb[:, p].rearrange("p e c -> p (e c)")
                c, end = CTX, CTX + n * GRID_W
                while c < end:
                    w = min(end - c, BANK - c % BANK)
                    at = (e0 - 1) * GRID_W + c - CTX
                    out.append((c, w, flat[:, at:at + w]))
                    c += w
                if edge:
                    out += [(CTX, P, rmask[:, 0]), (end - P, P, rmask[:, 1])]
            return out

        def added(p, t):
            out = []
            if t.key < LT and sink is not None:
                e = t.q - t.key + 1
                out.append((t.q, t.n, wband[:, e:e + t.n].rearrange("p e q -> p (e q)")))
            if t.key < LT and bias is not None:
                e = t.q - t.key + ND // 2
                for part in range(2):
                    out.append((t.q, t.n, bT[:, p, part, e:e + t.n].rearrange("p e q -> p (e q)")))
                for q in range(t.q, t.q + t.n):
                    if pieces[q].bias[2] and abs(t.key - q) == 2:
                        out.append((q, 1, rmask[:, 2 if t.key < q else 3]))
            return out

        with nc.Block() as block:
            @block.sync
            def _(sp):
                if sink is not None:
                    sp.dma_start(mtab[:, 0:2], k.ins["wmask"]).then_inc(s.tab, 16)
                    sp.dma_start(mtab[:, 2:5], k.ins["wband"]).then_inc(s.tab, 16)
                    sp.dma_start(sinks[:], sink.unsqueeze(0).broadcast_to([P, heads])).then_inc(s.tab, 16)
                if bias is not None:
                    sp.dma_start(cmask[:], k.ins["cmask"]).then_inc(s.tab, 16)
                    sp.dma_start(cmaskT[:], k.ins["cmaskT"]).then_inc(s.tab, 16)
                    sp.dma_start(mtab[:, 0:4], k.ins["rmask"]).then_inc(s.tab, 16)

                def fetch(i, p, free):
                    if bias is not None:
                        if free:
                            wait_then_store(sp, s.bp, (i - 1) * 2 + p + 1, s.mk)
                        bias(sp, i, p, raw[:, p], rawT[:, p], s.bl0 if p == 0 else s.bl1)
                    if free:
                        wait_then_store(sp, s.pv, (i - 1) * V + (p + 1) * NS, s.mk)
                    load_head(sp, i, p, (q_sb[:, p], k_sb[:, p], v_sb[:, p, :, 0:v_width]), None, s.ld0 if p == 0 else s.ld1)

                def pair(i, first, last):
                    if first:
                        fetch(0, 0, False)
                        fetch(0, 1, False)
                    for p in range(2):
                        if not last:
                            fetch(i + 1, p, True)
                        wait_then_store(sp, s.o, i * BLOCKS + (p + 1) * NB, s.mk)
                        dst = mix.rearrange("(t p) d -> p t d", p=P)[:, 0:NQ, bass.ds((i * 2 + p) * v_width + mix_col, v_width)]
                        sp.dma_start(dst, o_sb[:, p]).then_inc(s.st0 if p == 0 else s.st1, 16)
                walk(sp, PAIRS, pair)
                sp.wait_ge(s.st0, 16 * PAIRS)
                sp.wait_ge(s.st1, 16 * PAIRS)

            @block.tensor
            def _(pe):
                if tables:
                    pe.wait_ge(s.rt, 1 if sink is None else 2)
                pe.wait_ge(s.vone, 1)

                def rough(i, u, free):
                    p, piece = u // NQ, pieces[u % NQ]
                    if u % NQ == 0:
                        pe.wait_ge(s.ld0 if p == 0 else s.ld1, i * 16 * loads + 16 * loads)
                        if bias is not None:
                            pe.wait_ge(s.bp, i * 2 + p + 1)
                    if free:
                        pe.wait_ge(s.top, unit_nth(i, u - 1))
                    for c, key, n in piece.mm:
                        more = [m for m in rough_added(p, piece) if c <= m[0] < c + n]
                        mm = pe.matmul(rough_scores()[:, c:c + n], q_sb[:, p, 0, piece.q * P:(piece.q + 1) * P],
                                       k_sb[:, p, 0, key:key + n], start=True, stop=not more)
                        for y, (col, w, addend) in enumerate(more):
                            mm = pe.matmul(rough_scores()[:, col:col + w], k.identr[:], addend, start=False, stop=(y == len(more) - 1))
                    mm.then_inc(s.R, 1)

                def score(i, x, first):
                    p, t = x // NS, head_steps[x % NS]
                    b = p * NB + t.block
                    q0, nq = head_blocks[t.block]
                    out = scores(x)[:, 0:t.n * P]
                    prods = ((0, 0), (1, 0), (0, 1)) if parts == "three" else ((0, 0), (1, 0))
                    if not (first and x < SB):
                        pe.wait_ge(s.ex, nth(i, x - SB))
                    for y, (kp, qp) in enumerate(prods):
                        pe.matmul(out, k_sb[:, p, kp, t.key * P:(t.key + 1) * P], q_sb[:, p, qp, t.q * P:(t.q + t.n) * P],
                                  start=(y == 0), stop=False)
                    for q, n, addend in added(p, t):
                        pe.matmul(scores(x)[:, (q - t.q) * P:(q - t.q + n) * P], k.identr[:], addend, start=False, stop=False)
                    if t.first:
                        pe.wait_ge(s.dg, unit_nth(i, p * NQ + q0 + nq - 1))
                    pe.matmul(out, k.onesr[:], diag[:, b, t.q - q0:t.q - q0 + t.n].rearrange("p e q -> p (e q)"),
                              start=False, stop=True).then_inc(s.S, 1)

                def values(i, x, first):
                    x = x % V
                    p, t = x // NS, head_steps[x % NS]
                    b = p * NB + t.block
                    q0 = head_blocks[t.block][0]
                    pe.wait_ge(s.ex, nth(i, x))
                    if t.first and not (first and b == 0):
                        pe.wait_ge(s.ocp, block_nth(i, b - 1))
                    pe.matmul(k.ps[0:v_width + 1, OB, (t.q - q0) * P:(t.q - q0 + t.n) * P], v_sb[:, p, t.key],
                              pt_sb[:, x % PT, 0:t.n * P], start=t.first, stop=t.last).then_inc(s.pv, 1)

                def turn(i, b, first):
                    pe.wait_ge(s.ocp, block_nth(i, b))
                    if not (first and b == 0):
                        pe.wait_ge(s.o, block_nth(i, b - 1))
                    for j in range(head_blocks[b % NB][1]):
                        mm = pe.transpose(k.ps[:, TB, j * P:j * P + v_width + 1], oT_sb[:, b % 2, j * P:(j + 1) * P],
                                          k.ident[0:v_width + 1, 0:v_width + 1])
                    mm.then_inc(s.oT, 1)

                def pair(i, first, last):
                    for x in range(V):
                        if first and x == 0:
                            for u in range(NU):
                                if place[u] < 0:
                                    rough(0, u, u > 0)
                        score(i, x, first)
                        for n, u in maxima_at(x):
                            if not (last and n):
                                rough(i + n, u, True)
                        for n, b in blocks_at(x, 3):
                            if not (first and n):
                                turn(i - n, b, first)
                        if not (first and x < 2):
                            values(i - 1 if x < 2 else i, x - 2, first)
                walk(pe, PAIRS, pair)
                values(PAIRS - 1, V - 2, False)
                values(PAIRS - 1, V - 1, False)
                for b in after(3):
                    turn(PAIRS - 1, b, False)

            @block.scalar
            def _(act):
                def sink_exp(i, b):
                    act.wait_ge(s.sm, block_nth(i, b))
                    n = head_blocks[b % NB][1]
                    nc.scalar.activation(esink[:, b, 0:n], sinkm[:, b, 0:n], ACT.Exp).then_inc(s.es, 1)

                def exps(i, x, first):
                    t = head_steps[x % NS]
                    act.wait_ge(s.S, nth(i, x))
                    if not (first and x < PT):
                        act.wait_ge(s.pv, nth(i, x - PT))
                    nc.scalar.activation(pt_sb[:, x % PT, 0:t.n * P], scores(x)[:, 0:t.n * P], ACT.Exp).then_inc(s.ex, 1)

                def take_sums(i, b, first):
                    act.wait_ge(s.pv, nth(i, last_step[b]))
                    if not (first and b < 2):
                        act.wait_ge(s.oT, block_nth(i, b - 2))
                    n = head_blocks[b % NB][1] * P
                    nc.scalar.copy(oT_sb[:, b % 2, 0:n], k.ps[0:v_width + 1, OB, 0:n]).then_inc(s.ocp, 1)

                def pair(i, first, last):
                    for x in range(V):
                        if sink is not None and x in first_step:
                            sink_exp(i, first_step.index(x))
                        exps(i, x, first)
                        for n, b in blocks_at(x, 2):
                            if not (first and n):
                                take_sums(i - n, b, first and not n)
                walk(act, PAIRS, pair)
                for b in after(2):
                    take_sums(PAIRS - 1, b, False)

            @block.vector
            def _(dve):
                nc.vector.memset(v_sb[:, :, :, v_width:], 1.0).then_inc(s.vone, 1)
                if tables:
                    dve.wait_ge(s.tab, 16 * tables)
                if sink is not None:
                    nc.vector.tensor_copy(wmask[:], mtab[:, 0:2]).then_inc(s.rt, 1)
                    nc.vector.tensor_copy(wband[:], mtab[:, 2:5]).then_inc(s.rt, 1)
                if bias is not None:
                    nc.vector.tensor_copy(rmask[:], mtab[:, 0:4]).then_inc(s.rt, 1)

                def head_bias(i, p, free):
                    dve.wait_ge(s.bl0 if p == 0 else s.bl1, i * 6 * 16 + 6 * 16)
                    if free:
                        dve.wait_ge(s.S, nth(i - 1, (p + 1) * NS - 1))
                    nc.vector.tensor_tensor(b_sb[:, p], raw[:, p], cmask[:].unsqueeze(1).broadcast_to([P, BR, GRID_W]), ALU.add)
                    nc.vector.tensor_tensor(rawT[:, p], rawT[:, p], cmaskT[:].unsqueeze(1).broadcast_to([P, ND, P]),
                                            ALU.add).then_inc(s.bh, 1)
                    dve.wait_ge(s.bh, i * 4 + 2 * p + 1)
                    nc.vector.tensor_copy(bT[:, p, 0], rawT[:, p]).then_inc(s.bh, 1)
                    dve.wait_ge(s.bh, i * 4 + 2 * p + 2)
                    nc.vector.tensor_tensor(bT[:, p, 1], rawT[:, p], f32(bT[:, p, 0]), ALU.subtract).then_inc(s.bp, 1)

                def maximum(i, u, first):
                    p, q = u // NQ, u % NQ
                    b, j = p * NB + q // 4, q % 4
                    if bias is not None and q == 0:
                        head_bias(i, p, not first)
                    dve.wait_ge(s.R, unit_nth(i, u))
                    here, m = rough_scores()[:, 0:pieces[q].width], negmax[:, b, j:j + 1]
                    if sink is not None:
                        nc.vector.tensor_reduce(top[:, u % 2:u % 2 + 1], here, AX.X, ALU.max).then_inc(s.top, 1)
                        dve.wait_ge(s.top, unit_nth(i, u))
                        nc.vector.tensor_scalar(m, top[:, u % 2:u % 2 + 1], sinks[:, bass.ds(i * 2 + p, 1)], -1.0,
                                                ALU.max, ALU.mult).then_inc(s.nm, 1)
                        dve.wait_ge(s.nm, unit_nth(i, u))
                    else:
                        nc.vector.tensor_reduce(m, here, AX.X, ALU.max, negate=True).then_inc(s.top, 1)
                        dve.wait_ge(s.top, unit_nth(i, u))
                    if not first:
                        dve.wait_ge(s.S, nth(i - 1, last_step[b]))
                    nc.vector.tensor_scalar(diag[:, b, j], k.ident[:], f32(m), None, ALU.mult).then_inc(s.dg, 1)
                    n = head_blocks[b % NB][1]
                    if sink is not None and j == n - 1:
                        if not first:
                            dve.wait_ge(s.es, block_nth(i - 1, b))
                        nc.vector.tensor_scalar(sinkm[:, b, 0:n], f32(negmax[:, b, 0:n]), sinks[:, bass.ds(i * 2 + p, 1)], None,
                                                ALU.add).then_inc(s.sm, 1)

                def result(i, b, first):
                    p, (q0, n) = b // NB, head_blocks[b % NB]
                    me = block_nth(i, b)
                    turned = k.ps[:, TB].rearrange("p (j c) -> p j c", c=P)[:, 0:n]
                    dve.wait_ge(s.oT, me)
                    total = turned[:, :, v_width]
                    if sink is not None:
                        dve.wait_ge(s.es, me)
                        nc.vector.tensor_tensor(rowsum[:, 0:n], total, esink[:, b, 0:n], ALU.add).then_inc(s.ls, 1)
                        dve.wait_ge(s.ls, me)
                        total = rowsum[:, 0:n]
                    nc.vector.reciprocal(rowsum[:, 0:n], total).then_inc(s.ri, 1)
                    dve.wait_ge(s.ri, me)
                    if not first and b % NB == 0:
                        dve.wait_ge(s.st0 if p == 0 else s.st1, i * 16)
                    nc.vector.tensor_tensor(o_sb[:, p, q0:q0 + n], turned[:, :, 0:v_width],
                                            rowsum[:, 0:n].unsqueeze(2).broadcast_to([P, n, v_width]), ALU.mult).then_inc(s.o, 1)

                def pair(i, first, last):
                    for x in range(V):
                        if first and x == 0:
                            for u in range(NU):
                                if place[u] < 0:
                                    maximum(0, u, True)
                        for n, u in maxima_at(x):
                            if not (last and n):
                                maximum(i + n, u, first and not n)
                        for n, b in blocks_at(x, 3):
                            if not (first and n):
                                result(i - n, b, first)
                walk(dve, PAIRS, pair)
                for b in after(3):
                    result(PAIRS - 1, b, False)


def stacked_loader(qk, q_base, k_index, v_dram, v_index, v_width):
    def load(sp, i, p, places, _, sem):
        if sp is None:
            return 6
        q_sb, k_sb, v_sb = places
        h, kh, vh = i * 2 + p, k_index(i, p), v_index(i, p)
        one = lambda x: qk[bass.ds(x, 1)].squeeze(0)
        sp.dma_start(f32(q_sb[:, 0]), one(h + q_base)).then_inc(sem, 16)
        for part in range(2):
            for half in range(2):
                sp.dma_start(f32(k_sb[half * HD:(half + 1) * HD, part]), one(kh)[part * HD:(part + 1) * HD]).then_inc(sem, 16)
        sp.dma_start(v_sb, v_dram.rearrange("(t p) d -> p t d", p=P)[:, :, bass.ds(vh * v_width, v_width)]).then_inc(sem, 16)
    return load


def parts_loader(k):
    def load(sp, i, p, places, _, sem):
        if sp is None:
            return 3
        q_sb, k_sb, v_sb = places
        h = i * 2 + p
        one = lambda x: k.qkC[bass.ds(x, 1)].squeeze(0).rearrange("a r q -> r a q")
        sp.dma_start(f32(q_sb), one(h)).then_inc(sem, 16)
        sp.dma_start(f32(k_sb), one(h + MLA_HEADS)).then_inc(sem, 16)
        sp.dma_start(v_sb, k.vC.rearrange("(t p) d -> p t d", p=P)[:, :, bass.ds(h * MLA_V, MLA_V)]).then_inc(sem, 16)
    return load


def bias_loader(k):
    def load(sp, i, p, place, placeT, sem):
        first_row = (i * 2 + p) * RPB_R + 1
        for q in range(2):
            sp.dma_start(place[q * GRID_W:(q + 1) * GRID_W],
                         k.bias[:, bass.ds(first_row - q, 2 * NA_ROWS - 2)]).then_inc(sem, 16)
            for key in range(2):
                first = 1 + q - key
                rows = k.biasT[:, first:first + 2 * NA_ROWS - 2].rearrange("k (d two) h c -> k d two h c", two=2)[:, :, 0]
                sp.dma_start(placeT[key * GRID_W:(key + 1) * GRID_W, :, q * GRID_W:(q + 1) * GRID_W],
                             rows[:, :, bass.ds(i * 2 + p, 1)].squeeze(2)).then_inc(sem, 16)
    return load


def attend_diff(k, name, ins):
    nc = k.nc
    pieces = [Piece(q, [(0, TOK)]) for q in range(LT)] + [Piece(q, [(SEQ, CTX)]) for q in range(LT, NT)]
    NQ, V, PAIRS, DV = NT, 2 * NT, DIFF_HEADS // 2, 2 * HD
    names = "ld0 ld1 lam lp lr le l1 nl S mx ex r1 c mix T evA evD pv r0 o st0 st1"
    with phase(nc, name, names) as s, ExitStack() as st:
        def sb(nm, shape, dt=F32):
            return st.enter_context(nc.sbuf_tensor(f"{name}_{nm}", shape, dt))
        q_sb = sb("q", [P, 2, 2, TOK], F32R)
        k_sb = sb("k", [P, 2, 2, 2, TOK], F32R)
        v_sb = sb("v", [P, 2, NT, DV])
        e_sb = sb("e", [P, 2, 2, TOK])
        pt_sb = sb("pt", [P, 2, NT, P])
        negmax = sb("nm", [P, 2, 2])
        rowsum = sb("ls", [P, 4, 2])
        r1, coef, r0 = sb("r1", [P, 2]), sb("c", [P, 2]), sb("r0", [P, 2])
        o_sb = sb("o", [P, 2, NQ, DV])
        lam4, lprod, lsum, nlam = sb("lam4", [P, 4, HD]), sb("lprod", [P, 2, HD]), sb("lsum", [P, 2]), sb("nlam", [P, 1])
        OB = 6

        def scores(b):
            return k.ps[:, 3 * b:3 * b + 3].rearrange("p b c -> p (b c)")

        def nth(i, v):
            return i * V + v + 1

        def map_nth(i, v, m):
            return (i * V + v) * 2 + m + 1

        with nc.Block() as block:
            @block.sync
            def _(sp):
                sp.dma_start(lam4[:], ins["diff_lam"][0].unsqueeze(0).broadcast_to([P, 4, HD])).then_inc(s.lam, 16)

                def fetch(i, p):
                    sem = s.ld0 if p == 0 else s.ld1
                    hd = i * 2 + p
                    for m in range(2):
                        sp.dma_start(f32(q_sb[:, p, m]), k.qkA[hd * 2 + m]).then_inc(sem, 16)
                        for part in range(2):
                            for half in range(2):
                                sp.dma_start(f32(k_sb[half * HD:(half + 1) * HD, p, m, part]),
                                             k.qkA[8 + hd * 2 + m, part * HD:(part + 1) * HD]).then_inc(sem, 16)
                    sp.dma_start(v_sb[:, p], k.vA.rearrange("(t p) d -> p t d", p=P)[:, :, hd * DV:(hd + 1) * DV]).then_inc(sem, 16)

                fetch(0, 0)
                fetch(0, 1)
                for i in range(PAIRS):
                    for p in range(2):
                        sp.wait_ge(s.o, i * V + (p + 1) * NQ)
                        if i + 1 < PAIRS:
                            fetch(i + 1, p)
                        dst = k.mix[0].rearrange("(t p) d -> p t d", p=P)[:, :, (i * 2 + p) * DV:(i * 2 + p + 1) * DV]
                        sp.dma_start(dst, o_sb[:, p]).then_inc(s.st0 if p == 0 else s.st1, 16)
                sp.wait_ge(s.st0, 16 * PAIRS)
                sp.wait_ge(s.st1, 16 * PAIRS)

            @block.tensor
            def _(pe):
                def score(i, v, m):
                    i, v = i + v // V, v % V
                    p, u = v // NQ, pieces[v % NQ]
                    if v % NQ == 0 and m == 0:
                        pe.wait_ge(s.ld0 if p == 0 else s.ld1, (i + 1) * 16 * 11)
                    if i or v:
                        if m == 0:
                            pe.wait_ge(s.ex, map_nth(i, v - 1, 0))
                        else:
                            pe.wait_ge(s.evA, nth(i, v - 1))
                            pe.wait_ge(s.evD, nth(i, v - 1))
                    for c, key, n in u.mm:
                        for x in range(2):
                            mm = pe.matmul(scores(m)[:, c:c + n], q_sb[:, p, m, u.q * P:(u.q + 1) * P],
                                           k_sb[:, p, m, x, key:key + n], start=(x == 0), stop=(x == 1))
                    mm.then_inc(s.S, 1)

                def turn(i, v):
                    u = pieces[v % NQ]
                    pe.wait_ge(s.mix, nth(i, v))
                    for x in range(len(u.tiles)):
                        mm = pe.transpose(scores(1)[:, x * P:(x + 1) * P], e_sb[:, v % 2, 0, x * P:(x + 1) * P], k.ident[:])
                    mm.then_inc(s.T, 1)

                def values(i, v):
                    u = pieces[v % NQ]
                    pe.wait_ge(s.evA, nth(i, v))
                    pe.wait_ge(s.evD, nth(i, v))
                    if i or v >= 2:
                        pe.wait_ge(s.o, nth(i, v - 2))
                    for x, (t, n) in enumerate(u.tiles):
                        mm = pe.matmul(k.ps[:, OB + v % 2, 0:DV], pt_sb[:, v % 2, x], v_sb[:, v // NQ, t],
                                       start=(x == 0), stop=(x == len(u.tiles) - 1))
                    mm.then_inc(s.pv, 1)

                score(0, 0, 0)
                score(0, 0, 1)
                for i in range(PAIRS):
                    for v in range(V):
                        more = (i, v) != (PAIRS - 1, V - 1)
                        if more:
                            score(i, v + 1, 0)
                        turn(i, v)
                        if more:
                            score(i, v + 1, 1)
                        values(i, v)

            @block.scalar
            def _(act):
                act.wait_ge(s.lr, 1)
                nc.scalar.activation(lsum[:], lsum[:], ACT.Exp).then_inc(s.le, 1)

                def exps(i, v, m):
                    i, v = i + v // V, v % V
                    act.wait_ge(s.mx, map_nth(i, v, m))
                    w = pieces[v % NQ].width
                    nc.scalar.activation(e_sb[:, v % 2, m, 0:w], scores(m)[:, 0:w], ACT.Exp, bias=negmax[:, v % 2, m:m + 1],
                                         accum_out=rowsum[:, v % 4, m:m + 1]).then_inc(s.ex, 1)

                def evacuate(i, v):
                    u, b = pieces[v % NQ], v % 2
                    act.wait_ge(s.T, nth(i, v))
                    if i or v >= 2:
                        act.wait_ge(s.pv, nth(i, v - 2))
                    nt = len(u.tiles)
                    if nt <= 4:
                        ins = nc.scalar.copy(pt_sb[64:P, b, 0:nt], scores(1)[64:P, 0:nt * P].rearrange("p (t q) -> p t q", q=P))
                    else:
                        ins = nc.scalar.copy(pt_sb[:, b, 4:nt], scores(1)[:, 512:nt * P].rearrange("p (t q) -> p t q", q=P))
                    ins.then_inc(s.evA, 1)

                exps(0, 0, 0)
                exps(0, 0, 1)
                for i in range(PAIRS):
                    for v in range(V):
                        evacuate(i, v)
                        if (i, v) != (PAIRS - 1, V - 1):
                            exps(i, v + 1, 0)
                            exps(i, v + 1, 1)

            @block.vector
            def _(dve):
                dve.wait_ge(s.lam, 16)
                nc.vector.tensor_tensor(lprod[:], lam4[:, 0:4:2], lam4[:, 1:4:2], ALU.mult).then_inc(s.lp, 1)
                dve.wait_ge(s.lp, 1)
                nc.vector.tensor_reduce(lsum[:], lprod[:], AX.X, ALU.add).then_inc(s.lr, 1)
                dve.wait_ge(s.le, 1)
                nc.vector.tensor_tensor(nlam[:], lsum[:, 1:2], lsum[:, 0:1], ALU.subtract).then_inc(s.l1, 1)
                dve.wait_ge(s.l1, 1)
                nc.vector.tensor_scalar(nlam[:], nlam[:], -LAM_INIT, None, ALU.add).then_inc(s.nl, 1)
                dve.wait_ge(s.nl, 1)

                def maxima(i, v, m):
                    i, v = i + v // V, v % V
                    dve.wait_ge(s.S, map_nth(i, v, m))
                    nc.vector.tensor_reduce(negmax[:, v % 2, m:m + 1], scores(m)[:, 0:pieces[v % NQ].width], AX.X, ALU.max,
                                            negate=True).then_inc(s.mx, 1)

                def mixed(i, v):
                    b, w = v % 2, pieces[v % NQ].width
                    dve.wait_ge(s.ex, map_nth(i, v, 1))
                    nc.vector.reciprocal(r1[:, b:b + 1], rowsum[:, v % 4, 1:2]).then_inc(s.r1, 1)
                    dve.wait_ge(s.r1, nth(i, v))
                    nc.vector.tensor_scalar(coef[:, b:b + 1], rowsum[:, v % 4, 0:1], r1[:, b:b + 1], nlam[:, 0:1],
                                            ALU.mult, ALU.mult).then_inc(s.c, 1)
                    dve.wait_ge(s.c, nth(i, v))
                    nc.vector.scalar_tensor_tensor(out=e_sb[:, b, 0, 0:w], in0=e_sb[:, b, 1, 0:w], scalar=coef[:, b:b + 1],
                                                   in1=e_sb[:, b, 0, 0:w], op0=ALU.mult, op1=ALU.add).then_inc(s.mix, 1)

                def evacuate(i, v):
                    u, b = pieces[v % NQ], v % 2
                    dve.wait_ge(s.T, nth(i, v))
                    if i or v >= 2:
                        dve.wait_ge(s.pv, nth(i, v - 2))
                    nt = len(u.tiles)
                    if nt <= 4:
                        ins = nc.vector.tensor_copy(pt_sb[0:64, b, 0:nt], scores(1)[0:64, 0:nt * P].rearrange("p (t q) -> p t q", q=P))
                    else:
                        ins = nc.vector.tensor_copy(pt_sb[:, b, 0:4], scores(1)[:, 0:512].rearrange("p (t q) -> p t q", q=P))
                    ins.then_inc(s.evD, 1)

                def result(i, v):
                    b, p = v % 2, v // NQ
                    nc.vector.reciprocal(r0[:, b:b + 1], rowsum[:, v % 4, 0:1]).then_inc(s.r0, 1)
                    dve.wait_ge(s.r0, nth(i, v))
                    dve.wait_ge(s.pv, nth(i, v))
                    if i and v % NQ == 0:
                        dve.wait_ge(s.st0 if p == 0 else s.st1, i * 16)
                    nc.vector.tensor_scalar(o_sb[:, p, v % NQ], k.ps[:, OB + b, 0:DV], r0[:, b:b + 1], None,
                                            ALU.mult).then_inc(s.o, 1)

                maxima(0, 0, 0)
                maxima(0, 0, 1)
                for i in range(PAIRS):
                    for v in range(V):
                        more = (i, v) != (PAIRS - 1, V - 1)
                        mixed(i, v)
                        if more:
                            maxima(i, v + 1, 0)
                        evacuate(i, v)
                        if v:
                            result(i, v - 1)
                        elif i:
                            result(i - 1, V - 1)
                        if more:
                            maxima(i, v + 1, 1)
                result(PAIRS - 1, V - 1)


def out_project(k, name, layer, n_tok, w_out, subln=None):
    nc = k.nc
    nt = n_tok // P
    chunks = token_chunks(n_tok)
    SB = len(chunks)
    names = "in0 in1 g sqa red root ri ya yb T hi lo wr0 wr1 whi wlo mm x g2"
    with phase(nc, name, names) as s, ExitStack() as st:
        def sb(nm, shape, dt=F32):
            return st.enter_context(nc.sbuf_tensor(f"{name}_{nm}", shape, dt))
        rows = sb("rows", [P, 2, D_MODEL])
        oh, ol = sb("oh", [P, KT, n_tok], F32R), sb("ol", [P, KT, n_tok], F32R)
        raw = sb("raw", [P, 2, KT, P])
        wh, wl = sb("wh", [P, 2, KT, P], F32R), sb("wl", [P, 2, KT, P], F32R)
        if subln is not None:
            sq, rs, gain = sb("sq", [P, 512]), sb("rs", [P, 2, DIFF_HEADS]), sb("gain", [P, P])
        w_dram = w_out.rearrange("(f p) (n c) -> n p f c", p=P, c=P)

        with nc.Block() as block:
            @block.sync
            def _(sp):
                if subln is not None:
                    sp.dma_start(gain[:], subln.unsqueeze(0).broadcast_to([P, P])).then_inc(s.g, 16)
                for t in range(nt):
                    if t >= 2:
                        sp.wait_ge(s.T, t - 1)
                    sp.dma_start(rows[:, t % 2], k.mix[layer][t * P:(t + 1) * P]).then_inc(s.in0 if t % 2 == 0 else s.in1, 16)

                def pair(i, first, last):
                    for p in range(2):
                        if not first:
                            wait_then_store(sp, s.wlo, i * 2 + p - 1, s.g2)
                        sp.dma_start(raw[:, p], w_dram[bass.ds(i * 2 + p, 1)].squeeze(0)).then_inc(s.wr0 if p == 0 else s.wr1, 16)
                walk(sp, KT // 2, pair)

            @block.tensor
            def _(pe):
                for t in range(nt):
                    if subln is None:
                        pe.wait_ge(s.in0 if t % 2 == 0 else s.in1, 16 * (t // 2 + 1))
                    else:
                        pe.wait_ge(s.yb, t + 1)
                    if t >= 3:
                        pe.wait_ge(s.lo, t - 2)
                    for f in range(KT):
                        mm = pe.transpose(k.ps[:, 2 * (t % 3) + f // 4, (f % 4) * P:(f % 4 + 1) * P],
                                          rows[:, t % 2, f * P:(f + 1) * P], k.ident[:])
                    mm.then_inc(s.T, 1)

                def pair(i, first, last):
                    for p in range(2):
                        if first and p == 0:
                            pe.wait_ge(s.lo, nt)
                        pe.wait_ge(s.wlo, i * 2 + p + 1)
                        if not first:
                            pe.wait_ge(s.x, i * 2 + p - 1)
                        for f in range(KT):
                            for x, (w, o) in enumerate(((wh, oh), (wh, ol), (wl, oh))):
                                for c, (c0, n) in enumerate(chunks):
                                    mm = pe.matmul(k.ps[:, SB * p + c, 0:n], w[:, p, f], o[:, f, c0:c0 + n],
                                                   start=(f == 0 and x == 0), stop=(f == KT - 1 and x == 2))
                        mm.then_inc(s.mm, 1)
                walk(pe, KT // 2, pair)

            @block.scalar
            def _(act):
                for t in range(nt):
                    if subln is not None:
                        act.wait_ge(s.in0 if t % 2 == 0 else s.in1, 16 * (t // 2 + 1))
                        if t:
                            act.wait_ge(s.red, t)
                        nc.scalar.activation(sq[:], rows[:, t % 2, 0:512], ACT.Square).then_inc(s.sqa, 1)
                        act.wait_ge(s.red, t + 1)
                        nc.scalar.activation(rs[:, t % 2], rs[:, t % 2], ACT.Sqrt, bias=k.eps[:], scale=1.0 / P).then_inc(s.root, 1)
                    act.wait_ge(s.T, t + 1)
                    nc.scalar.copy(oh[:, :, t * P:(t + 1) * P],
                                   k.ps[:, 2 * (t % 3):2 * (t % 3) + 2].rearrange("p b (f q) -> p (b f) q", q=P)).then_inc(s.hi, 1)

                def pair(i, first, last):
                    for p in range(2):
                        act.wait_ge(s.wr0 if p == 0 else s.wr1, i * 16 + 16)
                        if not first:
                            act.wait_ge(s.mm, i * 2 + p - 1)
                        nc.scalar.copy(wh[:, p], raw[:, p]).then_inc(s.whi, 1)
                walk(act, KT // 2, pair)

            @block.vector
            def _(dve):
                if subln is not None:
                    dve.wait_ge(s.g, 16)
                    nc.vector.tensor_scalar(gain[:], gain[:], 1.0 - LAM_INIT, None, ALU.mult).then_inc(s.ya, 1)
                    dve.wait_ge(s.ya, 1)

                def norm(t):
                    heads = lambda ap: ap.rearrange("p (h d) -> p h d", d=P)
                    r = rows[:, t % 2, 0:512]
                    dve.wait_ge(s.sqa, t + 1)
                    nc.vector.tensor_reduce(rs[:, t % 2], heads(sq[:]), AX.X, ALU.add).then_inc(s.red, 1)
                    dve.wait_ge(s.root, t + 1)
                    nc.vector.reciprocal(rs[:, t % 2], rs[:, t % 2]).then_inc(s.ri, 1)
                    dve.wait_ge(s.ri, t + 1)
                    nc.vector.tensor_tensor(heads(r), heads(r), rs[:, t % 2].unsqueeze(2).broadcast_to([P, DIFF_HEADS, P]),
                                            ALU.mult).then_inc(s.ya, 1)
                    dve.wait_ge(s.ya, t + 2)
                    nc.vector.tensor_tensor(heads(r), heads(r), gain[:].unsqueeze(1).broadcast_to([P, DIFF_HEADS, P]),
                                            ALU.mult).then_inc(s.yb, 1)

                def lo(t):
                    dve.wait_ge(s.hi, t + 1)
                    q = slice(t * P, (t + 1) * P)
                    nc.vector.tensor_tensor(ol[:, :, q], k.ps[:, 2 * (t % 3):2 * (t % 3) + 2].rearrange("p b (f q) -> p (b f) q", q=P),
                                            f32(oh[:, :, q]), ALU.subtract).then_inc(s.lo, 1)

                for t in range(nt):
                    if subln is not None:
                        norm(t)
                    if t:
                        lo(t - 1)
                lo(nt - 1)

                def cut(i, p):
                    dve.wait_ge(s.whi, i * 2 + p + 1)
                    nc.vector.tensor_tensor(wl[:, p], raw[:, p], f32(wh[:, p]), ALU.subtract).then_inc(s.wlo, 1)

                def add(i, p):
                    dve.wait_ge(s.mm, i * 2 + p + 1)
                    add_gated(k, dve, layer, 2, i * 2 + p, SB * p, n_tok).then_inc(s.x, 1)

                def pair(i, first, last):
                    if first:
                        cut(0, 0)
                    cut(i, 1)
                    add(i, 0)
                    if not last:
                        cut(i + 1, 0)
                    add(i, 1)
                walk(dve, KT // 2, pair)


def add_gated(k, dve, layer, gate, n, bank, n_tok):
    for w, a, b in ((0, 0, SEQ), (1, SEQ, n_tok)):
        if b > a:
            x = k.xT[:, bass.ds(n, 1), a:b].squeeze(1)
            ps = k.ps[:, bank:bank + (n_tok + 511) // 512].rearrange("p b c -> p (b c)")[:, a:b]
            ins = k.nc.vector.scalar_tensor_tensor(out=x, in0=ps, scalar=k.mods[:, layer, gate, bass.ds(n, 1), w], in1=x,
                                                   op0=ALU.mult, op1=ALU.add)
    return ins


def mlp(k, name, layer, n_tok, w1, w2):
    nc = k.nc
    chunks = token_chunks(n_tok)
    SB = len(chunks)
    C, F, U = FF // FFC, FFC // P, FFC // P + KT
    names = "f fm hh h wr0 wr1 whi wlo mm relu sq gh g x tick"
    with phase(nc, name, names) as s, ExitStack() as st:
        def sb(nm, shape, dt=F32):
            return st.enter_context(nc.sbuf_tensor(f"{name}_{nm}", shape, dt))
        hh, hl = sb("hh", [P, KT, n_tok], F32R), sb("hl", [P, KT, n_tok], F32R)
        gh, gl = sb("gh", [P, F, n_tok], F32R), sb("gl", [P, F, n_tok], F32R)
        g = sb("g", [P, n_tok])
        raw = sb("raw", [P, 2, KT, P])
        w1h, w1l = sb("w1h", [P, 2, KT, P], F32R), sb("w1l", [P, 2, KT, P], F32R)
        w2h, w2l = sb("w2h", [P, 2, F, P], F32R), sb("w2l", [P, 2, F, P], F32R)
        w1_dram = w1.rearrange("(f p) (c n q) -> c n p f q", p=P, n=F, q=P)
        w2_dram = w2.rearrange("(c f p) (n q) -> c n p f q", f=F, p=P, q=P)

        def nth(c, e):
            return c * U + e + 1

        def places(e):
            return (w1h, w1l, KT) if e % U < F else (w2h, w2l, F)

        def waits_for(e):
            return e - 2 if (e >= F + 2 or 2 <= e < F) else e - U + (F - 2 if e < F else KT - 2)

        with nc.Block() as block:
            @block.sync
            def _(sp):
                def chunk(c, first, last):
                    for e in range(U):
                        if not (first and e < 2):
                            wait_then_store(sp, s.wlo, nth(c, e - 2), s.tick)
                        src = w1_dram[bass.ds(c, 1), e].squeeze(0) if e < F else w2_dram[bass.ds(c, 1), e - F].squeeze(0)
                        sp.dma_start(raw[:, e % 2, 0:places(e)[2]], src).then_inc(s.wr0 if e % 2 == 0 else s.wr1, 16)
                walk(sp, C, chunk)

            @block.tensor
            def _(pe):
                def unit(c, e, first):
                    pe.wait_ge(s.wlo, nth(c, e))
                    if not (first and e < 2):
                        b = (e - 2) % U
                        n = c - 1 if e < 2 else c
                        if b < F:
                            pe.wait_ge(s.relu, n * F + b + 1)
                        else:
                            pe.wait_ge(s.x, n * KT + b - F + 1)
                    wh, wl, nf = places(e)
                    mh, ml = (hh, hl) if e < F else (gh, gl)
                    for f in range(nf):
                        if first and e == 0:
                            pe.wait_ge(s.h, f + 1)
                        if e == F:
                            pe.wait_ge(s.g, c * F + f + 1)
                        for x, (w, m) in enumerate(((wh, mh), (wh, ml), (wl, mh))):
                            for b, (c0, n) in enumerate(chunks):
                                mm = pe.matmul(k.ps[:, SB * (e % 2) + b, 0:n], w[:, e % 2, f], m[:, f, c0:c0 + n],
                                               start=(f == 0 and x == 0), stop=(f == nf - 1 and x == 2))
                    mm.then_inc(s.mm, 1)

                def chunk(c, first, last):
                    for e in range(U):
                        unit(c, e, first)
                walk(pe, C, chunk)

            @block.scalar
            def _(act):
                def cut(c, e, first):
                    wh, _, nf = places(e)
                    act.wait_ge(s.wr0 if e % 2 == 0 else s.wr1, c * (8 * U) + (e // 2 + 1) * 16)
                    if waits_for(e) >= 0 or not first:
                        act.wait_ge(s.mm, nth(c, waits_for(e)))
                    nc.scalar.copy(wh[:, e % 2], raw[:, e % 2, 0:nf]).then_inc(s.whi, 1)

                cut(0, 0, True)
                for f in range(KT):
                    act.wait_ge(s.f, f + 1)
                    for w, a, b in ((0, 0, SEQ), (1, SEQ, n_tok)):
                        if b > a:
                            ins = nc.scalar.activation(g[:, a:b], g[:, a:b], ACT.Identity, scale=k.mods[:, layer, 4, f, w:w + 1],
                                                       bias=k.mods[:, layer, 3, f, w:w + 1])
                    ins.then_inc(s.fm, 1)

                def chunk(c, first, last):
                    for e in range(U):
                        if e + 1 < U:
                            cut(c, e + 1, first)
                        elif not last:
                            cut(c + 1, 0, False)
                        if e < F:
                            act.wait_ge(s.mm, nth(c, e))
                            if not (first and e == 0):
                                act.wait_ge(s.g, c * F + e)
                            nc.scalar.activation(g[:], k.ps[:, SB * (e % 2):SB * (e % 2) + SB].rearrange("p b c -> p (b c)")[:, 0:n_tok],
                                                 ACT.Relu).then_inc(s.relu, 1)
                walk(act, C, chunk)

            @block.vector
            def _(dve):
                def cut(c, e):
                    wh, wl, nf = places(e)
                    dve.wait_ge(s.whi, nth(c, e))
                    nc.vector.tensor_tensor(wl[:, e % 2], raw[:, e % 2, 0:nf], f32(wh[:, e % 2]), ALU.subtract).then_inc(s.wlo, 1)

                cut(0, 0)
                for f in range(KT):
                    if f:
                        dve.wait_ge(s.h, f)
                    nc.vector.tensor_tensor(g[:], k.xT[:, f, 0:n_tok], k.rstd[:, 0:n_tok], ALU.mult).then_inc(s.f, 1)
                    dve.wait_ge(s.fm, f + 1)
                    nc.vector.tensor_copy(hh[:, f], g[:]).then_inc(s.hh, 1)
                    dve.wait_ge(s.hh, f + 1)
                    nc.vector.tensor_tensor(hl[:, f], g[:], f32(hh[:, f]), ALU.subtract).then_inc(s.h, 1)

                def chunk(c, first, last):
                    for e in range(U):
                        if e + 1 < U:
                            cut(c, e + 1)
                        elif not last:
                            cut(c + 1, 0)
                        if e < F:
                            me = c * F + e + 1
                            dve.wait_ge(s.relu, me)
                            nc.vector.tensor_tensor(g[:], g[:], g[:], ALU.mult).then_inc(s.sq, 1)
                            dve.wait_ge(s.sq, me)
                            nc.vector.tensor_copy(gh[:, e], g[:]).then_inc(s.gh, 1)
                            dve.wait_ge(s.gh, me)
                            nc.vector.tensor_tensor(gl[:, e], g[:], f32(gh[:, e]), ALU.subtract).then_inc(s.g, 1)
                        else:
                            dve.wait_ge(s.mm, nth(c, e))
                            add_gated(k, dve, layer, 5, e - F, SB * (e % 2), n_tok).then_inc(s.x, 1)
                walk(dve, C, chunk)


def closing(k):
    nc = k.nc
    with phase(nc, "close", "T cp0 cp1 st0 st1") as s, ExitStack() as st:
        rows = st.enter_context(nc.sbuf_tensor("out_rows", [P, 2, D_MODEL], F32))
        out = k.out.rearrange("b (t p) d -> (b t) p d", p=P)
        with nc.Block() as block:
            @block.tensor
            def _(pe):
                for t in range(LT):
                    if t >= 2:
                        pe.wait_ge(s.cp0, t - 1)
                        pe.wait_ge(s.cp1, t - 1)
                    for f in range(KT):
                        mm = pe.transpose(k.ps[:, 2 * (t % 2) + f // 4, (f % 4) * P:(f % 4 + 1) * P],
                                          k.xT[:, f, t * P:(t + 1) * P], k.ident[:])
                    mm.then_inc(s.T, 1)

            @block.scalar
            def _(act):
                for t in range(LT):
                    act.wait_ge(s.T, t + 1)
                    if t >= 2:
                        act.wait_ge(s.st0 if t % 2 == 0 else s.st1, 16 * (t // 2))
                    nc.scalar.copy(rows[:, t % 2, 0:512], k.ps[:, 2 * (t % 2)]).then_inc(s.cp0, 1)

            @block.vector
            def _(dve):
                for t in range(LT):
                    dve.wait_ge(s.T, t + 1)
                    if t >= 2:
                        dve.wait_ge(s.st0 if t % 2 == 0 else s.st1, 16 * (t // 2))
                    nc.vector.tensor_copy(rows[:, t % 2, 512:1024], k.ps[:, 2 * (t % 2) + 1]).then_inc(s.cp1, 1)

            @block.sync
            def _(sp):
                for t in range(LT):
                    sp.wait_ge(s.cp0, t + 1)
                    sp.wait_ge(s.cp1, t + 1)
                    sp.dma_start(out[t], rows[:, t % 2]).then_inc(s.st0 if t % 2 == 0 else s.st1, 16)
                sp.wait_ge(s.st0, 16 * LT // 2)
                sp.wait_ge(s.st1, 16 * LT // 2)


def trunk(nc, out, **ins):
    with ExitStack() as st:
        k = Core(nc, st, ins, out)
        ev = ins["ev_w_in"][0]
        opening(k)
        norm_stats(k, "n0", TOK)
        project(k, "pa", 0, ev, 0, 1024, [
            Unit(0, 512, 8, ins["diff_q_g"][0], HD ** -0.5, True, k.qkA, 0),
            Unit(512, 512, 8, ins["diff_k_g"][0], 1.0, True, k.qkA, 8)])
        project(k, "pb", 0, ev, 1024, 1280, [
            Unit(512, 512, 8, ins["swa_q_g"][0], HD ** -0.5, True, k.qkB, 0),
            Unit(1024, 256, 2, ins["swa_k_g"][0], 1.0, True, k.qkB, 8, v=128, v_dst=k.vB),
            Unit(0, 512, v=512, v_dst=k.vA)])
        attend(k, "ab", window_pieces(), 8,
               stacked_loader(k.qkB, 0, lambda i, p: 8 + i // 2, k.vB, lambda i, p: i // 2, HD),
               "two", HD, k.mix[0], 512, sink=ins["swa_sink"][0])
        attend_diff(k, "aa", ins)
        out_project(k, "o0", 0, TOK, ins["w_out"][0], subln=ins["diff_subln_g"][0])
        norm_stats(k, "n1", TOK)
        mlp(k, "m0", 0, TOK, ins["mlp_w1"][0], ins["mlp_w2"][0])
        od = ins["od_w_in"][0]
        bias_pad(k, ins["na_rpb"][0])
        norm_stats(k, "n2", TOK)
        project_low_rank(k, "pq", 1, od, 0, MLA_QL, MLA_QL, ins["mla_qa_g"][0], ins["mla_wq_up"][0],
                         ins["mla_q_g"][0], MLA_QK ** -0.5, 0, False)
        project_low_rank(k, "pk", 1, od, MLA_QL, MLA_KVL + MLA_ROPE, MLA_KVL, ins["mla_kva_g"][0], ins["mla_wkv_up"][0],
                         ins["mla_k_g"][0], 1.0, MLA_HEADS, True)
        project(k, "pd", 1, od, MLA_QL + MLA_KVL + MLA_ROPE, 1536, [
            Unit(0, 512, 8, ins["na_q_g"][0], HD ** -0.5, False, k.qkD, 0),
            Unit(512, 512, 8, ins["na_k_g"][0], 1.0, False, k.qkD, 8),
            Unit(1024, 512, v=512, v_dst=k.vD)])
        attend(k, "ac", [Piece(q, [(0, TOK)]) for q in range(LT)], MLA_HEADS, parts_loader(k), "three", MLA_V, k.mix[1], 0)
        attend(k, "ad", neighbour_pieces(), NA_HEADS,
               stacked_loader(k.qkD, 0, lambda i, p: i * 2 + p + 8, k.vD, lambda i, p: i * 2 + p, HD),
               "two", HD, k.mix[1], 512, bias=bias_loader(k))
        out_project(k, "o1", 1, SEQ, ins["w_out"][1])
        norm_stats(k, "n3", SEQ)
        mlp(k, "m1", 1, SEQ, ins["mlp_w1"][1], ins["mlp_w2"][1])
        closing(k)


_OUTS = [((1, SEQ, D_MODEL), "float32")]


def kernel(**inputs):
    import numpy as _np
    import concourse.bacc as _bacc
    from concourse import mybir as _mybir
    from concourse.bass_utils import run_bass_kernel_spmd as _run

    nc = _bacc.Bacc("TRN2", target_bir_lowering=False, num_devices=1)
    arrays, args = {}, {}
    for name, a in {**inputs, **shape_constants()}.items():
        a = _np.ascontiguousarray(a)
        arrays[f"in_{name}"] = a
        args[name] = nc.dram_tensor(f"in_{name}", a.shape, _mybir.dt.from_np(a.dtype), kind="ExternalInput").ap()
    out = nc.dram_tensor("out_0", _OUTS[0][0], _mybir.dt.float32, kind="ExternalOutput").ap()
    trunk(nc, out, **args)
    r = _run(nc, [arrays], core_ids=[0])
    return r.results[0]["out_0"]
```

```python
from collections import namedtuple
from contextlib import ExitStack, contextmanager
import math

import numpy as np

import concourse.bass as bass
from concourse import mybir

ALU = mybir.AluOpType
ACT = mybir.ActivationFunctionType
AX = mybir.AxisListType
F32 = mybir.dt.float32
F32R = mybir.dt.float32r

P = 128
D_MODEL = 1024
KT = D_MODEL // P
SEQ = 1024
CTX = 256
TOK = SEQ + CTX
NT = TOK // P
LT = SEQ // P
GRID_W = 64
HD = 64
EPS = 1e-6
MASKED = -2.0 ** 100
DIFF_HEADS = 4
LAM_INIT = 0.8 - 0.6 * math.exp(0.0)
FF = 4 * D_MODEL
FFC = 512
MLA_HEADS, MLA_QK, MLA_NOPE, MLA_ROPE, MLA_V = 8, 96, 64, 32, 64
MLA_QL, MLA_KVL = 512, 256
NA_HEADS, NA_COLS, NA_ROWS = 8, 16, 8
RPB_R, RPB_C = 2 * NA_ROWS - 1, 2 * NA_COLS - 1
PADW = 2 * GRID_W - 1


def f32(ap):
    return ap.bitcast(F32)


@contextmanager
def phase(nc, name, sems):
    with ExitStack() as st:
        s = namedtuple("Semaphores", sems)(*[st.enter_context(nc.semaphore(f"{name}_{n}")) for n in sems.split()])
        yield s
        with nc.Block() as block:
            @block.sync
            def _(sp):
                for sem in s:
                    sp.sem_clear(sem)


def token_chunks(n):
    return [(c, min(512, n - c)) for c in range(0, n, 512)]


def shape_constants():
    out = {}

    def rope(rot):
        t = np.arange(SEQ, dtype=np.int32)
        row, col = (t // GRID_W).astype(np.float32), (t % GRID_W).astype(np.float32)
        nf = rot // 4
        freqs = np.power(np.float32(10000.0), -np.arange(nf, dtype=np.float32) / np.float32(nf)).astype(np.float32)
        ar, ac = row[:, None] * freqs, col[:, None] * freqs
        ang = np.concatenate([ar, ar, ac, ac], -1).astype(np.float32)
        cos, sin = np.cos(ang), np.sin(ang)
        sign = np.repeat(np.array([-1, 1, -1, 1], np.float32), nf)
        cos = np.concatenate([cos, np.ones((CTX, rot), np.float32)])
        sin = np.concatenate([sin * sign, np.zeros((CTX, rot), np.float32)])
        both = np.stack([cos, sin]).astype(np.float32)
        return np.ascontiguousarray(both.reshape(2, NT, P, rot).transpose(2, 0, 1, 3))

    out["rope64"] = rope(HD)
    out["rope32"] = rope(MLA_ROPE)
    out["ident"] = np.eye(P, dtype=np.float32)
    q, c = np.arange(P)[:, None], np.arange(P)[None, :]
    before, after = np.where(c >= q, 0, MASKED), np.where(c <= q, 0, MASKED)
    out["wmask"] = np.stack([before, after], 1).astype(np.float32)
    out["wband"] = np.stack([after.T, np.zeros((P, P)), before.T], 1).astype(np.float32)
    cq, ck = np.arange(GRID_W)[:, None], np.arange(GRID_W)[None, :]
    cs = np.clip(cq - NA_COLS // 2, 0, GRID_W - NA_COLS)
    col = np.where((ck >= cs) & (ck < cs + NA_COLS), 0, MASKED).astype(np.float32)
    out["cmask"] = np.concatenate([col, col], 0)
    out["cmaskT"] = np.tile(col.T, (2, 2))
    first, last = np.zeros((2, P, P), np.float32)
    first[GRID_W:, :GRID_W] = MASKED
    last[:GRID_W, :GRID_W] = MASKED
    last[:, GRID_W:] = MASKED
    out["rmask"] = np.ascontiguousarray(np.stack([first, last, first.T, last.T], 1))
    return out


class Core:

    def __init__(self, nc, st, ins, out):
        self.nc, self.ins, self.out = nc, ins, out

        def sb(name, shape, dt=F32):
            return st.enter_context(nc.sbuf_tensor(name, shape, dt))

        self.xT = sb("xT", [P, KT, TOK])
        self.rstd = sb("rstd", [P, TOK])
        self.mods = sb("mods", [P, 2, 6, KT, 2])
        self.ident = sb("ident_sb", [P, P])
        self.ones = sb("ones_sb", [P, P])
        self.identr = sb("identr_sb", [P, P], F32R)
        self.onesr = sb("onesr_sb", [P, P], F32R)
        self.eps = sb("eps_sb", [P, 1])
        self.ps = st.enter_context(nc.psum_tensor("ps", [P, 8, 512], F32))

        def dram(name, shape):
            return nc.dram_tensor(name, shape, F32, kind="Internal").ap()

        self.qkA = dram("qkA", [16, P, TOK])
        self.vA = dram("vA", [TOK, 512])
        self.qkB = dram("qkB", [10, P, TOK])
        self.vB = dram("vB", [TOK, P])
        self.qkC = dram("qkC", [16, 2, MLA_QK, TOK])
        self.vC = dram("vC", [TOK, 512])
        self.qkD = dram("qkD", [16, P, TOK])
        self.vD = dram("vD", [TOK, 512])
        self.mix = [dram(f"mix{i}", [TOK, D_MODEL]) for i in range(2)]
        self.bias = dram("rpb_bias", [GRID_W, NA_HEADS * RPB_R, GRID_W])
        self.biasT = dram("rpb_biasT", [GRID_W, RPB_R + 1, NA_HEADS, GRID_W])


def opening(k):
    nc, i = k.nc, k.ins
    names = ("consts rows rowsT cols ones neg e1 inv silu sh sl xin0 xin1 xin2 xin3 xTd xcpA xcpD "
             "aw0 aw1 aw2 whi wlo ada rowcp colT m1 modd m0")
    with phase(nc, "open", names) as s, ExitStack() as st:
        def sb(name, shape, dt=F32):
            return st.enter_context(nc.sbuf_tensor(name, shape, dt))
        HALF = D_MODEL // 2
        HF = HALF // P
        N_HALVES = 2 * 6 * D_MODEL // HALF
        XB, WB = 4, 3
        rows = sb("rows", [48, P])
        brows = sb("brows", [96, P])
        cols = sb("cols", [P, 48])
        bcols = sb("bcols", [P, 96])
        sil = sb("sil", [P, 16])
        tmp = sb("siltmp", [P, 16])
        sil4 = sb("sil4", [P, KT, 4], F32R)
        xin = sb("xin", [P, XB, D_MODEL])
        aw = sb("aw", [P, WB, KT, HALF])
        awh, awl = sb("awh", [P, 2, KT, HALF], F32R), sb("awl", [P, 2, KT, HALF], F32R)
        mrow = sb("mrow", [4, 2, HALF])
        msum = sb("msum", [P, HF, 2])
        ada_w = i["ada_w"].rearrange("l (k p) (j n) -> l j p k n", p=P, n=D_MODEL)
        x_rows = i["x"].rearrange("b (t p) d -> (b t) p d", p=P)
        ctx_rows = i["ctx"].rearrange("b (t p) d -> (b t) p d", p=P)
        TB, CB, AB = 0, 4, 6
        xin_sem, aw_sem = (s.xin0, s.xin1, s.xin2, s.xin3), (s.aw0, s.aw1, s.aw2)
        steps = [("x", t) for t in range(XB)]
        for n in range(N_HALVES):
            steps += [("ada", n)] + [("x", t) for t in (XB + 2 * n, XB + 2 * n + 1) if t < NT]

        with nc.Block() as block:
            @block.sync
            def _(sp):
                sp.dma_start(k.ident[:], i["ident"]).then_inc(s.consts, 16)
                sp.dma_start(rows[0:8, :], i["c"].rearrange("b (k p) -> (b k) p", p=P)).then_inc(s.rows, 16)
                sp.dma_start(rows[8:16, :], i["c_ctx"].rearrange("(k p) -> k p", p=P)).then_inc(s.rows, 16)
                sp.dma_start(rows[16:32, :], i["norm1_g"].rearrange("l (k p) -> (l k) p", p=P)).then_inc(s.rows, 16)
                sp.dma_start(rows[32:48, :], i["norm2_g"].rearrange("l (k p) -> (l k) p", p=P)).then_inc(s.rows, 16)
                sp.dma_start(brows[:], i["ada_b"].rearrange("l (k p) -> (l k) p", p=P)).then_inc(s.rows, 16)
                for what, n in steps:
                    if what == "x":
                        if n >= XB:
                            sp.wait_ge(s.xTd, n - XB + 1)
                        sp.dma_start(xin[:, n % XB], x_rows[n] if n < LT else ctx_rows[n - LT]).then_inc(xin_sem[n % XB], 16)
                    else:
                        if n >= WB:
                            sp.wait_ge(s.wlo, n - WB + 1)
                        c = (n % 2) * HALF
                        sp.dma_start(aw[:, n % WB], ada_w[n // 12, n // 2 % 6, :, :, c:c + HALF]).then_inc(aw_sem[n % WB], 16)

            @block.tensor
            def _(pe):
                pe.wait_ge(s.consts, 16)
                pe.wait_ge(s.rows, 80)
                pe.transpose(k.ps[:, CB, 0:48], rows[:], k.ident[0:48, 0:48])
                pe.transpose(k.ps[:, CB, 64:160], brows[:], k.ident[0:96, 0:96]).then_inc(s.rowsT, 1)

                def turn_x(t):
                    pe.wait_ge(xin_sem[t % XB], 16 * (t // XB + 1))
                    if t >= 2:
                        pe.wait_ge(s.xcpA, t - 1)
                        pe.wait_ge(s.xcpD, t - 1)
                    for f in range(KT):
                        b = TB + 2 * (t % 2) + f // 4
                        mm = pe.transpose(k.ps[:, b, (f % 4) * P:(f % 4 + 1) * P], xin[:, t % XB, f * P:(f + 1) * P], k.ident[:])
                    mm.then_inc(s.xTd, 1)

                def ada(n):
                    if n == 0:
                        pe.wait_ge(s.sl, 1)
                    pe.wait_ge(s.wlo, n + 1)
                    if n >= 2:
                        pe.wait_ge(s.rowcp, n - 1)
                    for f in range(KT):
                        o = k.ps[0:4, AB + n % 2, :]
                        pe.matmul(o, sil4[:, f], awh[:, n % 2, f], start=(f == 0), stop=False)
                        mm = pe.matmul(o, sil4[:, f], awl[:, n % 2, f], start=False, stop=(f == KT - 1))
                    mm.then_inc(s.ada, 1)

                def turn_rows(n):
                    pe.wait_ge(s.rowcp, n + 1)
                    pe.wait_ge(s.cols, 2)
                    if n >= 2:
                        pe.wait_ge(s.modd, n - 1)
                    for f in range(HF):
                        mm = pe.transpose(k.ps[:, CB + n % 2, 4 * f:4 * f + 4], mrow[:, n % 2, f * P:(f + 1) * P], k.ident[0:4, 0:4])
                    mm.then_inc(s.colT, 1)

                for what, n in steps:
                    if what == "x":
                        turn_x(n)
                    else:
                        ada(n)
                        if n:
                            turn_rows(n - 1)
                turn_rows(N_HALVES - 1)

            @block.scalar
            def _(act):
                act.wait_ge(s.cols, 2)
                nc.scalar.activation(tmp[:], cols[:, 0:16], ACT.Exp, scale=-1.0).then_inc(s.neg, 1)

                def rows_out(n):
                    act.wait_ge(s.ada, n + 1)
                    if n >= 2:
                        act.wait_ge(s.colT, n - 1)
                    nc.scalar.copy(mrow[:, n % 2], k.ps[0:4, AB + n % 2, :]).then_inc(s.rowcp, 1)

                for what, n in steps:
                    if what == "x":
                        act.wait_ge(s.xTd, n + 1)
                        nc.scalar.copy(k.xT[:, 0:4, n * P:(n + 1) * P],
                                       k.ps[:, TB + 2 * (n % 2), :].rearrange("p (f q) -> p f q", q=P)).then_inc(s.xcpA, 1)
                    else:
                        act.wait_ge(aw_sem[n % WB], 16 * (n // WB + 1))
                        if n >= 2:
                            act.wait_ge(s.ada, n - 1)
                        nc.scalar.copy(awh[:, n % 2], aw[:, n % WB]).then_inc(s.whi, 1)
                        if n:
                            rows_out(n - 1)
                rows_out(N_HALVES - 1)

            @block.vector
            def _(dve):
                nc.vector.memset(k.ones[:], 1.0).then_inc(s.ones, 1)
                nc.vector.memset(k.eps[:], EPS).then_inc(s.ones, 1)
                dve.wait_ge(s.ones, 2)
                nc.vector.tensor_copy(k.onesr[:], k.ones[:]).then_inc(s.ones, 1)
                dve.wait_ge(s.consts, 16)
                nc.vector.tensor_copy(k.identr[:], k.ident[:]).then_inc(s.ones, 1)
                dve.wait_ge(s.rowsT, 1)
                nc.vector.tensor_copy(cols[:], k.ps[:, CB, 0:48]).then_inc(s.cols, 1)
                nc.vector.tensor_copy(bcols[:], k.ps[:, CB, 64:160]).then_inc(s.cols, 1)
                dve.wait_ge(s.neg, 1)
                nc.vector.tensor_scalar(tmp[:], tmp[:], 1.0, None, ALU.add).then_inc(s.e1, 1)
                dve.wait_ge(s.e1, 1)
                nc.vector.reciprocal(tmp[:], tmp[:]).then_inc(s.inv, 1)
                dve.wait_ge(s.inv, 1)
                nc.vector.tensor_tensor(sil[:], cols[:, 0:16], tmp[:], ALU.mult).then_inc(s.silu, 1)
                dve.wait_ge(s.silu, 1)
                by_tile = sil[:].rearrange("p (w f) -> p f w", w=2)
                nc.vector.tensor_copy(sil4[:, :, 0:2], by_tile).then_inc(s.sh, 1)
                dve.wait_ge(s.sh, 1)
                nc.vector.tensor_tensor(sil4[:, :, 2:4], by_tile, f32(sil4[:, :, 0:2]), ALU.subtract).then_inc(s.sl, 1)

                def modulation(n):
                    l, j, f0 = n // 12, n // 2 % 6, (n % 2) * HF
                    dve.wait_ge(s.colT, n + 1)
                    if n:
                        dve.wait_ge(s.modd, n)
                    part = k.ps[:, CB + n % 2, 0:4 * HF].rearrange("p (f a) -> p f a", a=4)
                    c = (n // 2) * KT + f0
                    nc.vector.tensor_tensor(msum[:], part[:, :, 0:2], bcols[:, c:c + HF].unsqueeze(2).broadcast_to([P, HF, 2]),
                                            ALU.add).then_inc(s.m1, 1)
                    dve.wait_ge(s.m1, n + 1)
                    m = k.mods[:, l, j, f0:f0 + HF]
                    nc.vector.tensor_tensor(m, msum[:], part[:, :, 2:4], ALU.add).then_inc(s.modd, 1)
                    if j in (1, 4):
                        c = (16 if j == 1 else 32) + l * KT + f0
                        dve.wait_ge(s.modd, n + 1)
                        nc.vector.scalar_tensor_tensor(out=m, in0=m, scalar=1.0,
                                                       in1=cols[:, c:c + HF].unsqueeze(2).broadcast_to([P, HF, 2]),
                                                       op0=ALU.add, op1=ALU.mult).then_inc(s.m0, 1)

                for what, n in steps:
                    if what == "x":
                        dve.wait_ge(s.xTd, n + 1)
                        nc.vector.tensor_copy(k.xT[:, 4:8, n * P:(n + 1) * P],
                                              k.ps[:, TB + 2 * (n % 2) + 1, :].rearrange("p (f q) -> p f q", q=P)).then_inc(s.xcpD, 1)
                    else:
                        dve.wait_ge(s.whi, n + 1)
                        if n >= 2:
                            dve.wait_ge(s.ada, n - 1)
                        nc.vector.tensor_tensor(awl[:, n % 2], aw[:, n % WB], f32(awh[:, n % 2]), ALU.subtract).then_inc(s.wlo, 1)
                        if n >= 2:
                            modulation(n - 2)
                modulation(N_HALVES - 2)
                modulation(N_HALVES - 1)


def norm_stats(k, name, n_tok):
    nc = k.nc
    with phase(nc, name, "sq acc sum root") as s, ExitStack() as st:
        sq = st.enter_context(nc.sbuf_tensor(f"{name}_sq", [P, 2, TOK], F32))
        acc = st.enter_context(nc.sbuf_tensor(f"{name}_acc", [P, TOK], F32))
        chunks = token_chunks(n_tok)
        with nc.Block() as block:
            @block.scalar
            def _(act):
                for f in range(KT):
                    if f >= 2:
                        act.wait_ge(s.acc, f - 1)
                    nc.scalar.activation(sq[:, f % 2, 0:n_tok], k.xT[:, f, 0:n_tok], ACT.Square).then_inc(s.sq, 1)
                act.wait_ge(s.sum, 1)
                for c, (c0, n) in enumerate(chunks):
                    nc.scalar.activation(k.rstd[:, c0:c0 + n], k.ps[:, c, 0:n], ACT.Sqrt, bias=k.eps[:],
                                         scale=1.0 / D_MODEL).then_inc(s.root, 1)

            @block.vector
            def _(dve):
                for f in range(KT):
                    dve.wait_ge(s.sq, f + 1)
                    if f == 0:
                        nc.vector.tensor_copy(acc[:, 0:n_tok], sq[:, 0, 0:n_tok]).then_inc(s.acc, 1)
                    else:
                        dve.wait_ge(s.acc, f)
                        nc.vector.tensor_tensor(acc[:, 0:n_tok], acc[:, 0:n_tok], sq[:, f % 2, 0:n_tok],
                                                ALU.add).then_inc(s.acc, 1)
                for c, (c0, n) in enumerate(chunks):
                    dve.wait_ge(s.root, c + 1)
                    nc.vector.reciprocal(k.rstd[:, c0:c0 + n], k.rstd[:, c0:c0 + n])

            @block.tensor
            def _(pe):
                pe.wait_ge(s.acc, KT)
                for c, (c0, n) in enumerate(chunks):
                    mm = pe.matmul(k.ps[:, c, 0:n], k.ones[:], acc[:, c0:c0 + n], start=True, stop=True)
                mm.then_inc(s.sum, 1)


def at_tile(i, p):
    return i * 2 + p


def wait_then_store(sp, sem, value, begun):
    sp.wait_ge(sem, value)
    sp.sem_inc(begun, 1)


def walk_pairs(eng, pair):
    pair(0, True, False)
    with eng.Fori(1, NT // 2 - 1) as i:
        pair(i, False, False)
    pair(NT // 2 - 1, False, True)


def weight_places(s):
    return [s.wraw0, s.wraw1, s.wraw2, s.wraw3]


def load_weights(sp, s, raw, w_dram, n_k, n_raw):
    for f in range(n_k):
        if f >= n_raw:
            sp.wait_ge(s.wlo, f - n_raw + 1)
        sp.dma_start(raw[:, f % n_raw], w_dram[f]).then_inc(weight_places(s)[f % n_raw], 16)


def cut_hi(nc, act, s, raw, wh, n_k, n_raw):
    for f in range(n_k):
        act.wait_ge(weight_places(s)[f % n_raw], 16 * (f // n_raw + 1))
        nc.scalar.copy(wh[:, f], raw[:, f % n_raw]).then_inc(s.whi, 1)


def cut_lo(nc, dve, s, raw, wh, wl, n_k, n_raw):
    for f in range(n_k):
        dve.wait_ge(s.whi, f + 1)
        nc.vector.tensor_tensor(wl[:, f], raw[:, f % n_raw], f32(wh[:, f]), ALU.subtract).then_inc(s.wlo, 1)


def modulated(k, pool, s, h, modt, i, p, first):
    nc = k.nc
    tile, q = bass.ds(at_tile(i, p), 1), bass.ds(at_tile(i, p) * P, P)
    nth = i * 2 + p + 1
    if not first:
        pool.wait_ge(s.h, nth - 1)
        pool.sem_inc(s.pooled, 1)
    nc.gpsimd.tensor_tensor(h[:], k.xT[:, :, q], k.rstd[:, q].unsqueeze(1).broadcast_to([P, KT, P]),
                            ALU.mult).then_inc(s.fbase, 1)
    pool.wait_ge(s.fbase, nth)
    pool.sem_inc(s.pooled, 1)
    nc.gpsimd.tensor_tensor(h[:], h[:], modt[:, tile, 0].squeeze(1).unsqueeze(2).broadcast_to([P, KT, P]),
                            ALU.mult).then_inc(s.fscale, 1)
    pool.wait_ge(s.fscale, nth)
    pool.sem_inc(s.pooled, 1)
    nc.gpsimd.tensor_tensor(h[:], h[:], modt[:, tile, 1].squeeze(1).unsqueeze(2).broadcast_to([P, KT, P]),
                            ALU.add).then_inc(s.fmod, 1)


class Unit:

    def __init__(self, c0, width, heads=0, gain=None, gain_scale=1.0, rope=False, dst=None, base=0, v=0, v_dst=None):
        self.c0, self.width, self.heads, self.gain, self.gain_scale = c0, width, heads, gain, gain_scale
        self.rope, self.dst, self.base, self.v, self.v_dst = rope, dst, base, v, v_dst


def project(k, name, layer, w_in, col0, n_cols, units):
    nc = k.nc
    U = len(units)
    hu = [j for j, u in enumerate(units) if u.heads]
    HU = len(hu)
    vu = [j for j, u in enumerate(units) if u.v]
    VU = len(vu)
    assert HU == 2
    ropes = sum(1 for j in hu if units[j].rope)
    assert ropes in (0, 2)
    slots = [("mm", 0), ("turn", 1, -1)] + [("mm", j) for j in range(1, U)] + [("turn", 0, 0)]
    names = ("gains ropec fbase fmod h wraw0 wraw1 wraw2 wraw3 whi wlo mm sq red y root ri yn u w yf hi lo tr tc qd0 qd1 vc va0 va1 vb0 vb1 modt ht begun")
    with phase(nc, name, names) as s, ExitStack() as st:
        def sb(nm, shape, dt=F32):
            return st.enter_context(nc.sbuf_tensor(f"{name}_{nm}", shape, dt))
        wh, wl = sb("wh", [P, KT, n_cols], F32R), sb("wl", [P, KT, n_cols], F32R)
        n_raw = 4 if n_cols <= 1024 else 3
        raw = sb("wraw", [P, n_raw, n_cols])
        h = sb("hfull", [P, KT, P])
        hh, hl = sb("hh", [P, 2, KT, P], F32R), sb("hl", [P, 2, KT, P], F32R)
        modt = sb("modt", [P, NT, 2, KT])
        sq, y = sb("sqh", [P, 512]), sb("yh", [P, 512])
        w_, u_ = (sb("w_", [P, 512]), sb("u_", [P, 512])) if ropes else (None, None)
        rs = sb("rsh", [P, 8])
        qh = [sb(f"qh{n}", [P, 8, 2, HD], F32R) for n in range(HU)]
        stage = sb("stage", [P, 2, 8, P])
        vst = [sb(f"vst{n}", [P, 2, units[j].v]) for n, j in enumerate(vu)]
        gain = [sb(f"gain{n}", [P, HD]) for n in range(HU)]
        rope = sb("rope", [P, 2, NT, HD]) if ropes else None
        sint = sb("sint", [P, 2, HD]) if ropes else None
        w_dram = w_in.rearrange("(f p) n -> f p n", p=P)[:, :, col0:col0 + n_cols]
        TB = 4

        def v_stored(j, p):
            return ((s.va0, s.va1), (s.vb0, s.vb1))[vu.index(j)][p]

        def done(i, p, per, j):
            return (i * 2 + p) * per + j + 1

        with nc.Block() as block:
            @block.sync
            def _(sp):
                for n, j in enumerate(hu):
                    sp.dma_start(gain[n][:], units[j].gain.unsqueeze(0).broadcast_to([P, HD])).then_inc(s.gains, 16)
                if ropes:
                    sp.dma_start(rope[:], k.ins["rope64"]).then_inc(s.ropec, 16)
                load_weights(sp, s, raw, w_dram, KT, n_raw)

                def store_heads(n, i, p):
                    u = units[hu[n]]
                    wait_then_store(sp, s.tc, done(i, p, HU, n), s.begun)
                    dst = u.dst[u.base:u.base + u.heads].rearrange("h r q -> r h q")
                    sp.dma_start(dst[:, :, bass.ds(at_tile(i, p) * P, P)], stage[:, n, 0:u.heads]).then_inc(
                        s.qd0 if n == 0 else s.qd1, 16)

                def store_v(j, i, p):
                    n = vu.index(j)
                    wait_then_store(sp, s.vc, done(i, p, VU, n), s.begun)
                    sp.dma_start(units[j].v_dst[bass.ds(at_tile(i, p) * P, P)], vst[n][:, p]).then_inc(v_stored(j, p), 16)

                def pair(i, first, last):
                    for p in range(2):
                        for slot in slots:
                            if slot[0] == "turn" and not (first and p + slot[2] < 0):
                                store_heads(slot[1], i, p + slot[2])
                            if slot[0] == "mm" and units[slot[1]].v:
                                store_v(slot[1], i, p)
                walk_pairs(sp, pair)
                store_heads(HU - 1, NT // 2 - 1, 1)
                sp.wait_ge(s.qd0, 16 * NT)
                sp.wait_ge(s.qd1, 16 * NT)
                for j in vu:
                    for p in range(2):
                        sp.wait_ge(v_stored(j, p), 16 * (NT // 2))

            @block.tensor
            def _(pe):
                def products(j, i, p, first):
                    u = units[j]
                    if j == 0:
                        pe.wait_ge(s.h, done(i, p, 1, 0))
                    if not (first and p == 0):
                        if u.heads:
                            pe.wait_ge(s.y, done(i, p - 1, HU, hu.index(j)))
                        else:
                            pe.wait_ge(s.vc, done(i, p - 1, VU, vu.index(j)))
                    c = slice(u.c0, u.c0 + u.width)
                    for f in range(KT):
                        if first and p == 0 and j == 0:
                            pe.wait_ge(s.wlo, f + 1)
                        o = k.ps[:, j, 0:u.width]
                        pe.matmul(o, hh[:, p, f], wh[:, f, c], start=(f == 0), stop=False)
                        pe.matmul(o, hh[:, p, f], wl[:, f, c], start=False, stop=False)
                        mm = pe.matmul(o, hl[:, p, f], wh[:, f, c], start=False, stop=(f == KT - 1))
                    mm.then_inc(s.mm, 1)

                def turn(n, i, p, free):
                    u = units[hu[n]]
                    pe.wait_ge(s.lo, done(i, p, HU, n))
                    if free:
                        pe.wait_ge(s.tc, done(i, p - 1, HU, n))
                    for x in range(u.heads):
                        mm = pe.transpose(k.ps[:, TB + 2 * n + x // 4, (x % 4) * P:(x % 4 + 1) * P],
                                          f32(qh[n][:, x].rearrange("p a d -> p (a d)")), k.ident[:])
                    mm.then_inc(s.tr, 1)

                def pair(i, first, last):
                    for p in range(2):
                        for slot in slots:
                            if slot[0] == "mm":
                                products(slot[1], i, p, first)
                            elif not (first and p + slot[2] < 0):
                                turn(slot[1], i, p + slot[2], not (first and p + slot[2] <= 0))
                walk_pairs(pe, pair)
                turn(HU - 1, NT // 2 - 1, 1, True)

            @block.scalar
            def _(act):
                def modulate(i, p):
                    t = at_tile(i, p)
                    act.wait_ge(s.fbase, done(i, p, 1, 0))
                    if ropes:
                        nc.scalar.copy(sint[:, p % 2], rope[:, 1, bass.ds(t, 1)].squeeze(1))
                    for f in range(KT):
                        a = nc.scalar.activation(h[:, f], h[:, f], ACT.Identity,
                                                 scale=modt[:, bass.ds(t, 1), 0, f],
                                                 bias=modt[:, bass.ds(t, 1), 1, f])
                    a.then_inc(s.fmod, 1)

                def squares(j, i, p, first):
                    u, n = units[j], hu.index(j)
                    act.wait_ge(s.mm, done(i, p, U, j))
                    if not (first and p == 0 and n == 0):
                        act.wait_ge(s.red, done(i, p, HU, n - 1))
                    nc.scalar.activation(sq[:, 0:u.heads * HD], k.ps[:, j, 0:u.heads * HD], ACT.Square).then_inc(s.sq, 1)
                    act.wait_ge(s.red, done(i, p, HU, n))
                    nc.scalar.activation(rs[:, 0:u.heads], rs[:, 0:u.heads], ACT.Sqrt, bias=k.eps[:],
                                         scale=1.0 / HD).then_inc(s.root, 1)

                def values(j, i, p, first):
                    u = units[j]
                    act.wait_ge(s.mm, done(i, p, U, j))
                    if not first:
                        act.wait_ge(v_stored(j, p), i * 16)
                    nc.scalar.copy(vst[vu.index(j)][:, p], k.ps[:, j, u.heads * HD:u.heads * HD + u.v]).then_inc(s.vc, 1)

                def stage_heads(n, i, p, free):
                    u = units[hu[n]]
                    act.wait_ge(s.tr, done(i, p, HU, n))
                    if free:
                        act.wait_ge(s.qd0 if n == 0 else s.qd1, at_tile(i, p) * 16)
                    nc.scalar.copy(stage[:, n, 0:u.heads],
                                   k.ps[:, TB + 2 * n:TB + 2 * n + 2].rearrange("p b (x q) -> p (b x) q", q=P)[:, 0:u.heads]).then_inc(s.tc, 1)

                act.wait_ge(s.modt, 2)
                if ropes:
                    act.wait_ge(s.ropec, 16)
                modulate(0, 0)
                cut_hi(nc, act, s, raw, wh, KT, n_raw)

                def pair(i, first, last):
                    for p in range(2):
                        for x, slot in enumerate(slots):
                            if slot[0] == "mm":
                                if units[slot[1]].v:
                                    values(slot[1], i, p, first)
                                if units[slot[1]].heads:
                                    squares(slot[1], i, p, first)
                            elif not (first and p + slot[2] < 0):
                                stage_heads(slot[1], i, p + slot[2], not (first and p + slot[2] <= 0))
                            if x == 0 and not (last and p == 1):
                                modulate(i, p + 1)
                walk_pairs(act, pair)
                stage_heads(HU - 1, NT // 2 - 1, 1, True)

            @block.vector
            def _(dve):
                for w in range(2):
                    dst = modt[:, 0:LT, :, :] if w == 0 else modt[:, LT:NT, :, :]
                    n = LT if w == 0 else NT - LT
                    for c, part in ((0, 1), (1, 0)):
                        m = nc.vector.tensor_copy(dst[:, :, c], k.mods[:, layer, part, :, w].unsqueeze(1).broadcast_to([P, n, KT]))
                    m.then_inc(s.modt, 1)
                dve.wait_ge(s.gains, 16 * HU)
                for n, j in enumerate(hu):
                    if units[j].gain_scale != 1.0:
                        nc.vector.tensor_scalar(gain[n][:], gain[n][:], units[j].gain_scale, None, ALU.mult).then_inc(s.modt, 1)
                scaled = 2 + sum(1 for j in hu if units[j].gain_scale != 1.0)

                def base(i, p, first):
                    q = bass.ds(at_tile(i, p) * P, P)
                    if not first:
                        dve.wait_ge(s.h, done(i, p - 1, 1, 0))
                    nc.vector.tensor_tensor(h[:], k.xT[:, :, q], k.rstd[:, q].unsqueeze(1).broadcast_to([P, KT, P]),
                                            ALU.mult).then_inc(s.fbase, 1)

                def cut(i, p, first):
                    dve.wait_ge(s.fmod, done(i, p, 1, 0))
                    if not first:
                        dve.wait_ge(s.mm, done(i, p - 2, U, U - 1))
                    nc.vector.tensor_copy(hh[:, p % 2], h[:]).then_inc(s.ht, 1)
                    dve.wait_ge(s.ht, done(i, p, 1, 0))
                    nc.vector.tensor_tensor(hl[:, p % 2], h[:], f32(hh[:, p % 2]), ALU.subtract).then_inc(s.h, 1)

                def heads(j, i, p, first):
                    u, n = units[j], hu.index(j)
                    H, W = u.heads, u.heads * HD
                    me = done(i, p, HU, n)
                    v3 = lambda ap: ap[:, 0:W].rearrange("p (h d) -> p h d", d=HD)
                    dve.wait_ge(s.sq, me)
                    if not (first and p == 0 and n == 0):
                        dve.wait_ge(s.lo, done(i, p, HU, n - 1))
                    nc.vector.tensor_reduce(rs[:, 0:H], v3(sq), AX.X, ALU.add).then_inc(s.red, 1)
                    nc.vector.tensor_tensor(v3(y), v3(k.ps[:, j]), gain[n][:].unsqueeze(1).broadcast_to([P, H, HD]),
                                            ALU.mult).then_inc(s.y, 1)
                    dve.wait_ge(s.root, me)
                    nc.vector.reciprocal(rs[:, 0:H], rs[:, 0:H]).then_inc(s.ri, 1)
                    dve.wait_ge(s.ri, me)
                    dve.wait_ge(s.y, me)
                    nc.vector.tensor_tensor(v3(y), v3(y), rs[:, 0:H].unsqueeze(2).broadcast_to([P, H, HD]),
                                            ALU.mult).then_inc(s.yn, 1)
                    dve.wait_ge(s.yn, me)
                    if ropes:
                        cos = rope[:, 0, bass.ds(at_tile(i, p), 1)].broadcast_to([P, H, HD])
                        nc.vector.tensor_tensor(v3(w_), v3(y), cos, ALU.mult).then_inc(s.w, 1)
                        dve.wait_ge(s.w, me)
                        dve.wait_ge(s.u, me)
                        nc.vector.tensor_tensor(y[:, 0:W], w_[:, 0:W], u_[:, 0:W], ALU.add).then_inc(s.yf, 1)
                        dve.wait_ge(s.yf, me)
                    if not (first and p == 0):
                        dve.wait_ge(s.tr, done(i, p - 1, HU, n))
                    nc.vector.tensor_copy(qh[n][:, 0:H, 0], v3(y)).then_inc(s.hi, 1)
                    dve.wait_ge(s.hi, me)
                    nc.vector.tensor_tensor(qh[n][:, 0:H, 1], v3(y), f32(qh[n][:, 0:H, 0]), ALU.subtract).then_inc(s.lo, 1)

                base(0, 0, True)
                cut(0, 0, True)
                cut_lo(nc, dve, s, raw, wh, wl, KT, n_raw)
                dve.wait_ge(s.modt, scaled)
                if ropes:
                    dve.wait_ge(s.ropec, 16)

                def pair(i, first, last):
                    for p in range(2):
                        more = not (last and p == 1)
                        if more:
                            base(i, p + 1, False)
                        for x, j in enumerate(hu):
                            heads(j, i, p, first)
                            if x == 0 and more:
                                cut(i, p + 1, first and p == 0)
                walk_pairs(dve, pair)

            @block.gpsimd
            def _(pool):
                if ropes:
                    def pair(i, first, last):
                        for p in range(2):
                            for n, j in enumerate(hu):
                                H = units[j].heads
                                pool.wait_ge(s.yn, done(i, p, HU, n))
                                v5 = lambda ap: ap[:, 0:H * HD].rearrange("p (h a b d) -> p h a b d", a=2, b=2, d=HD // 4)
                                sin = sint[:, p:p + 1].rearrange("p o (a b d) -> p o a b d", a=2, b=2)
                                for b in range(2):
                                    ins = nc.gpsimd.tensor_tensor(v5(u_)[:, :, :, b], v5(y)[:, :, :, 1 - b],
                                                                  sin[:, :, :, b].broadcast_to([P, H, 2, HD // 4]), ALU.mult)
                                ins.then_inc(s.u, 1)
                    walk_pairs(pool, pair)


def project_low_rank(k, name, layer, w_in, col0, n_cols, rank, rank_gain, w_up, heads_gain, gain_scale, base, with_values):
    nc = k.nc
    H, D, R = MLA_HEADS, MLA_QK, MLA_ROPE
    RT = rank // P
    up = w_up.shape[1]
    UC = token_chunks(up)
    names = ("gains ropec fbase fscale fmod pooled h ht wraw0 wraw1 wraw2 wraw3 whi wlo ur0 ur1 uhi ulo mm sql rl rli low ah alo at atc up kn kr vc "
             "sqd red y root ri yn w u yf hi lo tr tc qd0 qd1 qd2 qd3 va0 va1 modt begun")
    with phase(nc, name, names) as s, ExitStack() as st:
        def sb(nm, shape, dt=F32):
            return st.enter_context(nc.sbuf_tensor(f"{name}_{nm}", shape, dt))
        wh, wl = sb("wh", [P, KT, n_cols], F32R), sb("wl", [P, KT, n_cols], F32R)
        uh, ul = sb("uph", [P, RT, up], F32R), sb("upl", [P, RT, up], F32R)
        n_raw = 4
        raw, uraw = sb("wraw", [P, n_raw, n_cols]), sb("uraw", [P, 2, up])
        h = sb("hfull", [P, KT, P])
        hh, hl = sb("hh", [P, 2, KT, P], F32R), sb("hl", [P, 2, KT, P], F32R)
        modt = sb("modt", [P, NT, 2, KT])
        lsum, lr = sb("lsum", [P, 1]), sb("lr", [P, 1])
        lsq = sb("lsq", [P, rank])
        low = sb("low", [P, rank])
        lowc = sb("lowc", [P, 2, rank], F32R)
        lowT = sb("lowT", [P, 2, RT, P], F32R)
        kr = sb("kr", [P, 2, R]) if with_values else None
        sq, y = sb("sqh", [P, H, D]), sb("yh", [P, H, D])
        w_, u_ = sb("w_", [P, H, R]), sb("u_", [P, H, R])
        rs = sb("rsh", [P, H])
        qh = sb("qh", [P, H, 2, D], F32R)
        stage = sb("stage", [D, 4, 4, P])
        vst = sb("vst", [P, 2, H * MLA_V]) if with_values else None
        rgain, gain = sb("rgain", [P, rank]), sb("gain", [P, D])
        rope = sb("rope", [P, 2, NT, R])
        w_dram = w_in.rearrange("(f p) n -> f p n", p=P)[:, :, col0:col0 + n_cols]
        u_dram = w_up.rearrange("(f p) n -> f p n", p=P)
        IB, LB, UB, TB = (0, 7), 1, 3, 5
        ups = k.ps[:, UB:UB + 2].rearrange("p b c -> p (b c)")

        def n1(i, p):
            return i * 2 + p + 1

        def batch(i, p, b):
            return (i * 2 + p) * 4 + b + 1

        with nc.Block() as block:
            @block.sync
            def _(sp):
                sp.dma_start(rgain[:], rank_gain.unsqueeze(0).broadcast_to([P, rank])).then_inc(s.gains, 16)
                sp.dma_start(gain[:], heads_gain.unsqueeze(0).broadcast_to([P, D])).then_inc(s.gains, 16)
                sp.dma_start(rope[:], k.ins["rope32"]).then_inc(s.ropec, 16)
                load_weights(sp, s, raw, w_dram, KT, n_raw)
                for f in range(RT):
                    if f >= 2:
                        sp.wait_ge(s.ulo, f - 1)
                    sp.dma_start(uraw[:, f % 2], u_dram[f]).then_inc(s.ur0 if f % 2 == 0 else s.ur1, 16)

                def pair(i, first, last):
                    for p in range(2):
                        if with_values:
                            wait_then_store(sp, s.vc, n1(i, p), s.begun)
                            sp.dma_start(k.vC[bass.ds(at_tile(i, p) * P, P)], vst[:, p]).then_inc(s.va0 if p == 0 else s.va1, 16)
                        for b in range(4):
                            wait_then_store(sp, s.tc, batch(i, p, b), s.begun)
                            dst = k.qkC[base + 2 * b:base + 2 * b + 2].rearrange("h a r q -> r (h a) q")
                            sp.dma_start(dst[:, :, bass.ds(at_tile(i, p) * P, P)], stage[:, b]).then_inc(
                                (s.qd0, s.qd1, s.qd2, s.qd3)[b], 16)
                walk_pairs(sp, pair)
                for q in (s.qd0, s.qd1, s.qd2, s.qd3):
                    sp.wait_ge(q, 16 * NT)
                if with_values:
                    sp.wait_ge(s.va0, 16 * (NT // 2))
                    sp.wait_ge(s.va1, 16 * (NT // 2))

            @block.tensor
            def _(pe):
                def products(i, p, first):
                    pe.wait_ge(s.h, n1(i, p))
                    if not (first and p < 2):
                        pe.wait_ge(s.low, n1(i, p - 2))
                        if with_values:
                            pe.wait_ge(s.kr, n1(i, p - 2))
                    for f in range(KT):
                        if first and p == 0:
                            pe.wait_ge(s.wlo, f + 1)
                        o = k.ps[:, IB[p % 2], 0:n_cols]
                        pe.matmul(o, hh[:, p % 2, f], wh[:, f], start=(f == 0), stop=False)
                        pe.matmul(o, hh[:, p % 2, f], wl[:, f], start=False, stop=False)
                        mm = pe.matmul(o, hl[:, p % 2, f], wh[:, f], start=False, stop=(f == KT - 1))
                    mm.then_inc(s.mm, 1)

                def turn_low(i, p, free):
                    pe.wait_ge(s.alo, n1(i, p))
                    if free:
                        pe.wait_ge(s.atc, n1(i, p - 1))
                    for a in range(2):
                        for f in range(RT):
                            mm = pe.transpose(k.ps[:, LB + a, f * P:(f + 1) * P], f32(lowc[:, a, f * P:(f + 1) * P]), k.ident[:])
                    mm.then_inc(s.at, 1)

                def up_products(i, p, free, first):
                    pe.wait_ge(s.atc, n1(i, p))
                    if free:
                        pe.wait_ge(s.y if not with_values else s.vc, n1(i, p - 1))
                    if first:
                        pe.wait_ge(s.ulo, RT)
                    for c0, n in UC:
                        for f in range(RT):
                            o, c = ups[:, c0:c0 + n], slice(c0, c0 + n)
                            pe.matmul(o, lowT[:, 0, f], uh[:, f, c], start=(f == 0), stop=False)
                            pe.matmul(o, lowT[:, 0, f], ul[:, f, c], start=False, stop=False)
                            mm = pe.matmul(o, lowT[:, 1, f], uh[:, f, c], start=False, stop=(f == RT - 1))
                    mm.then_inc(s.up, 1)

                def turn_heads(i, p, free):
                    pe.wait_ge(s.lo, n1(i, p))
                    for b in range(4):
                        if free or b >= 2:
                            pe.wait_ge(s.tc, batch(i, p, b - 2))
                        for x in range(4):
                            mm = pe.transpose(k.ps[0:D, TB + b % 2, x * P:(x + 1) * P],
                                              f32(qh[:, 2 * b + x // 2, x % 2]), k.ident[:])
                        mm.then_inc(s.tr, 1)

                products(0, 0, True)

                def pair(i, first, last):
                    for p in range(2):
                        turn_low(i, p, not (first and p == 0))
                        if not (last and p == 1):
                            products(i, p + 1, first)
                        up_products(i, p, not (first and p == 0), first and p == 0)
                        if not (first and p == 0):
                            turn_heads(i, p - 1, not (first and p == 1))
                walk_pairs(pe, pair)
                turn_heads(NT // 2 - 1, 1, True)

            @block.scalar
            def _(act):
                def low_rank(i, p, first):
                    act.wait_ge(s.mm, n1(i, p))
                    if with_values:
                        if not (first and p < 2):
                            act.wait_ge(s.kn, n1(i, p - 2))
                        nc.scalar.copy(kr[:, p % 2], k.ps[:, IB[p % 2], rank:rank + R]).then_inc(s.kr, 1)
                    if not (first and p == 0):
                        act.wait_ge(s.low, n1(i, p - 1))
                    nc.scalar.activation(lsq[:], k.ps[:, IB[p % 2], 0:rank], ACT.Square,
                                         accum_out=lsum[:]).then_inc(s.sql, 1)
                    act.wait_ge(s.sql, n1(i, p))
                    nc.scalar.activation(lr[:], lsum[:], ACT.Sqrt, bias=k.eps[:], scale=1.0 / rank).then_inc(s.rl, 1)

                def stage_low(i, p, free):
                    act.wait_ge(s.at, n1(i, p))
                    if free:
                        act.wait_ge(s.up, n1(i, p - 1))
                    nc.scalar.copy(lowT[:], k.ps[:, LB:LB + 2].rearrange("p a (f q) -> p a f q", q=P)[:, :, 0:RT]).then_inc(s.atc, 1)

                def heads(i, p, first):
                    act.wait_ge(s.up, n1(i, p))
                    if with_values:
                        if not (first and p == 0):
                            act.wait_ge(s.lo, n1(i, p - 1))
                        if not first:
                            act.wait_ge(s.va0 if p == 0 else s.va1, i * 16)
                        up3 = ups.rearrange("p (h d) -> p h d", d=MLA_NOPE + MLA_V)
                        nc.scalar.copy(y[:, :, 0:MLA_NOPE], up3[:, :, 0:MLA_NOPE])
                        nc.scalar.copy(y[:, :, MLA_NOPE:D], kr[:, p:p + 1].broadcast_to([P, H, R])).then_inc(s.kn, 1)
                        nc.scalar.copy(vst[:, p].rearrange("p (h d) -> p h d", d=MLA_V), up3[:, :, MLA_NOPE:]).then_inc(s.vc, 1)
                        act.wait_ge(s.kn, n1(i, p))
                        if not (first and p == 0):
                            act.wait_ge(s.red, n1(i, p - 1))
                        nc.scalar.activation(sq[:], y[:], ACT.Square).then_inc(s.sqd, 1)
                    else:
                        if not (first and p == 0):
                            act.wait_ge(s.red, n1(i, p - 1))
                        nc.scalar.activation(sq[:], ups[:, 0:H * D].rearrange("p (h d) -> p h d", d=D), ACT.Square).then_inc(s.sqd, 1)

                def roots(i, p):
                    act.wait_ge(s.red, n1(i, p))
                    nc.scalar.activation(rs[:], rs[:], ACT.Sqrt, bias=k.eps[:], scale=1.0 / D).then_inc(s.root, 1)

                def stage_heads(i, p, free):
                    for b in range(4):
                        act.wait_ge(s.tr, batch(i, p, b))
                        if free:
                            act.wait_ge((s.qd0, s.qd1, s.qd2, s.qd3)[b], at_tile(i, p) * 16)
                        nc.scalar.copy(stage[:, b], k.ps[0:D, TB + b % 2].rearrange("p (x q) -> p x q", q=P)).then_inc(s.tc, 1)

                cut_hi(nc, act, s, raw, wh, KT, n_raw)
                for f in range(RT):
                    act.wait_ge(s.ur0 if f % 2 == 0 else s.ur1, 16 * (f // 2 + 1))
                    nc.scalar.copy(uh[:, f], uraw[:, f % 2]).then_inc(s.uhi, 1)

                low_rank(0, 0, True)

                def pair(i, first, last):
                    for p in range(2):
                        stage_low(i, p, not (first and p == 0))
                        if not (last and p == 1):
                            low_rank(i, p + 1, first)
                        heads(i, p, first)
                        if not (first and p == 0):
                            stage_heads(i, p - 1, not (first and p == 1))
                        roots(i, p)
                walk_pairs(act, pair)
                stage_heads(NT // 2 - 1, 1, True)

            @block.vector
            def _(dve):
                for w in range(2):
                    dst = modt[:, 0:LT, :, :] if w == 0 else modt[:, LT:NT, :, :]
                    n = LT if w == 0 else NT - LT
                    for c, part in ((0, 1), (1, 0)):
                        m = nc.vector.tensor_copy(dst[:, :, c], k.mods[:, layer, part, :, w].unsqueeze(1).broadcast_to([P, n, KT]))
                    m.then_inc(s.modt, 1)
                dve.wait_ge(s.gains, 32)
                nc.vector.tensor_scalar(gain[:], gain[:], gain_scale, None, ALU.mult).then_inc(s.modt, 1)

                def cut(i, p, first):
                    dve.wait_ge(s.fmod, n1(i, p))
                    if not (first and p < 2):
                        dve.wait_ge(s.mm, n1(i, p - 2))
                    nc.vector.tensor_copy(hh[:, p % 2], h[:]).then_inc(s.ht, 1)
                    dve.wait_ge(s.ht, n1(i, p))
                    nc.vector.tensor_tensor(hl[:, p % 2], h[:], f32(hh[:, p % 2]), ALU.subtract).then_inc(s.h, 1)

                def low_rank(i, p, first):
                    me = n1(i, p)
                    dve.wait_ge(s.rl, me)
                    nc.vector.reciprocal(lr[:], lr[:]).then_inc(s.rli, 1)
                    dve.wait_ge(s.rli, me)
                    if not (first and p == 0):
                        dve.wait_ge(s.alo, n1(i, p - 1))
                    nc.vector.scalar_tensor_tensor(out=low[:], in0=k.ps[:, IB[p % 2], 0:rank], scalar=lr[:, 0:1], in1=rgain[:],
                                                   op0=ALU.mult, op1=ALU.mult).then_inc(s.low, 1)
                    dve.wait_ge(s.low, me)
                    if not (first and p == 0):
                        dve.wait_ge(s.at, n1(i, p - 1))
                    nc.vector.tensor_copy(lowc[:, 0], low[:]).then_inc(s.ah, 1)
                    dve.wait_ge(s.ah, me)
                    nc.vector.tensor_tensor(lowc[:, 1], low[:], f32(lowc[:, 0]), ALU.subtract).then_inc(s.alo, 1)

                def heads(i, p, first):
                    me = n1(i, p)
                    dve.wait_ge(s.sqd, me)
                    nc.vector.tensor_reduce(rs[:], sq[:], AX.X, ALU.add).then_inc(s.red, 1)
                    src = y[:] if with_values else ups[:, 0:H * D].rearrange("p (h d) -> p h d", d=D)
                    if not with_values and not (first and p == 0):
                        dve.wait_ge(s.lo, n1(i, p - 1))
                    nc.vector.tensor_tensor(y[:], src, gain[:].unsqueeze(1).broadcast_to([P, H, D]), ALU.mult).then_inc(s.y, 1)
                    dve.wait_ge(s.root, me)
                    nc.vector.reciprocal(rs[:], rs[:]).then_inc(s.ri, 1)
                    dve.wait_ge(s.ri, me)
                    dve.wait_ge(s.y, me)
                    nc.vector.tensor_tensor(y[:], y[:], rs[:].unsqueeze(2).broadcast_to([P, H, D]), ALU.mult).then_inc(s.yn, 1)
                    dve.wait_ge(s.yn, me)
                    if not (first and p == 0):
                        dve.wait_ge(s.yf, n1(i, p - 1))
                    t = bass.ds(at_tile(i, p), 1)
                    rot = y[:, :, MLA_NOPE:D]
                    nc.vector.tensor_tensor(w_[:], rot, rope[:, 0, t].broadcast_to([P, H, R]), ALU.mult).then_inc(s.w, 1)
                    v5 = lambda ap: ap.rearrange("p h (a b d) -> p h a b d", a=2, b=2)
                    sin = v5(rope[:, 1, t])
                    for b in range(2):
                        ins = nc.vector.tensor_tensor(v5(u_[:])[:, :, :, b], v5(rot)[:, :, :, 1 - b],
                                                      sin[:, :, :, b].broadcast_to([P, H, 2, R // 4]), ALU.mult)
                    ins.then_inc(s.u, 1)
                    dve.wait_ge(s.w, me)
                    dve.wait_ge(s.u, me)
                    nc.vector.tensor_tensor(rot, w_[:], u_[:], ALU.add).then_inc(s.yf, 1)
                    dve.wait_ge(s.yf, me)
                    if not (first and p == 0):
                        dve.wait_ge(s.tr, batch(i, p - 1, 3))
                    nc.vector.tensor_copy(qh[:, :, 0], y[:]).then_inc(s.hi, 1)
                    dve.wait_ge(s.hi, me)
                    nc.vector.tensor_tensor(qh[:, :, 1], y[:], f32(qh[:, :, 0]), ALU.subtract).then_inc(s.lo, 1)

                cut_lo(nc, dve, s, raw, wh, wl, KT, n_raw)
                cut(0, 0, True)
                cut(0, 1, True)
                for f in range(RT):
                    dve.wait_ge(s.uhi, f + 1)
                    nc.vector.tensor_tensor(ul[:, f], uraw[:, f % 2], f32(uh[:, f]), ALU.subtract).then_inc(s.ulo, 1)
                dve.wait_ge(s.modt, 3)
                dve.wait_ge(s.ropec, 16)

                low_rank(0, 0, True)

                def pair(i, first, last):
                    for p in range(2):
                        if not (last and p == 1):
                            low_rank(i, p + 1, first)
                        if not last:
                            cut(i, p + 2, first)
                        heads(i, p, first)
                walk_pairs(dve, pair)

            @block.gpsimd
            def _(pool):
                pool.wait_ge(s.modt, 2)
                modulated(k, pool, s, h, modt, 0, 0, True)
                modulated(k, pool, s, h, modt, 0, 1, False)

                def pair(i, first, last):
                    for p in range(2):
                        if not last:
                            modulated(k, pool, s, h, modt, i, p + 2, False)
                walk_pairs(pool, pair)


class BiasSpread:
    NAMES = "zero rows rowsR wide wideR turned bias"
    HR = NA_HEADS * RPB_R

    def __init__(self, k, rpb):
        self.k, self.rpb = k, rpb

    def tiles(self, sb):
        self.rows, self.rowsR = sb("pad_rows", [self.HR, PADW + 1]), sb("pad_rowsR", [self.HR, PADW + 1])
        self.wide = sb("pad_wide", [self.HR, GRID_W * (PADW + 1)])
        self.turned = sb("pad_turned", [self.HR, GRID_W, GRID_W])

    def falling(self):
        return self.wide[:, GRID_W - 1:GRID_W - 1 + GRID_W * PADW].rearrange("r (c j) -> r c j", c=GRID_W)[:, :, :GRID_W]

    def on_gpsimd(self, s, pool):
        nc = self.k.nc
        copies = self.wide[:].rearrange("r (c j) -> r c j", c=GRID_W)
        nc.gpsimd.memset(self.rows[:], 0.0).then_inc(s.zero, 1)
        nc.gpsimd.memset(self.rowsR[:], 0.0).then_inc(s.zero, 1)
        pool.wait_ge(s.rows, 16)
        nc.gpsimd.tensor_copy(copies, self.rows[:].unsqueeze(1).to_broadcast([self.HR, GRID_W, PADW + 1])).then_inc(s.wide, 1)
        pool.wait_ge(s.rowsR, 16 * RPB_R)
        pool.wait_ge(s.bias, 16)
        nc.gpsimd.tensor_copy(copies, self.rowsR[:].unsqueeze(1).to_broadcast([self.HR, GRID_W, PADW + 1])).then_inc(s.wideR, 1)
        pool.wait_ge(s.wideR, 1)
        nc.gpsimd.tensor_copy(self.turned[:], self.falling().rearrange("r c j -> r j c")).then_inc(s.turned, 1)

    def loads(self, s, sp):
        sp.wait_ge(s.zero, 2)
        mid = (PADW - RPB_C) // 2
        sp.dma_start(self.rows[:, mid:mid + RPB_C], self.rpb.rearrange("h r c -> (h r) c")).then_inc(s.rows, 16)
        for r in range(RPB_R):
            at = (RPB_R - 1 - r) * NA_HEADS
            sp.dma_start(self.rowsR[at:at + NA_HEADS, mid:mid + RPB_C], self.rpb[:, r]).then_inc(s.rowsR, 16)
        sp.wait_ge(s.wide, 1)
        sp.dma_start(self.k.bias.rearrange("c r k -> r c k"), self.falling()).then_inc(s.bias, 16)

    def last_store(self, s, sp):
        sp.wait_ge(s.turned, 1)
        sp.dma_start(self.k.biasT[:, 0:RPB_R].rearrange("k r h c -> (r h) k c"), self.turned[:]).then_inc(s.bias, 16)


class Piece:

    def __init__(self, q, runs, masks=(), bias=None):
        self.q, self.masks, self.bias = q, masks, bias
        self.tiles, self.mm, col = [], [], 0
        for key, n in runs:
            for c in range(0, n, P):
                self.tiles.append(((key + c) // P, min(P, n - c)))
            while n:
                m = min(n, 512 - col % 512)
                if self.mm and self.mm[-1][0] + self.mm[-1][2] == col and self.mm[-1][1] + self.mm[-1][2] == key and col % 512:
                    self.mm[-1] = (self.mm[-1][0], self.mm[-1][1], self.mm[-1][2] + m)
                else:
                    self.mm.append((col, key, m))
                col, key, n = col + m, key + m, n - m
        self.width = col


def window_pieces():
    out = []
    for q in range(LT):
        lo, hi = max(0, q - 1), min(LT, q + 2)
        masks = ([(0, CTX)] if q > 0 else []) + ([(1, CTX + (q + 1 - lo) * P)] if q < LT - 1 else [])
        out.append(Piece(q, [(SEQ, CTX), (lo * P, (hi - lo) * P)], masks=masks))
    return out + [Piece(q, [(SEQ, CTX)]) for q in range(LT, NT)]


def neighbour_pieces():
    out = []
    for q in range(LT):
        rows = [min(max(r - NA_ROWS // 2, 0), 2 * LT - NA_ROWS) for r in (2 * q, 2 * q + 1)]
        n = rows[1] - rows[0] + NA_ROWS
        n += n % 2
        out.append(Piece(q, [(SEQ, CTX), (rows[0] * GRID_W, n * GRID_W)],
                         bias=(rows[0] - 2 * q + NA_ROWS - 1, n, rows[1] > rows[0])))
    return out


def walk(eng, n, body):
    body(0, True, False)
    if n > 2:
        with eng.Fori(1, n - 1) as i:
            body(i, False, False)
    body(n - 1, False, True)


class Step:

    def __init__(self, block, key, q, n, first, last):
        self.block, self.key, self.q, self.n, self.first, self.last = block, key, q, n, first, last


def steps_of_head(pieces):
    seen = [[t for t, _ in u.tiles] for u in pieces]
    out, blocks = [], []
    for b, q0 in enumerate(range(0, len(pieces), 4)):
        tiles = range(q0, min(q0 + 4, len(pieces)))
        blocks.append((q0, len(tiles)))
        for key in [LT] + list(range(LT)) + list(range(LT + 1, NT)):
            qs = [q for q in tiles if key in seen[q]]
            if qs:
                assert qs == list(range(qs[0], qs[-1] + 1))
                out.append(Step(b, key, qs[0], len(qs), key == LT, key == NT - 1))
    return out, blocks


def attend(k, name, pieces, heads, load_head, parts, v_width, mix, mix_col, sink=None, bias=None, beside=None):
    nc = k.nc
    NQ = len(pieces)
    PAIRS = heads // 2
    BANK = 512
    head_steps, head_blocks = steps_of_head(pieces)
    NS, NB = len(head_steps), len(head_blocks)
    V, NU, BLOCKS = 2 * NS, 2 * NQ, 2 * NB
    PT = 4
    assert V % PT == 0
    wide = max(p.width for p in pieces)
    RB = -(-wide // BANK)
    SB = 2 if RB == 3 else 4
    OB, TB = 6, 7
    loads = load_head(None, None, None, None, None, None)
    last_step = [max(x for x in range(V) if (x // NS) * NB + head_steps[x % NS].block == b) for b in range(BLOCKS)]
    first_step = [0] + [x + 1 for x in last_step[:-1]]
    place = [V] * NU
    for u in 2 * list(reversed(range(NU))):
        b = (u // NQ) * NB + u % NQ // 4
        following = place[u + 1] if u + 1 < NU else place[0] + V
        place[u] = min(first_step[b] - 2, following - max(1, NS // NQ))

    def maxima_at(x):
        return [(n, u) for n in range(2) for u in range(NU) if place[u] + n * V == x]

    def blocks_at(x, later):
        return [(n, b) for n in range(2) for b in range(BLOCKS) if last_step[b] + later == x + n * V]

    def after(later):
        return [b for b in range(BLOCKS) if last_step[b] + later >= V]

    names = "ld0 ld1 st0 st1 tab rt vone R top nm sm dg S ex pv ocp oT es ls ri o mk bl0 bl1 bh bp"
    if beside is not None:
        names += " " + beside.NAMES
    with phase(nc, name, names) as s, ExitStack() as st:
        def sb(nm, shape, dt=F32):
            return st.enter_context(nc.sbuf_tensor(f"{name}_{nm}", shape, dt))
        rows = MLA_QK if parts == "three" else P
        q_sb = sb("q", [rows, 2, 2 if parts == "three" else 1, TOK], F32R)
        k_sb = sb("k", [rows, 2, 2, TOK], F32R)
        v_sb = sb("v", [P, 2, NT, v_width + 1])
        pt_sb = sb("pt", [P, PT, BANK])
        diag = sb("diag", [P, BLOCKS, 4, P], F32R)
        negmax = sb("nm", [P, BLOCKS, 4], F32R if sink is not None else F32)
        oT_sb = sb("oT", [v_width + 1, 2, BANK])
        top, rowsum = sb("top", [P, 2]), sb("ls", [P, 4])
        o_sb = sb("o", [P, 2, NQ, v_width])
        if sink is not None:
            sinkm, esink = sb("sinkm", [P, BLOCKS, 4]), sb("es", [P, BLOCKS, 4])
            wmask, wband = sb("wm", [P, 2, P], F32R), sb("wb", [P, 3, P], F32R)
            sinks = sb("sinks", [P, heads])
        if bias is not None:
            BR, ND = 2 * NA_ROWS - 2, NA_ROWS - 1
            raw, rawT = sb("br", [P, 2, BR, GRID_W]), sb("brT", [P, 2, ND, P])
            b_sb, bT = sb("b", [P, 2, BR, GRID_W], F32R), sb("bT", [P, 2, 2, ND, P], F32R)
            cmask, cmaskT = sb("cm", [P, GRID_W]), sb("cmT", [P, P])
            rmask = sb("rm", [P, 4, P], F32R)
        mtab = sb("mtab", [P, 5, P]) if sink is not None or bias is not None else None
        tables = 3 if sink is not None or bias is not None else 0
        if beside is not None:
            beside.tiles(sb)

        def rough_scores():
            return k.ps[:, 0:RB].rearrange("p b c -> p (b c)")

        def scores(x):
            return k.ps[:, RB + x % SB]

        def nth(i, x):
            return i * V + x + 1

        def unit_nth(i, u):
            return i * NU + u + 1

        def block_nth(i, b):
            return i * BLOCKS + b + 1

        def rough_added(p, u):
            out = [(c, P, wmask[:, m]) for m, c in u.masks]
            if u.bias:
                e0, n, edge = u.bias
                flat = b_sb[:, p].rearrange("p e c -> p (e c)")
                c, end = CTX, CTX + n * GRID_W
                while c < end:
                    w = min(end - c, BANK - c % BANK)
                    at = (e0 - 1) * GRID_W + c - CTX
                    out.append((c, w, flat[:, at:at + w]))
                    c += w
                if edge:
                    out += [(CTX, P, rmask[:, 0]), (end - P, P, rmask[:, 1])]
            return out

        def added(p, t):
            out = []
            if t.key < LT and sink is not None:
                e = t.q - t.key + 1
                out.append((t.q, t.n, wband[:, e:e + t.n].rearrange("p e q -> p (e q)")))
            if t.key < LT and bias is not None:
                e = t.q - t.key + ND // 2
                for part in range(2):
                    out.append((t.q, t.n, bT[:, p, part, e:e + t.n].rearrange("p e q -> p (e q)")))
                for q in range(t.q, t.q + t.n):
                    if pieces[q].bias[2] and abs(t.key - q) == 2:
                        out.append((q, 1, rmask[:, 2 if t.key < q else 3]))
            return out

        with nc.Block() as block:
            @block.sync
            def _(sp):
                if sink is not None:
                    sp.dma_start(mtab[:, 0:2], k.ins["wmask"]).then_inc(s.tab, 16)
                    sp.dma_start(mtab[:, 2:5], k.ins["wband"]).then_inc(s.tab, 16)
                    sp.dma_start(sinks[:], sink.unsqueeze(0).broadcast_to([P, heads])).then_inc(s.tab, 16)
                if bias is not None:
                    sp.dma_start(cmask[:], k.ins["cmask"]).then_inc(s.tab, 16)
                    sp.dma_start(cmaskT[:], k.ins["cmaskT"]).then_inc(s.tab, 16)
                    sp.dma_start(mtab[:, 0:4], k.ins["rmask"]).then_inc(s.tab, 16)

                def fetch(i, p, free):
                    if bias is not None:
                        if free:
                            wait_then_store(sp, s.bp, (i - 1) * 2 + p + 1, s.mk)
                        bias(sp, i, p, raw[:, p], rawT[:, p], s.bl0 if p == 0 else s.bl1)
                    if free:
                        wait_then_store(sp, s.pv, (i - 1) * V + (p + 1) * NS, s.mk)
                    load_head(sp, i, p, (q_sb[:, p], k_sb[:, p], v_sb[:, p, :, 0:v_width]), None, s.ld0 if p == 0 else s.ld1)

                def pair(i, first, last):
                    if first:
                        fetch(0, 0, False)
                        fetch(0, 1, False)
                        if beside is not None:
                            beside.loads(s, sp)
                    for p in range(2):
                        if not last:
                            fetch(i + 1, p, True)
                        wait_then_store(sp, s.o, i * BLOCKS + (p + 1) * NB, s.mk)
                        dst = mix.rearrange("(t p) d -> p t d", p=P)[:, 0:NQ, bass.ds((i * 2 + p) * v_width + mix_col, v_width)]
                        sp.dma_start(dst, o_sb[:, p]).then_inc(s.st0 if p == 0 else s.st1, 16)
                    if first and beside is not None:
                        beside.last_store(s, sp)
                walk(sp, PAIRS, pair)
                if beside is not None:
                    sp.wait_ge(s.bias, 32)
                sp.wait_ge(s.st0, 16 * PAIRS)
                sp.wait_ge(s.st1, 16 * PAIRS)

            @block.tensor
            def _(pe):
                if tables:
                    pe.wait_ge(s.rt, 1 if sink is None else 2)
                pe.wait_ge(s.vone, 1)

                def rough(i, u, free):
                    p, piece = u // NQ, pieces[u % NQ]
                    if u % NQ == 0:
                        pe.wait_ge(s.ld0 if p == 0 else s.ld1, i * 16 * loads + 16 * loads)
                        if bias is not None:
                            pe.wait_ge(s.bp, i * 2 + p + 1)
                    if free:
                        pe.wait_ge(s.top, unit_nth(i, u - 1))
                    for c, key, n in piece.mm:
                        more = [m for m in rough_added(p, piece) if c <= m[0] < c + n]
                        mm = pe.matmul(rough_scores()[:, c:c + n], q_sb[:, p, 0, piece.q * P:(piece.q + 1) * P],
                                       k_sb[:, p, 0, key:key + n], start=True, stop=not more)
                        for y, (col, w, addend) in enumerate(more):
                            mm = pe.matmul(rough_scores()[:, col:col + w], k.identr[:], addend, start=False, stop=(y == len(more) - 1))
                    mm.then_inc(s.R, 1)

                def score(i, x, first):
                    p, t = x // NS, head_steps[x % NS]
                    b = p * NB + t.block
                    q0, nq = head_blocks[t.block]
                    out = scores(x)[:, 0:t.n * P]
                    prods = ((0, 0), (1, 0), (0, 1)) if parts == "three" else ((0, 0), (1, 0))
                    if not (first and x < SB):
                        pe.wait_ge(s.ex, nth(i, x - SB))
                    for y, (kp, qp) in enumerate(prods):
                        pe.matmul(out, k_sb[:, p, kp, t.key * P:(t.key + 1) * P], q_sb[:, p, qp, t.q * P:(t.q + t.n) * P],
                                  start=(y == 0), stop=False)
                    for q, n, addend in added(p, t):
                        pe.matmul(scores(x)[:, (q - t.q) * P:(q - t.q + n) * P], k.identr[:], addend, start=False, stop=False)
                    if t.first:
                        pe.wait_ge(s.dg, unit_nth(i, p * NQ + q0 + nq - 1))
                    pe.matmul(out, k.onesr[:], diag[:, b, t.q - q0:t.q - q0 + t.n].rearrange("p e q -> p (e q)"),
                              start=False, stop=True).then_inc(s.S, 1)

                def values(i, x, first):
                    x = x % V
                    p, t = x // NS, head_steps[x % NS]
                    b = p * NB + t.block
                    q0 = head_blocks[t.block][0]
                    pe.wait_ge(s.ex, nth(i, x))
                    if t.first and not (first and b == 0):
                        pe.wait_ge(s.ocp, block_nth(i, b - 1))
                    pe.matmul(k.ps[0:v_width + 1, OB, (t.q - q0) * P:(t.q - q0 + t.n) * P], v_sb[:, p, t.key],
                              pt_sb[:, x % PT, 0:t.n * P], start=t.first, stop=t.last).then_inc(s.pv, 1)

                def turn(i, b, first):
                    pe.wait_ge(s.ocp, block_nth(i, b))
                    if not (first and b == 0):
                        pe.wait_ge(s.o, block_nth(i, b - 1))
                    for j in range(head_blocks[b % NB][1]):
                        mm = pe.transpose(k.ps[:, TB, j * P:j * P + v_width + 1], oT_sb[:, b % 2, j * P:(j + 1) * P],
                                          k.ident[0:v_width + 1, 0:v_width + 1])
                    mm.then_inc(s.oT, 1)

                def pair(i, first, last):
                    for x in range(V):
                        if first and x == 0:
                            for u in range(NU):
                                if place[u] < 0:
                                    rough(0, u, u > 0)
                        score(i, x, first)
                        for n, u in maxima_at(x):
                            if not (last and n):
                                rough(i + n, u, True)
                        for n, b in blocks_at(x, 3):
                            if not (first and n):
                                turn(i - n, b, first)
                        if not (first and x < 2):
                            values(i - 1 if x < 2 else i, x - 2, first)
                walk(pe, PAIRS, pair)
                values(PAIRS - 1, V - 2, False)
                values(PAIRS - 1, V - 1, False)
                for b in after(3):
                    turn(PAIRS - 1, b, False)

            @block.scalar
            def _(act):
                def sink_exp(i, b):
                    act.wait_ge(s.sm, block_nth(i, b))
                    n = head_blocks[b % NB][1]
                    nc.scalar.activation(esink[:, b, 0:n], sinkm[:, b, 0:n], ACT.Exp).then_inc(s.es, 1)

                def exps(i, x, first):
                    t = head_steps[x % NS]
                    act.wait_ge(s.S, nth(i, x))
                    if not (first and x < PT):
                        act.wait_ge(s.pv, nth(i, x - PT))
                    nc.scalar.activation(pt_sb[:, x % PT, 0:t.n * P], scores(x)[:, 0:t.n * P], ACT.Exp).then_inc(s.ex, 1)

                def take_sums(i, b, first):
                    act.wait_ge(s.pv, nth(i, last_step[b]))
                    if not (first and b < 2):
                        act.wait_ge(s.oT, block_nth(i, b - 2))
                    n = head_blocks[b % NB][1] * P
                    nc.scalar.copy(oT_sb[:, b % 2, 0:n], k.ps[0:v_width + 1, OB, 0:n]).then_inc(s.ocp, 1)

                def pair(i, first, last):
                    for x in range(V):
                        if sink is not None and x in first_step:
                            sink_exp(i, first_step.index(x))
                        exps(i, x, first)
                        for n, b in blocks_at(x, 2):
                            if not (first and n):
                                take_sums(i - n, b, first and not n)
                walk(act, PAIRS, pair)
                for b in after(2):
                    take_sums(PAIRS - 1, b, False)

            @block.vector
            def _(dve):
                nc.vector.memset(v_sb[:, :, :, v_width:], 1.0).then_inc(s.vone, 1)
                if tables:
                    dve.wait_ge(s.tab, 16 * tables)
                if sink is not None:
                    nc.vector.tensor_copy(wmask[:], mtab[:, 0:2]).then_inc(s.rt, 1)
                    nc.vector.tensor_copy(wband[:], mtab[:, 2:5]).then_inc(s.rt, 1)
                if bias is not None:
                    nc.vector.tensor_copy(rmask[:], mtab[:, 0:4]).then_inc(s.rt, 1)

                def head_bias(i, p, free):
                    dve.wait_ge(s.bl0 if p == 0 else s.bl1, i * 6 * 16 + 6 * 16)
                    if free:
                        dve.wait_ge(s.S, nth(i - 1, (p + 1) * NS - 1))
                    nc.vector.tensor_tensor(b_sb[:, p], raw[:, p], cmask[:].unsqueeze(1).broadcast_to([P, BR, GRID_W]), ALU.add)
                    nc.vector.tensor_tensor(rawT[:, p], rawT[:, p], cmaskT[:].unsqueeze(1).broadcast_to([P, ND, P]),
                                            ALU.add).then_inc(s.bh, 1)
                    dve.wait_ge(s.bh, i * 4 + 2 * p + 1)
                    nc.vector.tensor_copy(bT[:, p, 0], rawT[:, p]).then_inc(s.bh, 1)
                    dve.wait_ge(s.bh, i * 4 + 2 * p + 2)
                    nc.vector.tensor_tensor(bT[:, p, 1], rawT[:, p], f32(bT[:, p, 0]), ALU.subtract).then_inc(s.bp, 1)

                def maximum(i, u, first):
                    p, q = u // NQ, u % NQ
                    b, j = p * NB + q // 4, q % 4
                    if bias is not None and q == 0:
                        head_bias(i, p, not first)
                    dve.wait_ge(s.R, unit_nth(i, u))
                    here, m = rough_scores()[:, 0:pieces[q].width], negmax[:, b, j:j + 1]
                    if sink is not None:
                        nc.vector.tensor_reduce(top[:, u % 2:u % 2 + 1], here, AX.X, ALU.max).then_inc(s.top, 1)
                        dve.wait_ge(s.top, unit_nth(i, u))
                        nc.vector.tensor_scalar(m, top[:, u % 2:u % 2 + 1], sinks[:, bass.ds(i * 2 + p, 1)], -1.0,
                                                ALU.max, ALU.mult).then_inc(s.nm, 1)
                        dve.wait_ge(s.nm, unit_nth(i, u))
                    else:
                        nc.vector.tensor_reduce(m, here, AX.X, ALU.max, negate=True).then_inc(s.top, 1)
                        dve.wait_ge(s.top, unit_nth(i, u))
                    if not first:
                        dve.wait_ge(s.S, nth(i - 1, last_step[b]))
                    nc.vector.tensor_scalar(diag[:, b, j], k.ident[:], f32(m), None, ALU.mult).then_inc(s.dg, 1)
                    n = head_blocks[b % NB][1]
                    if sink is not None and j == n - 1:
                        if not first:
                            dve.wait_ge(s.es, block_nth(i - 1, b))
                        nc.vector.tensor_scalar(sinkm[:, b, 0:n], f32(negmax[:, b, 0:n]), sinks[:, bass.ds(i * 2 + p, 1)], None,
                                                ALU.add).then_inc(s.sm, 1)

                def result(i, b, first):
                    p, (q0, n) = b // NB, head_blocks[b % NB]
                    me = block_nth(i, b)
                    turned = k.ps[:, TB].rearrange("p (j c) -> p j c", c=P)[:, 0:n]
                    dve.wait_ge(s.oT, me)
                    total = turned[:, :, v_width]
                    if sink is not None:
                        dve.wait_ge(s.es, me)
                        nc.vector.tensor_tensor(rowsum[:, 0:n], total, esink[:, b, 0:n], ALU.add).then_inc(s.ls, 1)
                        dve.wait_ge(s.ls, me)
                        total = rowsum[:, 0:n]
                    nc.vector.reciprocal(rowsum[:, 0:n], total).then_inc(s.ri, 1)
                    dve.wait_ge(s.ri, me)
                    if not first and b % NB == 0:
                        dve.wait_ge(s.st0 if p == 0 else s.st1, i * 16)
                    nc.vector.tensor_tensor(o_sb[:, p, q0:q0 + n], turned[:, :, 0:v_width],
                                            rowsum[:, 0:n].unsqueeze(2).broadcast_to([P, n, v_width]), ALU.mult).then_inc(s.o, 1)

                def pair(i, first, last):
                    for x in range(V):
                        if first and x == 0:
                            for u in range(NU):
                                if place[u] < 0:
                                    maximum(0, u, True)
                        for n, u in maxima_at(x):
                            if not (last and n):
                                maximum(i + n, u, first and not n)
                        for n, b in blocks_at(x, 3):
                            if not (first and n):
                                result(i - n, b, first)
                walk(dve, PAIRS, pair)
                for b in after(3):
                    result(PAIRS - 1, b, False)

            @block.gpsimd
            def _(pool):
                if beside is not None:
                    beside.on_gpsimd(s, pool)


def stacked_loader(qk, q_base, k_index, v_dram, v_index, v_width):
    def load(sp, i, p, places, _, sem):
        if sp is None:
            return 6
        q_sb, k_sb, v_sb = places
        h, kh, vh = i * 2 + p, k_index(i, p), v_index(i, p)
        one = lambda x: qk[bass.ds(x, 1)].squeeze(0)
        sp.dma_start(f32(q_sb[:, 0]), one(h + q_base)).then_inc(sem, 16)
        for part in range(2):
            for half in range(2):
                sp.dma_start(f32(k_sb[half * HD:(half + 1) * HD, part]), one(kh)[part * HD:(part + 1) * HD]).then_inc(sem, 16)
        sp.dma_start(v_sb, v_dram.rearrange("(t p) d -> p t d", p=P)[:, :, bass.ds(vh * v_width, v_width)]).then_inc(sem, 16)
    return load


def parts_loader(k):
    def load(sp, i, p, places, _, sem):
        if sp is None:
            return 3
        q_sb, k_sb, v_sb = places
        h = i * 2 + p
        one = lambda x: k.qkC[bass.ds(x, 1)].squeeze(0).rearrange("a r q -> r a q")
        sp.dma_start(f32(q_sb), one(h)).then_inc(sem, 16)
        sp.dma_start(f32(k_sb), one(h + MLA_HEADS)).then_inc(sem, 16)
        sp.dma_start(v_sb, k.vC.rearrange("(t p) d -> p t d", p=P)[:, :, bass.ds(h * MLA_V, MLA_V)]).then_inc(sem, 16)
    return load


def bias_loader(k):
    def load(sp, i, p, place, placeT, sem):
        first_row = (i * 2 + p) * RPB_R + 1
        for q in range(2):
            sp.dma_start(place[q * GRID_W:(q + 1) * GRID_W],
                         k.bias[:, bass.ds(first_row - q, 2 * NA_ROWS - 2)]).then_inc(sem, 16)
            for key in range(2):
                first = 1 + q - key
                rows = k.biasT[:, first:first + 2 * NA_ROWS - 2].rearrange("k (d two) h c -> k d two h c", two=2)[:, :, 0]
                sp.dma_start(placeT[key * GRID_W:(key + 1) * GRID_W, :, q * GRID_W:(q + 1) * GRID_W],
                             rows[:, :, bass.ds(i * 2 + p, 1)].squeeze(2)).then_inc(sem, 16)
    return load


def attend_diff(k, name, ins):
    nc = k.nc
    pieces = [Piece(q, [(0, TOK)]) for q in range(LT)] + [Piece(q, [(SEQ, CTX)]) for q in range(LT, NT)]
    NQ, V, PAIRS, DV = NT, 2 * NT, DIFF_HEADS // 2, 2 * HD
    names = "ld0 ld1 lam lp lr le l1 nl S mx ex r1 c mix T ev pv r0 o st0 st1"
    with phase(nc, name, names) as s, ExitStack() as st:
        def sb(nm, shape, dt=F32):
            return st.enter_context(nc.sbuf_tensor(f"{name}_{nm}", shape, dt))
        q_sb = sb("q", [P, 2, 2, TOK], F32R)
        k_sb = sb("k", [P, 2, 2, 2, TOK], F32R)
        v_sb = sb("v", [P, 2, NT, DV])
        e_sb = sb("e", [P, 3, 2, TOK])
        pt_sb = sb("pt", [P, 2, NT, P])
        negmax = sb("nm", [P, 2, 2])
        rowsum = sb("ls", [P, 4, 2])
        r1, coef, r0 = sb("r1", [P, 2]), sb("c", [P, 2]), sb("r0", [P, 2])
        o_sb = sb("o", [P, 2, NQ, DV])
        lam4, lprod, lsum, nlam = sb("lam4", [P, 4, HD]), sb("lprod", [P, 2, HD]), sb("lsum", [P, 2]), sb("nlam", [P, 1])
        TB, OB = 6, 7
        def scores(b):
            return k.ps[:, 3 * b:3 * b + 3].rearrange("p b c -> p (b c)")

        def nth(i, v):
            return i * V + v + 1

        def map_nth(i, v, m):
            return (i * V + v) * 2 + m + 1

        def turns(v):
            return -(-len(pieces[v % NQ].tiles) // 4)

        def turn_nth(i, v, c):
            return i * sum(turns(x) for x in range(V)) + sum(turns(x) for x in range(v)) + c + 1

        N = PAIRS * V

        def unit(n):
            return n // V, n % V

        def exp_place(i, v):
            return (i * V + v) % 3

        with nc.Block() as block:
            @block.sync
            def _(sp):
                sp.dma_start(lam4[:], ins["diff_lam"][0].unsqueeze(0).broadcast_to([P, 4, HD])).then_inc(s.lam, 16)

                def fetch(i, p):
                    sem = s.ld0 if p == 0 else s.ld1
                    hd = i * 2 + p
                    for m in range(2):
                        sp.dma_start(f32(q_sb[:, p, m]), k.qkA[hd * 2 + m]).then_inc(sem, 16)
                        for part in range(2):
                            for half in range(2):
                                sp.dma_start(f32(k_sb[half * HD:(half + 1) * HD, p, m, part]),
                                             k.qkA[8 + hd * 2 + m, part * HD:(part + 1) * HD]).then_inc(sem, 16)
                    sp.dma_start(v_sb[:, p], k.vA.rearrange("(t p) d -> p t d", p=P)[:, :, hd * DV:(hd + 1) * DV]).then_inc(sem, 16)

                fetch(0, 0)
                fetch(0, 1)
                for i in range(PAIRS):
                    for p in range(2):
                        sp.wait_ge(s.o, i * V + (p + 1) * NQ)
                        if i + 1 < PAIRS:
                            fetch(i + 1, p)
                        dst = k.mix[0].rearrange("(t p) d -> p t d", p=P)[:, :, (i * 2 + p) * DV:(i * 2 + p + 1) * DV]
                        sp.dma_start(dst, o_sb[:, p]).then_inc(s.st0 if p == 0 else s.st1, 16)
                sp.wait_ge(s.st0, 16 * PAIRS)
                sp.wait_ge(s.st1, 16 * PAIRS)

            @block.tensor
            def _(pe):
                def score(i, v, m):
                    i, v = i + v // V, v % V
                    p, u = v // NQ, pieces[v % NQ]
                    if v % NQ == 0 and m == 0:
                        pe.wait_ge(s.ld0 if p == 0 else s.ld1, (i + 1) * 16 * 11)
                    if i or v:
                        pe.wait_ge(s.ex, map_nth(i, v - 1, m))
                    for c, key, n in u.mm:
                        for x in range(2):
                            mm = pe.matmul(scores(m)[:, c:c + n], q_sb[:, p, m, u.q * P:(u.q + 1) * P],
                                           k_sb[:, p, m, x, key:key + n], start=(x == 0), stop=(x == 1))
                    mm.then_inc(s.S, 1)

                def turn(i, v, c):
                    if c == 0:
                        pe.wait_ge(s.mix, nth(i, v))
                    if i or v or c:
                        pe.wait_ge(s.ev, turn_nth(i, v, c) - 1)
                    for x in range(4 * c, min(4 * c + 4, len(pieces[v % NQ].tiles))):
                        mm = pe.transpose(k.ps[:, TB, (x - 4 * c) * P:(x - 4 * c + 1) * P],
                                          e_sb[:, exp_place(i, v), 0, x * P:(x + 1) * P], k.ident[:])
                    mm.then_inc(s.T, 1)

                def values(i, v, c):
                    u = pieces[v % NQ]
                    nt = len(u.tiles)
                    pe.wait_ge(s.ev, turn_nth(i, v, c))
                    if c == 0 and (i or v):
                        pe.wait_ge(s.o, nth(i, v - 1))
                    for x in range(4 * c, min(4 * c + 4, nt)):
                        mm = pe.matmul(k.ps[:, OB, 0:DV], pt_sb[:, v % 2, x], v_sb[:, v // NQ, u.tiles[x][0]],
                                       start=(x == 0), stop=(x == nt - 1))
                    if c == turns(v) - 1:
                        mm.then_inc(s.pv, 1)

                score(0, 0, 0)
                score(0, 0, 1)
                score(0, 1, 0)
                for n in range(N):
                    if n + 1 < N:
                        score(*unit(n + 1), 1)
                    turn(*unit(n), 0)
                    if n:
                        values(*unit(n - 1), turns((n - 1) % V) - 1)
                    if n + 2 < N:
                        score(*unit(n + 2), 0)
                    for c in range(1, turns(n % V)):
                        turn(*unit(n), c)
                        values(*unit(n), c - 1)
                values(*unit(N - 1), turns(V - 1) - 1)

            @block.scalar
            def _(act):
                act.wait_ge(s.lr, 1)
                nc.scalar.activation(lsum[:], lsum[:], ACT.Exp).then_inc(s.le, 1)

                def exps(i, v, m):
                    i, v = i + v // V, v % V
                    act.wait_ge(s.mx, map_nth(i, v, m))
                    if m == 0 and (i or v >= 3):
                        j, x = unit(i * V + v - 3)
                        act.wait_ge(s.T, turn_nth(j, x, turns(x) - 1))
                    w = pieces[v % NQ].width
                    nc.scalar.activation(e_sb[:, exp_place(i, v), m, 0:w], scores(m)[:, 0:w], ACT.Exp, bias=negmax[:, v % 2, m:m + 1],
                                         accum_out=rowsum[:, v % 4, m:m + 1]).then_inc(s.ex, 1)

                def evacuate(i, v, c):
                    act.wait_ge(s.T, turn_nth(i, v, c))
                    if c == 0 and (i or v >= 2):
                        act.wait_ge(s.pv, nth(i, v - 2))
                    lo, hi = 4 * c, min(4 * c + 4, len(pieces[v % NQ].tiles))
                    nc.scalar.copy(pt_sb[:, v % 2, lo:hi],
                                   k.ps[:, TB, 0:(hi - lo) * P].rearrange("p (t q) -> p t q", q=P)).then_inc(s.ev, 1)

                exps(0, 0, 0)
                exps(0, 0, 1)
                exps(0, 1, 0)
                for n in range(N):
                    evacuate(*unit(n), 0)
                    if n + 1 < N:
                        exps(*unit(n + 1), 1)
                    for c in range(1, turns(n % V)):
                        evacuate(*unit(n), c)
                        if c == 1 and n + 2 < N:
                            exps(*unit(n + 2), 0)
                    if turns(n % V) == 1 and n + 2 < N:
                        exps(*unit(n + 2), 0)

            @block.vector
            def _(dve):
                dve.wait_ge(s.lam, 16)
                nc.vector.tensor_tensor(lprod[:], lam4[:, 0:4:2], lam4[:, 1:4:2], ALU.mult).then_inc(s.lp, 1)
                dve.wait_ge(s.lp, 1)
                nc.vector.tensor_reduce(lsum[:], lprod[:], AX.X, ALU.add).then_inc(s.lr, 1)
                dve.wait_ge(s.le, 1)
                nc.vector.tensor_tensor(nlam[:], lsum[:, 1:2], lsum[:, 0:1], ALU.subtract).then_inc(s.l1, 1)
                dve.wait_ge(s.l1, 1)
                nc.vector.tensor_scalar(nlam[:], nlam[:], -LAM_INIT, None, ALU.add).then_inc(s.nl, 1)
                dve.wait_ge(s.nl, 1)

                def maxima(i, v, m):
                    i, v = i + v // V, v % V
                    dve.wait_ge(s.S, map_nth(i, v, m))
                    nc.vector.tensor_reduce(negmax[:, v % 2, m:m + 1], scores(m)[:, 0:pieces[v % NQ].width], AX.X, ALU.max,
                                            negate=True).then_inc(s.mx, 1)

                def mixed(i, v):
                    b, e, w = v % 2, exp_place(i, v), pieces[v % NQ].width
                    dve.wait_ge(s.ex, map_nth(i, v, 1))
                    nc.vector.reciprocal(r1[:, b:b + 1], rowsum[:, v % 4, 1:2]).then_inc(s.r1, 1)
                    dve.wait_ge(s.r1, nth(i, v))
                    nc.vector.tensor_scalar(coef[:, b:b + 1], rowsum[:, v % 4, 0:1], r1[:, b:b + 1], nlam[:, 0:1],
                                            ALU.mult, ALU.mult).then_inc(s.c, 1)
                    dve.wait_ge(s.c, nth(i, v))
                    nc.vector.scalar_tensor_tensor(out=e_sb[:, e, 0, 0:w], in0=e_sb[:, e, 1, 0:w], scalar=coef[:, b:b + 1],
                                                   in1=e_sb[:, e, 0, 0:w], op0=ALU.mult, op1=ALU.add).then_inc(s.mix, 1)

                def result(i, v):
                    b, p = v % 2, v // NQ
                    nc.vector.reciprocal(r0[:, b:b + 1], rowsum[:, v % 4, 0:1]).then_inc(s.r0, 1)
                    dve.wait_ge(s.r0, nth(i, v))
                    dve.wait_ge(s.pv, nth(i, v))
                    if i and v % NQ == 0:
                        dve.wait_ge(s.st0 if p == 0 else s.st1, i * 16)
                    nc.vector.tensor_scalar(o_sb[:, p, v % NQ], k.ps[:, OB, 0:DV], r0[:, b:b + 1], None,
                                            ALU.mult).then_inc(s.o, 1)

                maxima(0, 0, 0)
                maxima(0, 0, 1)
                maxima(0, 1, 0)
                mixed(0, 0)
                for n in range(N):
                    if n + 1 < N:
                        maxima(*unit(n + 1), 1)
                    if n:
                        result(*unit(n - 1))
                    if n + 2 < N:
                        maxima(*unit(n + 2), 0)
                    if n + 1 < N:
                        mixed(*unit(n + 1))
                result(*unit(N - 1))


def out_project(k, name, layer, n_tok, w_out, subln=None):
    nc = k.nc
    nt = n_tok // P
    chunks = token_chunks(n_tok)
    SB = len(chunks)
    names = "in0 in1 in2 in3 g sqa red root ri ya yb T hi lo wr0 wr1 whi wlo mm x g2"
    with phase(nc, name, names) as s, ExitStack() as st:
        def sb(nm, shape, dt=F32):
            return st.enter_context(nc.sbuf_tensor(f"{name}_{nm}", shape, dt))
        RB = 4
        rows = sb("rows", [P, RB, D_MODEL])
        oh, ol = sb("oh", [P, KT, n_tok], F32R), sb("ol", [P, KT, n_tok], F32R)
        raw = sb("raw", [P, 2, KT, P])
        wh, wl = sb("wh", [P, 2, KT, P], F32R), sb("wl", [P, 2, KT, P], F32R)
        if subln is not None:
            sq, rs, gain = sb("sq", [P, 512]), sb("rs", [P, 2, DIFF_HEADS]), sb("gain", [P, P])
        rows_in = (s.in0, s.in1, s.in2, s.in3)
        w_dram = w_out.rearrange("(f p) (n c) -> n p f c", p=P, c=P)

        with nc.Block() as block:
            @block.sync
            def _(sp):
                if subln is not None:
                    sp.dma_start(gain[:], subln.unsqueeze(0).broadcast_to([P, P])).then_inc(s.g, 16)
                for t in range(nt):
                    if t >= RB:
                        sp.wait_ge(s.T, t - RB + 1)
                    sp.dma_start(rows[:, t % RB], k.mix[layer][t * P:(t + 1) * P]).then_inc(rows_in[t % RB], 16)

                def pair(i, first, last):
                    for p in range(2):
                        if not first:
                            wait_then_store(sp, s.wlo, i * 2 + p - 1, s.g2)
                        sp.dma_start(raw[:, p], w_dram[bass.ds(i * 2 + p, 1)].squeeze(0)).then_inc(s.wr0 if p == 0 else s.wr1, 16)
                walk(sp, KT // 2, pair)

            @block.tensor
            def _(pe):
                for t in range(nt):
                    if subln is None:
                        pe.wait_ge(rows_in[t % RB], 16 * (t // RB + 1))
                    else:
                        pe.wait_ge(s.yb, t + 1)
                    if t >= 3:
                        pe.wait_ge(s.lo, t - 2)
                    for f in range(KT):
                        mm = pe.transpose(k.ps[:, 2 * (t % 3) + f // 4, (f % 4) * P:(f % 4 + 1) * P],
                                          rows[:, t % RB, f * P:(f + 1) * P], k.ident[:])
                    mm.then_inc(s.T, 1)

                def pair(i, first, last):
                    for p in range(2):
                        if first and p == 0:
                            pe.wait_ge(s.lo, nt)
                        pe.wait_ge(s.wlo, i * 2 + p + 1)
                        if not first:
                            pe.wait_ge(s.x, i * 2 + p - 1)
                        for f in range(KT):
                            for x, (w, o) in enumerate(((wh, oh), (wh, ol), (wl, oh))):
                                for c, (c0, n) in enumerate(chunks):
                                    mm = pe.matmul(k.ps[:, SB * p + c, 0:n], w[:, p, f], o[:, f, c0:c0 + n],
                                                   start=(f == 0 and x == 0), stop=(f == KT - 1 and x == 2))
                        mm.then_inc(s.mm, 1)
                walk(pe, KT // 2, pair)

            @block.scalar
            def _(act):
                def roots(t):
                    act.wait_ge(rows_in[t % RB], 16 * (t // RB + 1))
                    if t:
                        act.wait_ge(s.red, t)
                    nc.scalar.activation(sq[:], rows[:, t % RB, 0:512], ACT.Square).then_inc(s.sqa, 1)
                    act.wait_ge(s.red, t + 1)
                    nc.scalar.activation(rs[:, t % 2], rs[:, t % 2], ACT.Sqrt, bias=k.eps[:], scale=1.0 / P).then_inc(s.root, 1)

                if subln is not None:
                    roots(0)
                for t in range(nt):
                    if subln is not None and t + 1 < nt:
                        roots(t + 1)
                    act.wait_ge(s.T, t + 1)
                    nc.scalar.copy(oh[:, :, t * P:(t + 1) * P],
                                   k.ps[:, 2 * (t % 3):2 * (t % 3) + 2].rearrange("p b (f q) -> p (b f) q", q=P)).then_inc(s.hi, 1)

                def pair(i, first, last):
                    for p in range(2):
                        act.wait_ge(s.wr0 if p == 0 else s.wr1, i * 16 + 16)
                        if not first:
                            act.wait_ge(s.mm, i * 2 + p - 1)
                        nc.scalar.copy(wh[:, p], raw[:, p]).then_inc(s.whi, 1)
                walk(act, KT // 2, pair)

            @block.vector
            def _(dve):
                if subln is not None:
                    dve.wait_ge(s.g, 16)
                    nc.vector.tensor_scalar(gain[:], gain[:], 1.0 - LAM_INIT, None, ALU.mult).then_inc(s.ya, 1)
                    dve.wait_ge(s.ya, 1)

                def norm(t):
                    heads = lambda ap: ap.rearrange("p (h d) -> p h d", d=P)
                    r = rows[:, t % RB, 0:512]
                    dve.wait_ge(s.sqa, t + 1)
                    nc.vector.tensor_reduce(rs[:, t % 2], heads(sq[:]), AX.X, ALU.add).then_inc(s.red, 1)
                    dve.wait_ge(s.root, t + 1)
                    nc.vector.reciprocal(rs[:, t % 2], rs[:, t % 2]).then_inc(s.ri, 1)
                    dve.wait_ge(s.ri, t + 1)
                    nc.vector.tensor_tensor(heads(r), heads(r), rs[:, t % 2].unsqueeze(2).broadcast_to([P, DIFF_HEADS, P]),
                                            ALU.mult).then_inc(s.ya, 1)
                    dve.wait_ge(s.ya, t + 2)
                    nc.vector.tensor_tensor(heads(r), heads(r), gain[:].unsqueeze(1).broadcast_to([P, DIFF_HEADS, P]),
                                            ALU.mult).then_inc(s.yb, 1)

                def lo(t):
                    dve.wait_ge(s.hi, t + 1)
                    q = slice(t * P, (t + 1) * P)
                    nc.vector.tensor_tensor(ol[:, :, q], k.ps[:, 2 * (t % 3):2 * (t % 3) + 2].rearrange("p b (f q) -> p (b f) q", q=P),
                                            f32(oh[:, :, q]), ALU.subtract).then_inc(s.lo, 1)

                for t in range(nt):
                    if subln is not None:
                        norm(t)
                    if t:
                        lo(t - 1)
                lo(nt - 1)

                def cut(i, p):
                    dve.wait_ge(s.whi, i * 2 + p + 1)
                    nc.vector.tensor_tensor(wl[:, p], raw[:, p], f32(wh[:, p]), ALU.subtract).then_inc(s.wlo, 1)

                def add(i, p):
                    dve.wait_ge(s.mm, i * 2 + p + 1)
                    add_gated(k, dve, layer, 2, i * 2 + p, SB * p, n_tok).then_inc(s.x, 1)

                def pair(i, first, last):
                    if first:
                        cut(0, 0)
                    cut(i, 1)
                    add(i, 0)
                    if not last:
                        cut(i + 1, 0)
                    add(i, 1)
                walk(dve, KT // 2, pair)


def add_gated(k, dve, layer, gate, n, bank, n_tok):
    for w, a, b in ((0, 0, SEQ), (1, SEQ, n_tok)):
        if b > a:
            x = k.xT[:, bass.ds(n, 1), a:b].squeeze(1)
            ps = k.ps[:, bank:bank + (n_tok + 511) // 512].rearrange("p b c -> p (b c)")[:, a:b]
            ins = k.nc.vector.scalar_tensor_tensor(out=x, in0=ps, scalar=k.mods[:, layer, gate, bass.ds(n, 1), w], in1=x,
                                                   op0=ALU.mult, op1=ALU.add)
    return ins


def mlp(k, name, layer, n_tok, w1, w2):
    nc = k.nc
    chunks = token_chunks(n_tok)
    SB = len(chunks)
    C, F, U = FF // FFC, FFC // P, FFC // P + KT
    names = "f fm hh h wr0 wr1 whi wlo mm relu sq gh g x tick"
    with phase(nc, name, names) as s, ExitStack() as st:
        def sb(nm, shape, dt=F32):
            return st.enter_context(nc.sbuf_tensor(f"{name}_{nm}", shape, dt))
        hh, hl = sb("hh", [P, KT, n_tok], F32R), sb("hl", [P, KT, n_tok], F32R)
        gh, gl = sb("gh", [P, F, n_tok], F32R), sb("gl", [P, F, n_tok], F32R)
        g = sb("g", [P, n_tok])
        raw = sb("raw", [P, 2, KT, P])
        w1h, w1l = sb("w1h", [P, 2, KT, P], F32R), sb("w1l", [P, 2, KT, P], F32R)
        w2h, w2l = sb("w2h", [P, 2, F, P], F32R), sb("w2l", [P, 2, F, P], F32R)
        w1_dram = w1.rearrange("(f p) (c n q) -> c n p f q", p=P, n=F, q=P)
        w2_dram = w2.rearrange("(c f p) (n q) -> c n p f q", f=F, p=P, q=P)

        def nth(c, e):
            return c * U + e + 1

        def places(e):
            return (w1h, w1l, KT) if e % U < F else (w2h, w2l, F)

        def waits_for(e):
            return e - 2 if (e >= F + 2 or 2 <= e < F) else e - U + (F - 2 if e < F else KT - 2)

        with nc.Block() as block:
            @block.sync
            def _(sp):
                def chunk(c, first, last):
                    for e in range(U):
                        if not (first and e < 2):
                            wait_then_store(sp, s.wlo, nth(c, e - 2), s.tick)
                        src = w1_dram[bass.ds(c, 1), e].squeeze(0) if e < F else w2_dram[bass.ds(c, 1), e - F].squeeze(0)
                        sp.dma_start(raw[:, e % 2, 0:places(e)[2]], src).then_inc(s.wr0 if e % 2 == 0 else s.wr1, 16)
                walk(sp, C, chunk)

            @block.tensor
            def _(pe):
                def unit(c, e, first):
                    pe.wait_ge(s.wlo, nth(c, e))
                    if not (first and e < 2):
                        b = (e - 2) % U
                        n = c - 1 if e < 2 else c
                        if b < F:
                            pe.wait_ge(s.relu, n * F + b + 1)
                        else:
                            pe.wait_ge(s.x, n * KT + b - F + 1)
                    wh, wl, nf = places(e)
                    mh, ml = (hh, hl) if e < F else (gh, gl)
                    for f in range(nf):
                        if first and e == 0:
                            pe.wait_ge(s.h, (f + 1) * SB)
                        if e == F:
                            pe.wait_ge(s.g, c * F + f + 1)
                        for x, (w, m) in enumerate(((wh, mh), (wh, ml), (wl, mh))):
                            for b, (c0, n) in enumerate(chunks):
                                mm = pe.matmul(k.ps[:, SB * (e % 2) + b, 0:n], w[:, e % 2, f], m[:, f, c0:c0 + n],
                                               start=(f == 0 and x == 0), stop=(f == nf - 1 and x == 2))
                    mm.then_inc(s.mm, 1)

                def chunk(c, first, last):
                    for e in range(U):
                        unit(c, e, first)
                walk(pe, C, chunk)

            @block.scalar
            def _(act):
                def cut(c, e, first):
                    wh, _, nf = places(e)
                    act.wait_ge(s.wr0 if e % 2 == 0 else s.wr1, c * (8 * U) + (e // 2 + 1) * 16)
                    if waits_for(e) >= 0 or not first:
                        act.wait_ge(s.mm, nth(c, waits_for(e)))
                    nc.scalar.copy(wh[:, e % 2], raw[:, e % 2, 0:nf]).then_inc(s.whi, 1)

                cut(0, 0, True)
                for f in range(KT):
                    for c, (c0, n) in enumerate(chunks):
                        act.wait_ge(s.f, f * SB + c + 1)
                        w, here = (1 if c0 >= SEQ else 0), g[:, c0:c0 + n]
                        nc.scalar.activation(here, here, ACT.Identity, scale=k.mods[:, layer, 4, f, w:w + 1],
                                             bias=k.mods[:, layer, 3, f, w:w + 1]).then_inc(s.fm, 1)

                def chunk(c, first, last):
                    for e in range(U):
                        if e + 1 < U:
                            cut(c, e + 1, first)
                        elif not last:
                            cut(c + 1, 0, False)
                        if e < F:
                            act.wait_ge(s.mm, nth(c, e))
                            if not (first and e == 0):
                                act.wait_ge(s.g, c * F + e)
                            nc.scalar.activation(g[:], k.ps[:, SB * (e % 2):SB * (e % 2) + SB].rearrange("p b c -> p (b c)")[:, 0:n_tok],
                                                 ACT.Relu).then_inc(s.relu, 1)
                walk(act, C, chunk)

            @block.vector
            def _(dve):
                def cut(c, e):
                    wh, wl, nf = places(e)
                    dve.wait_ge(s.whi, nth(c, e))
                    nc.vector.tensor_tensor(wl[:, e % 2], raw[:, e % 2, 0:nf], f32(wh[:, e % 2]), ALU.subtract).then_inc(s.wlo, 1)

                cut(0, 0)
                for f in range(KT):
                    for c, (c0, n) in enumerate(chunks):
                        at = slice(c0, c0 + n)
                        dve.wait_ge(s.fm, f * SB + c + 1)
                        nc.vector.tensor_copy(hh[:, f, at], g[:, at]).then_inc(s.hh, 1)
                        dve.wait_ge(s.hh, f * SB + c + 1)
                        nc.vector.tensor_tensor(hl[:, f, at], g[:, at], f32(hh[:, f, at]), ALU.subtract).then_inc(s.h, 1)

                def chunk(c, first, last):
                    for e in range(U):
                        if e + 1 < U:
                            cut(c, e + 1)
                        elif not last:
                            cut(c + 1, 0)
                        if e < F:
                            me = c * F + e + 1
                            dve.wait_ge(s.relu, me)
                            nc.vector.tensor_tensor(g[:], g[:], g[:], ALU.mult).then_inc(s.sq, 1)
                            dve.wait_ge(s.sq, me)
                            nc.vector.tensor_copy(gh[:, e], g[:]).then_inc(s.gh, 1)
                            dve.wait_ge(s.gh, me)
                            nc.vector.tensor_tensor(gl[:, e], g[:], f32(gh[:, e]), ALU.subtract).then_inc(s.g, 1)
                        else:
                            dve.wait_ge(s.mm, nth(c, e))
                            add_gated(k, dve, layer, 5, e - F, SB * (e % 2), n_tok).then_inc(s.x, 1)
                walk(dve, C, chunk)

            @block.gpsimd
            def _(pool):
                for f in range(KT):
                    for c, (c0, n) in enumerate(chunks):
                        if f:
                            pool.wait_ge(s.h, (f - 1) * SB + c + 1)
                        nc.gpsimd.tensor_tensor(g[:, c0:c0 + n], k.xT[:, f, c0:c0 + n], k.rstd[:, c0:c0 + n],
                                                ALU.mult).then_inc(s.f, 1)


def closing(k):
    nc = k.nc
    with phase(nc, "close", "T cp0 cp1 st0 st1") as s, ExitStack() as st:
        rows = st.enter_context(nc.sbuf_tensor("out_rows", [P, 2, D_MODEL], F32))
        out = k.out.rearrange("b (t p) d -> (b t) p d", p=P)
        with nc.Block() as block:
            @block.tensor
            def _(pe):
                for t in range(LT):
                    if t >= 2:
                        pe.wait_ge(s.cp0, t - 1)
                        pe.wait_ge(s.cp1, t - 1)
                    for f in range(KT):
                        mm = pe.transpose(k.ps[:, 2 * (t % 2) + f // 4, (f % 4) * P:(f % 4 + 1) * P],
                                          k.xT[:, f, t * P:(t + 1) * P], k.ident[:])
                    mm.then_inc(s.T, 1)

            @block.scalar
            def _(act):
                for t in range(LT):
                    act.wait_ge(s.T, t + 1)
                    if t >= 2:
                        act.wait_ge(s.st0 if t % 2 == 0 else s.st1, 16 * (t // 2))
                    nc.scalar.copy(rows[:, t % 2, 0:512], k.ps[:, 2 * (t % 2)]).then_inc(s.cp0, 1)

            @block.vector
            def _(dve):
                for t in range(LT):
                    dve.wait_ge(s.T, t + 1)
                    if t >= 2:
                        dve.wait_ge(s.st0 if t % 2 == 0 else s.st1, 16 * (t // 2))
                    nc.vector.tensor_copy(rows[:, t % 2, 512:1024], k.ps[:, 2 * (t % 2) + 1]).then_inc(s.cp1, 1)

            @block.sync
            def _(sp):
                for t in range(LT):
                    sp.wait_ge(s.cp0, t + 1)
                    sp.wait_ge(s.cp1, t + 1)
                    sp.dma_start(out[t], rows[:, t % 2]).then_inc(s.st0 if t % 2 == 0 else s.st1, 16)
                sp.wait_ge(s.st0, 16 * LT // 2)
                sp.wait_ge(s.st1, 16 * LT // 2)


def trunk(nc, out, **ins):
    with ExitStack() as st:
        k = Core(nc, st, ins, out)
        ev = ins["ev_w_in"][0]
        opening(k)
        norm_stats(k, "n0", TOK)
        project(k, "pa", 0, ev, 0, 1024, [
            Unit(0, 512, 8, ins["diff_q_g"][0], HD ** -0.5, True, k.qkA, 0),
            Unit(512, 512, 8, ins["diff_k_g"][0], 1.0, True, k.qkA, 8)])
        project(k, "pb", 0, ev, 1024, 1280, [
            Unit(512, 512, 8, ins["swa_q_g"][0], HD ** -0.5, True, k.qkB, 0),
            Unit(1024, 256, 2, ins["swa_k_g"][0], 1.0, True, k.qkB, 8, v=128, v_dst=k.vB),
            Unit(0, 512, v=512, v_dst=k.vA)])
        attend(k, "ab", window_pieces(), 8,
               stacked_loader(k.qkB, 0, lambda i, p: 8 + i // 2, k.vB, lambda i, p: i // 2, HD),
               "two", HD, k.mix[0], 512, sink=ins["swa_sink"][0], beside=BiasSpread(k, ins["na_rpb"][0]))
        attend_diff(k, "aa", ins)
        out_project(k, "o0", 0, TOK, ins["w_out"][0], subln=ins["diff_subln_g"][0])
        norm_stats(k, "n1", TOK)
        mlp(k, "m0", 0, TOK, ins["mlp_w1"][0], ins["mlp_w2"][0])
        od = ins["od_w_in"][0]
        norm_stats(k, "n2", TOK)
        project_low_rank(k, "pq", 1, od, 0, MLA_QL, MLA_QL, ins["mla_qa_g"][0], ins["mla_wq_up"][0],
                         ins["mla_q_g"][0], MLA_QK ** -0.5, 0, False)
        project_low_rank(k, "pk", 1, od, MLA_QL, MLA_KVL + MLA_ROPE, MLA_KVL, ins["mla_kva_g"][0], ins["mla_wkv_up"][0],
                         ins["mla_k_g"][0], 1.0, MLA_HEADS, True)
        project(k, "pd", 1, od, MLA_QL + MLA_KVL + MLA_ROPE, 1536, [
            Unit(0, 512, 8, ins["na_q_g"][0], HD ** -0.5, False, k.qkD, 0),
            Unit(512, 512, 8, ins["na_k_g"][0], 1.0, False, k.qkD, 8),
            Unit(1024, 512, v=512, v_dst=k.vD)])
        attend(k, "ac", [Piece(q, [(0, TOK)]) for q in range(LT)], MLA_HEADS, parts_loader(k), "three", MLA_V, k.mix[1], 0)
        attend(k, "ad", neighbour_pieces(), NA_HEADS,
               stacked_loader(k.qkD, 0, lambda i, p: i * 2 + p + 8, k.vD, lambda i, p: i * 2 + p, HD),
               "two", HD, k.mix[1], 512, bias=bias_loader(k))
        out_project(k, "o1", 1, SEQ, ins["w_out"][1])
        norm_stats(k, "n3", SEQ)
        mlp(k, "m1", 1, SEQ, ins["mlp_w1"][1], ins["mlp_w2"][1])
        closing(k)


_OUTS = [((1, SEQ, D_MODEL), "float32")]


def kernel(**inputs):
    import numpy as _np
    import concourse.bacc as _bacc
    from concourse import mybir as _mybir
    from concourse.bass_utils import run_bass_kernel_spmd as _run

    nc = _bacc.Bacc("TRN2", target_bir_lowering=False, num_devices=1)
    arrays, args = {}, {}
    for name, a in {**inputs, **shape_constants()}.items():
        a = _np.ascontiguousarray(a)
        arrays[f"in_{name}"] = a
        args[name] = nc.dram_tensor(f"in_{name}", a.shape, _mybir.dt.from_np(a.dtype), kind="ExternalInput").ap()
    out = nc.dram_tensor("out_0", _OUTS[0][0], _mybir.dt.float32, kind="ExternalOutput").ap()
    trunk(nc, out, **args)
    r = _run(nc, [arrays], core_ids=[0])
    return r.results[0]["out_0"]
```
